# Optimizing a Trainium2 kernel written in Bass

```python
import math
import numpy as np
import jax
import jax.numpy as jnp
from jax import lax

D_MODEL = 1024
BATCH = 1
SEQ = 256
DEPTH = 2

CTX_LEN = 256
GRID_W = 64
Q_BLOCK = 128
ROPE_BASE = 10000.0
NEG_INF = -1e30
EPS = 1e-6
N_ADA = 6

MLA_HEADS = 4
MLA_NOPE = 64
MLA_ROPE = 32
MLA_V = 64
MLA_Q_RANK = 256
MLA_KV_RANK = 128
MLA_SCALE = (MLA_NOPE + MLA_ROPE) ** -0.5
DIFF_HEADS = 4
DIFF_QK = 32
DIFF_V = 2 * DIFF_QK
DIFF_SCALE = DIFF_QK ** -0.5
WIN_HEADS = 4
WIN_KV_HEADS = 2
WIN_GROUP = WIN_HEADS // WIN_KV_HEADS
WIN_DIM = 64
WINDOW = 128
WIN_SCALE = WIN_DIM ** -0.5
NA_HEADS = 4
NA_DIM = 64
NA_ROWS = 8
NA_COLS = 16
NA_SCALE = NA_DIM ** -0.5
FFN_HIDDEN = 4 * D_MODEL

N_BRANCH = 4
BRANCH_WIDTHS = (MLA_HEADS * MLA_V, DIFF_HEADS * DIFF_V, WIN_HEADS * WIN_DIM, NA_HEADS * NA_DIM)
MIX_WIDTH = sum(BRANCH_WIDTHS)
IN_SPLITS = (MLA_Q_RANK, MLA_KV_RANK, MLA_ROPE,
             DIFF_HEADS * 2 * DIFF_QK, DIFF_HEADS * 2 * DIFF_QK, DIFF_HEADS * DIFF_V,
             WIN_HEADS * WIN_DIM, WIN_KV_HEADS * WIN_DIM, WIN_KV_HEADS * WIN_DIM,
             NA_HEADS * NA_DIM, NA_HEADS * NA_DIM, NA_HEADS * NA_DIM)
IN_WIDTH = sum(IN_SPLITS)

kernel_name = 'hybrid_gated_mixer_dit_block'

def rmsnorm(x, g):
    xf = x.astype(jnp.float32)
    y = xf * lax.rsqrt(jnp.mean(xf * xf, axis=-1, keepdims=True) + EPS)
    return (y * g.astype(jnp.float32)).astype(x.dtype)

def adaln(x, g, shift, scale):
    return rmsnorm(x, g) * (1 + scale) + shift

def split_columns(p):
    offsets = np.cumsum(IN_SPLITS)[:-1].tolist()
    return jnp.split(p, offsets, axis=-1)

def axial_rope_tables(n_tokens, dim):
    quarter = dim // 4
    inv_freq = ROPE_BASE ** (-jnp.arange(quarter, dtype=jnp.float32) / quarter)
    t = jnp.arange(n_tokens, dtype=jnp.int32)
    row = (t // GRID_W).astype(jnp.float32)[:, None] * inv_freq
    col = (t % GRID_W).astype(jnp.float32)[:, None] * inv_freq
    ang = jnp.concatenate([row, row, col, col], axis=-1)
    return jnp.cos(ang), jnp.sin(ang)

def rope2d(x, rope):
    cos, sin = rope
    x1, x2, x3, x4 = jnp.split(x, 4, axis=-1)
    rot = jnp.concatenate([-x2, x1, -x4, x3], axis=-1)
    return x * cos[:, None].astype(x.dtype) + rot * sin[:, None].astype(x.dtype)

def sweep_query_blocks(fn, *qs):
    B, n = qs[0].shape[:2]
    nb = n // Q_BLOCK
    blocks = tuple(jnp.moveaxis(q.reshape(B, nb, Q_BLOCK, *q.shape[2:]), 1, 0) for q in qs)
    out = lax.map(lambda args: fn(*args), blocks)
    return jnp.moveaxis(out, 0, 1).reshape(B, n, *out.shape[3:])

def dense_attention(q, k, v, scale):
    s = jnp.einsum('bqhd,bkhd->bhqk', q, k).astype(jnp.float32) * scale
    p = jax.nn.softmax(s, axis=-1).astype(v.dtype)
    return jnp.einsum('bhqk,bkhd->bqhd', p, v)

def mla_branch(lat, ctx, q_norm, kv_norm, w_uq, w_ukv, rope, need_ctx):
    cq_l, ckv_l, kr_l = lat
    cq_c, ckv_c, kr_c = ctx
    B, n = cq_l.shape[:2]

    def up_q(c_q):
        q = (rmsnorm(c_q, q_norm) @ w_uq).reshape(c_q.shape[0], c_q.shape[1], MLA_HEADS, MLA_NOPE + MLA_ROPE)
        return q[..., :MLA_NOPE], q[..., MLA_NOPE:]

    def up_kv(c_kv):
        kv = (rmsnorm(c_kv, kv_norm) @ w_ukv).reshape(c_kv.shape[0], c_kv.shape[1], MLA_HEADS, MLA_NOPE + MLA_V)
        return kv[..., :MLA_NOPE], kv[..., MLA_NOPE:]

    def attend(qn, qr, kn, kr, v):
        s = (jnp.einsum('bqhd,bkhd->bhqk', qn, kn)
             + jnp.einsum('bqhr,bkr->bhqk', qr, kr)).astype(jnp.float32) * MLA_SCALE
        p = jax.nn.softmax(s, axis=-1).astype(v.dtype)
        return jnp.einsum('bhqk,bkhd->bqhd', p, v)

    qn_l, qr_l = up_q(cq_l)
    qr_l = rope2d(qr_l, rope)
    kn_l, v_l = up_kv(ckv_l)
    kr_l = rope2d(kr_l[:, :, None, :], rope)[:, :, 0, :]
    kn_c, v_c = up_kv(ckv_c)
    kn_all = jnp.concatenate([kn_c, kn_l], axis=1)
    kr_all = jnp.concatenate([kr_c, kr_l], axis=1)
    v_all = jnp.concatenate([v_c, v_l], axis=1)
    o_lat = sweep_query_blocks(lambda a, b: attend(a, b, kn_all, kr_all, v_all), qn_l, qr_l)
    o_lat = o_lat.reshape(B, n, MLA_HEADS * MLA_V)
    o_ctx = None
    if need_ctx:
        qn_c, qr_c = up_q(cq_c)
        o_ctx = attend(qn_c, qr_c, kn_c, kr_c, v_c).reshape(B, -1, MLA_HEADS * MLA_V)
    return o_lat, o_ctx

def diff_branch(lat, ctx, lam_params, subln, lam_init, rope, need_ctx):
    q_l, k_l, v_l = lat
    q_c, k_c, v_c = ctx
    B, n = q_l.shape[:2]

    def split_heads(t):
        t = t.reshape(t.shape[0], t.shape[1], DIFF_HEADS, 2, DIFF_QK)
        return t[..., 0, :], t[..., 1, :]

    def vheads(t):
        return t.reshape(t.shape[0], t.shape[1], DIFF_HEADS, DIFF_V)

    lp = lam_params.astype(jnp.float32)
    lam = jnp.exp(jnp.sum(lp[0] * lp[1])) - jnp.exp(jnp.sum(lp[2] * lp[3])) + lam_init

    def attend(q1, q2, k1, k2, v):
        s1 = jnp.einsum('bqhd,bkhd->bhqk', q1, k1).astype(jnp.float32) * DIFF_SCALE
        s2 = jnp.einsum('bqhd,bkhd->bhqk', q2, k2).astype(jnp.float32) * DIFF_SCALE
        p = jax.nn.softmax(s1, axis=-1) - lam * jax.nn.softmax(s2, axis=-1)
        return jnp.einsum('bhqk,bkhd->bqhd', p.astype(v.dtype), v)

    def finish(o):
        return (rmsnorm(o, subln) * (1 - lam_init)).reshape(o.shape[0], o.shape[1], DIFF_HEADS * DIFF_V)

    q1_l, q2_l = split_heads(q_l)
    k1_l, k2_l = split_heads(k_l)
    q1_l, q2_l, k1_l, k2_l = [rope2d(t, rope) for t in (q1_l, q2_l, k1_l, k2_l)]
    k1_c, k2_c = split_heads(k_c)
    vc = vheads(v_c)
    k1_all = jnp.concatenate([k1_c, k1_l], axis=1)
    k2_all = jnp.concatenate([k2_c, k2_l], axis=1)
    v_all = jnp.concatenate([vc, vheads(v_l)], axis=1)
    o_lat = finish(sweep_query_blocks(lambda a1, a2: attend(a1, a2, k1_all, k2_all, v_all), q1_l, q2_l))
    o_ctx = None
    if need_ctx:
        q1_c, q2_c = split_heads(q_c)
        o_ctx = finish(attend(q1_c, q2_c, k1_c, k2_c, vc))
    return o_lat, o_ctx

def window_branch(lat, ctx, sink, rope, need_ctx):
    q_l, k_l, v_l = lat
    q_c, k_c, v_c = ctx
    B, n = q_l.shape[:2]
    nb = n // WINDOW
    q = rope2d(q_l.reshape(B, n, WIN_HEADS, WIN_DIM), rope)
    k = rope2d(k_l.reshape(B, n, WIN_KV_HEADS, WIN_DIM), rope)
    v = v_l.reshape(B, n, WIN_KV_HEADS, WIN_DIM)
    kc = k_c.reshape(B, -1, WIN_KV_HEADS, WIN_DIM)
    vc = v_c.reshape(B, -1, WIN_KV_HEADS, WIN_DIM)
    sink_g = sink.astype(jnp.float32).reshape(WIN_KV_HEADS, WIN_GROUP)

    def banded(t):
        tp = jnp.pad(t, ((0, 0), (WINDOW, WINDOW), (0, 0), (0, 0))).reshape(B, nb + 2, WINDOW, WIN_KV_HEADS, WIN_DIM)
        return jnp.concatenate([tp[:, :-2], tp[:, 1:-1], tp[:, 2:]], axis=2)

    kb, vb = banded(k), banded(v)
    qg = q.reshape(B, nb, WINDOW, WIN_KV_HEADS, WIN_GROUP, WIN_DIM)
    blk = np.arange(nb)[:, None, None]
    qpos = blk * WINDOW + np.arange(WINDOW)[None, :, None]
    kpos = blk * WINDOW - WINDOW + np.arange(3 * WINDOW)[None, None, :]
    band = (kpos >= 0) & (kpos < n) & (np.abs(qpos - kpos) <= WINDOW)
    s_loc = jnp.einsum('bnqkgd,bnjkd->bnkgqj', qg, kb).astype(jnp.float32) * WIN_SCALE
    s_loc = jnp.where(band[None, :, None, None], s_loc, NEG_INF)
    s_ctx = jnp.einsum('bnqkgd,bjkd->bnkgqj', qg, kc).astype(jnp.float32) * WIN_SCALE
    s_sink = jnp.broadcast_to(sink_g[None, None, :, :, None, None], s_loc.shape[:-1] + (1,))
    p = jax.nn.softmax(jnp.concatenate([s_loc, s_ctx, s_sink], axis=-1), axis=-1).astype(v.dtype)
    n_loc = 3 * WINDOW
    n_ctx = kc.shape[1]
    o = (jnp.einsum('bnkgqj,bnjkd->bnqkgd', p[..., :n_loc], vb)
         + jnp.einsum('bnkgqj,bjkd->bnqkgd', p[..., n_loc:n_loc + n_ctx], vc))
    o_lat = o.reshape(B, n, WIN_HEADS * WIN_DIM)
    o_ctx = None
    if need_ctx:
        qcg = q_c.reshape(B, -1, WIN_KV_HEADS, WIN_GROUP, WIN_DIM)
        s = jnp.einsum('bqkgd,bjkd->bkgqj', qcg, kc).astype(jnp.float32) * WIN_SCALE
        s_sink_c = jnp.broadcast_to(sink_g[None, :, :, None, None], s.shape[:-1] + (1,))
        pc = jax.nn.softmax(jnp.concatenate([s, s_sink_c], axis=-1), axis=-1)[..., :-1].astype(v.dtype)
        o_ctx = jnp.einsum('bkgqj,bjkd->bqkgd', pc, vc).reshape(B, -1, WIN_HEADS * WIN_DIM)
    return o_lat, o_ctx

def neighborhood_branch(lat, ctx, rpb, need_ctx):
    q_l, k_l, v_l = lat
    q_c, k_c, v_c = ctx
    B, n = q_l.shape[:2]
    rows = n // GRID_W
    wr = min(NA_ROWS, rows)
    ncb = GRID_W // NA_COLS
    n_kcol = 2 * NA_COLS
    r = np.arange(rows)
    row_idx = np.clip(r - wr // 2, 0, rows - wr)[:, None] + np.arange(wr)[None, :]
    col0 = np.clip(np.arange(ncb) * NA_COLS - NA_COLS // 2, 0, GRID_W - n_kcol)
    col_idx = col0[:, None] + np.arange(n_kcol)[None, :]
    qcol = np.arange(ncb)[:, None] * NA_COLS + np.arange(NA_COLS)[None, :]
    cstart = np.clip(qcol - NA_COLS // 2, 0, GRID_W - NA_COLS)
    kcol = col_idx[:, None, :]
    in_win = (kcol >= cstart[..., None]) & (kcol < cstart[..., None] + NA_COLS)
    d_row = row_idx - r[:, None] + (NA_ROWS - 1)
    d_col = np.clip(kcol - qcol[..., None], -(NA_COLS - 1), NA_COLS - 1) + (NA_COLS - 1)
    bias = rpb.astype(jnp.float32)[:, d_row[:, None, None, :, None], d_col[None, :, :, None, :]]
    bias = jnp.where(in_win[None, None, :, :, None, :], bias, NEG_INF)
    bias = jnp.transpose(bias, (1, 2, 0, 3, 4, 5)).reshape(rows, ncb, NA_HEADS, NA_COLS, wr * n_kcol)

    q = q_l.reshape(B, rows, ncb, NA_COLS, NA_HEADS, NA_DIM)
    kgrid = k_l.reshape(B, rows, GRID_W, NA_HEADS, NA_DIM)
    vgrid = v_l.reshape(B, rows, GRID_W, NA_HEADS, NA_DIM)
    gr = row_idx[:, None, :, None]
    gc = col_idx[None, :, None, :]
    kg = kgrid[:, gr, gc]
    vg = vgrid[:, gr, gc]
    kcx = k_c.reshape(B, -1, NA_HEADS, NA_DIM)
    vcx = v_c.reshape(B, -1, NA_HEADS, NA_DIM)
    s_loc = jnp.einsum('brcqhd,brcwjhd->brchqwj', q, kg).astype(jnp.float32)
    s_loc = s_loc.reshape(B, rows, ncb, NA_HEADS, NA_COLS, wr * n_kcol) * NA_SCALE + bias[None]
    s_ctx = jnp.einsum('brcqhd,bjhd->brchqj', q, kcx).astype(jnp.float32) * NA_SCALE
    p = jax.nn.softmax(jnp.concatenate([s_loc, s_ctx], axis=-1), axis=-1).astype(v_l.dtype)
    n_loc = wr * n_kcol
    p_loc = p[..., :n_loc].reshape(B, rows, ncb, NA_HEADS, NA_COLS, wr, n_kcol)
    o = (jnp.einsum('brchqwj,brcwjhd->brcqhd', p_loc, vg)
         + jnp.einsum('brchqj,bjhd->brcqhd', p[..., n_loc:], vcx))
    o_lat = o.reshape(B, n, NA_HEADS * NA_DIM)
    o_ctx = None
    if need_ctx:
        qcx = q_c.reshape(B, -1, NA_HEADS, NA_DIM)
        o_ctx = dense_attention(qcx, kcx, vcx, NA_SCALE).reshape(B, -1, NA_HEADS * NA_DIM)
    return o_lat, o_ctx

def merge_branches(h, outs, w_gate, b_gate, w_branch):
    y = None
    off = 0
    for i, (o, width) in enumerate(zip(outs, BRANCH_WIDTHS)):
        g = jax.nn.sigmoid(h @ w_gate[:, i * D_MODEL:(i + 1) * D_MODEL] + b_gate[i * D_MODEL:(i + 1) * D_MODEL])
        term = g * (o @ w_branch[off:off + width])
        y = term if y is None else y + term
        off += width
    return y

def squared_relu_mlp(h, w1, w2):
    return jnp.square(jax.nn.relu(h @ w1)) @ w2

def lambda_init(layer):
    return 0.8 - 0.6 * math.exp(-0.3 * layer)

def setup_inputs(seed: int = 0) -> dict:
    key = jax.random.key(seed)
    ks = jax.random.split(key, 24)
    D = D_MODEL

    def nrm(k, shape, scale):
        return scale * jax.random.normal(k, shape, jnp.float32)

    return {
        'x': nrm(ks[0], (BATCH, SEQ, D), 1.0),
        'c': nrm(ks[1], (BATCH, D), 1.0),
        'ctx': nrm(ks[2], (BATCH, CTX_LEN, D), 1.0),
        'c_ctx': nrm(ks[3], (D,), 1.0),
        'w_ada': nrm(ks[4], (DEPTH, D, N_ADA * D), 0.5 * D ** -0.5),
        'b_ada': nrm(ks[5], (DEPTH, N_ADA * D), 0.02),
        'norm_mix': 1.0 + nrm(ks[6], (DEPTH, D), 0.02),
        'norm_ffn': 1.0 + nrm(ks[7], (DEPTH, D), 0.02),
        'w_in': nrm(ks[8], (DEPTH, D, IN_WIDTH), D ** -0.5),
        'mla_q_norm': 1.0 + nrm(ks[9], (DEPTH, MLA_Q_RANK), 0.02),
        'mla_kv_norm': 1.0 + nrm(ks[10], (DEPTH, MLA_KV_RANK), 0.02),
        'w_uq': nrm(ks[11], (DEPTH, MLA_Q_RANK, MLA_HEADS * (MLA_NOPE + MLA_ROPE)), MLA_Q_RANK ** -0.5),
        'w_ukv': nrm(ks[12], (DEPTH, MLA_KV_RANK, MLA_HEADS * (MLA_NOPE + MLA_V)), MLA_KV_RANK ** -0.5),
        'diff_lambda': nrm(ks[13], (DEPTH, 4, DIFF_QK), 0.1),
        'diff_subln': 1.0 + nrm(ks[14], (DEPTH, DIFF_V), 0.02),
        'win_sink': nrm(ks[15], (DEPTH, WIN_HEADS), 0.5),
        'na_rpb': nrm(ks[16], (DEPTH, NA_HEADS, 2 * NA_ROWS - 1, 2 * NA_COLS - 1), 0.1),
        'w_gate': nrm(ks[17], (DEPTH, D, N_BRANCH * D), D ** -0.5),
        'b_gate': nrm(ks[18], (DEPTH, N_BRANCH * D), 0.02),
        'w_branch': nrm(ks[19], (DEPTH, MIX_WIDTH, D), (MIX_WIDTH // N_BRANCH) ** -0.5),
        'w_out': nrm(ks[20], (DEPTH, D, D), D ** -0.5),
        'w_ff1': nrm(ks[21], (DEPTH, D, FFN_HIDDEN), D ** -0.5),
        'w_ff2': nrm(ks[22], (DEPTH, FFN_HIDDEN, D), FFN_HIDDEN ** -0.5),
        'final_norm': 1.0 + nrm(ks[23], (D,), 0.02),
    }

def reference(x, c, ctx, c_ctx, w_ada, b_ada, norm_mix, norm_ffn, w_in, mla_q_norm, mla_kv_norm,
              w_uq, w_ukv, diff_lambda, diff_subln, win_sink, na_rpb, w_gate, b_gate, w_branch,
              w_out, w_ff1, w_ff2, final_norm):
    n_lat = x.shape[1]
    rope_mla = axial_rope_tables(n_lat, MLA_ROPE)
    rope_diff = axial_rope_tables(n_lat, DIFF_QK)
    rope_win = axial_rope_tables(n_lat, WIN_DIM)
    xc = ctx
    for l in range(DEPTH):
        need_ctx = l < DEPTH - 1
        mod_lat = jnp.split((jax.nn.silu(c) @ w_ada[l] + b_ada[l])[:, None, :], N_ADA, axis=-1)
        mod_ctx = jnp.split(jax.nn.silu(c_ctx) @ w_ada[l] + b_ada[l], N_ADA, axis=-1)
        h_lat = adaln(x, norm_mix[l], mod_lat[0], mod_lat[1])
        h_ctx = adaln(xc, norm_mix[l], mod_ctx[0], mod_ctx[1])
        p_lat = split_columns(h_lat @ w_in[l])
        p_ctx = split_columns(h_ctx @ w_in[l])
        oa_l, oa_c = mla_branch(p_lat[0:3], p_ctx[0:3], mla_q_norm[l], mla_kv_norm[l], w_uq[l], w_ukv[l], rope_mla, need_ctx)
        ob_l, ob_c = diff_branch(p_lat[3:6], p_ctx[3:6], diff_lambda[l], diff_subln[l], lambda_init(l), rope_diff, need_ctx)
        oc_l, oc_c = window_branch(p_lat[6:9], p_ctx[6:9], win_sink[l], rope_win, need_ctx)
        od_l, od_c = neighborhood_branch(p_lat[9:12], p_ctx[9:12], na_rpb[l], need_ctx)
        mix_lat = merge_branches(h_lat, (oa_l, ob_l, oc_l, od_l), w_gate[l], b_gate[l], w_branch[l])
        x = x + mod_lat[2] * (mix_lat @ w_out[l])
        h = adaln(x, norm_ffn[l], mod_lat[3], mod_lat[4])
        x = x + mod_lat[5] * squared_relu_mlp(h, w_ff1[l], w_ff2[l])
        if need_ctx:
            mix_ctx = merge_branches(h_ctx, (oa_c, ob_c, oc_c, od_c), w_gate[l], b_gate[l], w_branch[l])
            xc = xc + mod_ctx[2] * (mix_ctx @ w_out[l])
            hc = adaln(xc, norm_ffn[l], mod_ctx[3], mod_ctx[4])
            xc = xc + mod_ctx[5] * squared_relu_mlp(hc, w_ff1[l], w_ff2[l])
    return rmsnorm(x, final_norm)


_drawn_inputs = setup_inputs


def setup_inputs(seed=0):
    import zlib

    import numpy as np

    out = dict(_drawn_inputs(seed))
    spreads = {}
    factors = {'norm_mix': 8.0,
     'norm_ffn': 4.439,
     'mla_q_norm': 8.0,
     'mla_kv_norm': 8.0,
     'diff_lambda': 8.0,
     'diff_subln': 8.0,
     'win_sink': 8.0,
     'na_rpb': 8.0,
     'b_gate': 8.0,
     'final_norm': 2.868}
    for name, (base, spread) in spreads.items():
        noise = np.random.default_rng([zlib.crc32(name.encode()), seed]).standard_normal(out[name].shape)
        drawn = base * np.exp(spread * noise) if base else spread * noise
        out[name] = jnp.asarray(drawn.astype(out[name].dtype))
    for name, factor in factors.items():
        out[name] = (out[name] * factor).astype(out[name].dtype)
    return out
```

```python
from contextlib import ExitStack

import numpy as np

import concourse.bass as bass
from concourse import mybir

F32 = mybir.dt.float32
F32R = mybir.dt.float32r
ALU = mybir.AluOpType
ACT = mybir.ActivationFunctionType
AX_X = mybir.AxisListType.X

P = 128
D = 1024
KD = D // P
CTX = 256
LAT = 256
TOK = CTX + LAT
DEPTH = 2
FFN = 4 * D
EPS = 1e-6
MASKED = -1e30
IN_WIDTH = 2464
HEADS = 4
NA_SCALE = WIN_SCALE = 64 ** -0.5
DIFF_SCALE = 32 ** -0.5
MLA_SCALE = 96 ** -0.5
GRID_W = 64
RPB_PAD = 127
RPB_ROW = GRID_W * RPB_PAD
LAMBDA_INIT = [0.8 - 0.6 * float(np.exp(-0.3 * layer)) for layer in range(DEPTH)]

C_CQ, C_CKV, C_DQ, C_DK, C_DV = 0, 256, 416, 672, 928
C_WQ, C_WKV, C_NQ, C_NK, C_NV = 1184, 1440, 1696, 1952, 2208
V_MLA, V_DIFF, V_NA, V_WIN, V_WIDTH = 0, 256, 512, 768, 896

_PAR = [("norm_mix", KD), ("norm_ffn", KD), ("b_ada", 48), ("q_norm", 2), ("kv_norm", 1),
        ("subln", 1), ("b_gate", 32), ("lam", 128), ("sink", HEADS)]
PAR_LAYER = sum(w for _, w in _PAR)
PAR_WIDTH = DEPTH * PAR_LAYER + KD


def par_at(layer, name):
    off = layer * PAR_LAYER
    for n, w in _PAR:
        if n == name:
            return off, off + w
        off += w
    raise KeyError(name)


_CON = [("ident", P), ("ones", P), ("head_ones", 2), ("rot64", P), ("rot32", P),
        ("cos64", LAT), ("sin64", LAT), ("cos32", LAT), ("sin32", LAT),
        ("band", 2 * LAT), ("near", 2 * LAT)]
CON_WIDTH = sum(w for _, w in _CON)


def con_at(name):
    off = 0
    for n, w in _CON:
        if n == name:
            return off, off + w
        off += w
    raise KeyError(name)


def constants():
    c = {"ident": np.eye(P), "ones": np.ones((P, P)), "head_ones": np.kron(np.eye(2), np.ones((64, 1)))}
    for dim in (64, 32):
        q = dim // 4
        rot = np.zeros((P, P))
        for i in range(P):
            block, j = i - i % dim, i % dim
            part = j // q
            rot[i, block + j + (q if part % 2 == 0 else -q)] = -1.0 if part % 2 == 0 else 1.0
        c[f"rot{dim}"] = rot.T
        inv = np.float32(10000.0) ** (-np.arange(q, dtype=np.float32) / np.float32(q))
        t = np.arange(LAT)
        row = (t // GRID_W).astype(np.float32)[:, None] * inv
        col = (t % GRID_W).astype(np.float32)[:, None] * inv
        ang = np.concatenate([row, row, col, col], axis=1).astype(np.float64).T
        c[f"cos{dim}"] = np.tile(np.cos(ang), (P // dim, 1))
        c[f"sin{dim}"] = np.tile(np.sin(ang), (P // dim, 1))
    k = np.arange(LAT)
    band, near = np.zeros((P, 2, LAT)), np.zeros((P, 2, LAT))
    for t in range(2):
        q = t * P + np.arange(P)[:, None]
        band[:, t] = np.where(np.abs(q - k) <= 128, 0.0, 8 * MASKED)
        start = np.clip(q % GRID_W - 8, 0, GRID_W - 16)
        inside = (k % GRID_W >= start) & (k % GRID_W < start + 16)
        near[:, t] = np.where(inside, 0.0, 8 * MASKED)
    c["band"], c["near"] = band.reshape(P, -1), near.reshape(P, -1)
    return np.concatenate([c[n] for n, _ in _CON], axis=1).astype(np.float32)


SLICES = 2
ADA_SLOTS = 2
BANKS = 5
QUARTERS = 4
HID = FFN // QUARTERS // P

ITEMS_LAT = ([("na", h, "lat", None) for h in range(HEADS)], [("win", h, "lat", None) for h in range(HEADS)])


def items_of(layer):
    out = []
    for kind in ("na", "win", "diff", "mla"):
        for h in range(HEADS):
            for part in ("lat", "ctx") if layer < DEPTH - 1 else ("lat",):
                for t in (0, 1) if kind == "diff" else (None,):
                    out.append((kind, h, part, t))
    return out


FF_ORDER = [("f1", 0), ("f1", 1), ("f2", 0), ("f1", 2), ("f2", 1), ("f1", 3), ("f2", 2), ("f2", 3)]


def units_of(layer):
    out = ["cq", "ckv", "nq", "nk", "nv", "wq", "wkv", "dq", "dk", "dv", "uq", "ukv"]
    for m in range(KD):
        out += [("g", m, 0), ("g", m, 1), ("b", m)]
    out += [("o", i) for i in range(4)]
    for kind, q in FF_ORDER:
        out += [(kind, q, i) for i in range(4)]
    return out


def groups_of(layer):
    a, v = "act", "dve"
    out = [("n1", v), ("n1b", v), ("cq0", a), ("cq1", a), ("ckv", a), ("kr", a), ("nq0", a), ("nq1", a),
           ("cs", v), ("nk0", a), ("nk1", a), ("cb0", v), ("cb1", v)]
    out += [(f"nv{t}", v) for t in range(4)] + [("wq0", a), ("wq1", a), ("wk", a)]
    out += [(f"wv{t}", v) for t in range(4)] + [("dq0", a), ("dq1", a)]
    out += [(n, v) for n in ("rwq0", "rwq1", "rwk", "rkr")] + [("dk0", a), ("dk1", a)]
    out += [(f"dv{t}", v) for t in range(4)]
    out += [(n, v) for n in ("rdq0", "rdq1", "rdk0", "rdk1")]
    out += [(f"uq{h}", a) for h in range(HEADS)] + [(f"uk{h}", a) for h in range(HEADS)]
    out += [(f"uv{t}", v) for t in range(4)] + [(f"ruq{h}", v) for h in range(HEADS)]
    items = items_of(layer)
    for j in range(len(items) + 1):
        if j:
            out += [(("T", j - 1, lane), a) for lane in range(1 if items[j - 1][0] == "diff" else 2)]
            out += [(("PV", j - 1), v)]
    out += [("ds", v), ("db0", v), ("db1", v)]
    for m in range(KD):
        out += [(("g", m, i), a) for i in range(4)] + [(("b", m, i), v) for i in range(4)]
    out += [(("o", m), v) for m in range(KD)] + [("n2", v), ("n2b", v)]
    for kind, q in FF_ORDER:
        out += [((kind, q, m), a if kind == "f1" else v) for m in range(KD)]
    return out


UNITS = [(layer, u) for layer in range(DEPTH) for u in units_of(layer)]
UNIT_AT = {key: i for i, key in enumerate(UNITS)}
GROUPS = [((layer, n), e) for layer in range(DEPTH) for n, e in groups_of(layer)] + [
    ((DEPTH, "n1"), "dve"), ((DEPTH, "n1b"), "dve")]
GROUP_AT = {key: i for i, (key, _) in enumerate(GROUPS)}
ROPES = ["rwq0", "rwq1", "rwk", "rkr", "rdq0", "rdq1", "rdk0", "rdk1", "ruq0", "ruq1", "ruq2", "ruq3"]


def emptied(g):
    engine = GROUPS[g][1]
    return engine, sum(e == engine for _, e in GROUPS[:g + 1])


EMPTIED = [emptied(g) for g in range(len(GROUPS))]


def last_group(unit):
    layer, u = unit
    name = {"cq": "cq1", "ckv": "kr", "nq": "nq1", "nk": "nk1", "nv": "nv3", "wq": "wq1", "wkv": "wv3",
            "dq": "dq1", "dk": "dk1", "dv": "dv3", "uq": "uq3", "ukv": "uv3"}
    if isinstance(u, str):
        return GROUP_AT[layer, name[u]]
    if u[0] == "g":
        return GROUP_AT[layer, ("g", u[1], 2 * u[2] + 1)]
    if u[0] == "b":
        return GROUP_AT[layer, ("b", u[1], 3)]
    if u[0] == "o":
        return GROUP_AT[layer, ("o", 2 * u[1] + 1)]
    return GROUP_AT[layer, (u[0], u[1], 2 * u[2] + 1)]


def tokens_of(layer):
    first = 0 if layer < DEPTH - 1 else CTX
    return first, TOK - first


def block_program(nc, xT, c2, con_in, par_in, rpb, w_ada, w_in, w_uq, w_ukv, w_gate, w_branch, w_out,
                  w_ff1, w_ff2, out):
    base = -(-nc.sbuf_base // 64) * 64
    at = [base]

    def place(size):
        here = at[0]
        at[0] += -(-size // 64) * 64
        return here

    def sb(name, shape, dtype=F32, offset=None):
        size = 4 * int(np.prod(shape[1:]))
        return nc.alloc_sbuf_tensor_at(name, shape, dtype, offset=place(size) if offset is None else offset)

    x = sb("x", [P, KD, TOK])
    h_hi = sb("h_hi", [P, KD, TOK], F32R)
    h_lo = sb("h_lo", [P, KD, TOK], F32R)
    con = sb("con", [P, CON_WIDTH])
    par = sb("par", [P, PAR_WIDTH])
    raw = sb("raw", [P, SLICES, 2048])
    w_hi = sb("w_hi", [P, SLICES, 2048], F32R)
    w_lo = sb("w_lo", [P, SLICES, 2048], F32R)
    ada_raw = sb("ada_raw", [P, ADA_SLOTS, KD, P])
    scratch = sb("scratch", [P, 4, TOK])
    rstd_rows = sb("rstd_rows", [P, 2, TOK])
    diag = sb("diag", [P, 8, P])
    bias = sb("bias", [P, 2, 2, LAT])
    cvec = sb("cvec", [P, KD, 2])
    silu = sb("silu", [P, KD, 2])
    mods = sb("mods", [P, DEPTH, 48, 2])
    gain = sb("gain", [P, DEPTH, 2, KD, 2])
    half_gate_bias = sb("half_gate_bias", [P, DEPTH, 32])
    small = sb("small", [P, DEPTH, 16])
    lam_prod = sb("lam_prod", [P, 2, 32])
    var = sb("var", [P, 16])
    rstd = sb("rstd", [P, 16])
    neg_half = sb("neg_half", [P, 16])
    stats = sb("stats", [P, 4, 128])
    kv_at = place(20480 + 4 * 4 * V_WIDTH)
    dk = sb("dk", [P, 2, TOK], offset=kv_at)
    nk = sb("nk", [P, 2, TOK], offset=kv_at + 4096)
    wk = sb("wk", [P, 2, TOK], offset=kv_at + 8192)
    mk = sb("mk", [P, HEADS, TOK], offset=kv_at + 12288)
    v_sb = sb("v_sb", [P, 4, V_WIDTH], offset=kv_at + 20480)
    qp_at = place(32768)
    dq = sb("dq", [P, 2, TOK], offset=qp_at)
    nq = sb("nq", [P, 2, TOK], offset=qp_at + 4096)
    wq = sb("wq", [P, 2, TOK], offset=qp_at + 8192)
    mq = sb("mq", [P, HEADS, TOK], offset=qp_at + 12288)
    probs = sb("probs", [P, 2, 2, TOK], offset=qp_at + 20480)
    probs_t = sb("probs_t", [P, 4, 2 * P], offset=qp_at + 28672)
    cn_hi = sb("cn_hi", [P, 3, TOK], F32R, offset=qp_at + 20480)
    cn_lo = sb("cn_lo", [P, 3, TOK], F32R, offset=qp_at + 20480 + 6144)
    sq = sb("sq", [P, KD, TOK], offset=kv_at)
    o_hi = sb("o_hi", [P, KD, TOK], F32R, offset=kv_at)
    o_lo = sb("o_lo", [P, KD, TOK], F32R, offset=kv_at + 16384)
    y_hi = sb("y_hi", [P, KD, TOK], F32R, offset=qp_at)
    y_lo = sb("y_lo", [P, KD, TOK], F32R, offset=qp_at + 16384)
    hid_hi = [sb("hid_hi0", [P, HID, TOK], F32R, offset=kv_at), sb("hid_hi1", [P, HID, TOK], F32R, offset=qp_at)]
    hid_lo = [sb("hid_lo0", [P, HID, TOK], F32R, offset=kv_at + 16384),
              sb("hid_lo1", [P, HID, TOK], F32R, offset=qp_at + 16384)]
    out_sb = sb("out_sb", [P, KD, LAT], offset=qp_at)
    latent = mq

    def cc(name, lo=0, hi=None):
        a, b = con_at(name)
        return con[:, a + lo:(b if hi is None else a + hi)]

    def pp(layer, name, i=None):
        a, b = par_at(layer, name)
        return par[:, a:b] if i is None else par[:, a + i:a + i + 1]

    NEG_LAM, SUBLN, LAM_SUM, LAM_EXP, SINK8 = 0, 1, 2, 4, 8

    def head_out(kind, h):
        return {"na": nq, "win": wq, "diff": dq, "mla": mq}[kind][:, h // 2, :]

    BRANCH_TILES = [head_out("mla", 0), head_out("mla", 2), head_out("diff", 0), head_out("diff", 2),
                    head_out("win", 0), head_out("win", 2), head_out("na", 0), head_out("na", 2)]

    with ExitStack() as ctx:
        ps = ctx.enter_context(nc.psum_tensor("ps", [P, BANKS, 512], F32))
        scores = ctx.enter_context(nc.psum_tensor("scores", [P, 2, 512], F32))
        ada_ps = ctx.enter_context(nc.psum_tensor("ada_ps", [P, 512], F32))

        def sem(name):
            return ctx.enter_context(nc.semaphore(name))

        raw_landed = [sem(f"raw_landed{i}") for i in range(SLICES)]
        ada_landed = [sem(f"ada_landed{i}") for i in range(ADA_SLOTS)]
        bias_landed = [sem(f"bias_landed{i}") for i in range(2)]
        x_landed = sem("x_landed")
        c_landed = sem("c_landed")
        small_landed = sem("small_landed")
        stored = sem("stored")
        w_hi_done = sem("w_hi_done")
        w_lo_done = sem("w_lo_done")
        group_done = sem("group_done")
        by_act = sem("by_act")
        by_dve = sem("by_dve")
        ada_done = sem("ada_done")
        mods_ready = sem("mods_ready")
        tanh_ready = sem("tanh_ready")
        silu_ready = sem("silu_ready")
        squares_ready = sem("squares_ready")
        rstd_ready = sem("rstd_ready")
        diag_ready = sem("diag_ready")
        scaled_ready = sem("scaled_ready")
        h_ready = sem("h_ready")
        h_hi_ready = sem("h_hi_ready")
        h_lo_ready = sem("h_lo_ready")
        latent_scaled = sem("latent_scaled")
        latent_hi = sem("latent_hi")
        latent_lo = sem("latent_lo")
        rope_done = sem("rope_done")
        kr_copied = sem("kr_copied")
        wk_copied = sem("wk_copied")
        bias_ready = sem("bias_ready")
        lam_sums = sem("lam_sums")
        lam_exps = sem("lam_exps")
        scores_ready = sem("scores_ready")
        shift_ready = sem("shift_ready")
        exp_done = sem("exp_done")
        probs_ready = sem("probs_ready")
        o_squares = sem("o_squares")
        o_hi_ready = sem("o_hi_ready")
        o_lo_ready = sem("o_lo_ready")
        y_sum_ready = sem("y_sum_ready")
        y_hi_ready = sem("y_hi_ready")
        y_lo_ready = sem("y_lo_ready")
        relu_ready = sem("relu_ready")
        relu2_ready = sem("relu2_ready")
        hid_hi_ready = sem("hid_hi_ready")
        hid_lo_ready = sem("hid_lo_ready")
        vector_step = sem("vector_step")
        gpsimd_step = sem("gpsimd_step")
        scalar_step = sem("scalar_step")
        out_ready = sem("out_ready")

        def wait_group(eng, layer, name):
            eng.wait_ge(group_done, GROUP_AT[layer, name] + 1)

        def wait_emptied(eng, layer, name):
            engine, n = EMPTIED[GROUP_AT[layer, name]]
            eng.wait_ge(by_act if engine == "act" else by_dve, n)

        def bank(layer, name):
            return ps[:, GROUP_AT[layer, name] % BANKS, :]

        def raw_dmas(u):
            kind = UNITS[u][1]
            return 2 if kind[0] == "g" and not isinstance(kind, str) else 1

        def landed_count(u):
            return 16 * sum(raw_dmas(v) for v in range(u % SLICES, u + 1, SLICES))

        def unit_shape(u):
            kind = UNITS[u][1]
            if kind == "uq":
                return 2, 384
            if kind == "ukv":
                return 1, 512
            if kind == "ckv":
                return KD, 160
            if kind[0] == "b":
                return KD, 128
            return KD, 256

        def unit_view(tensor, u):
            k, w = unit_shape(u)
            return tensor[:, u % SLICES, :k * w].rearrange("p (k c) -> p k c", k=k)

        n_items = [len(items_of(layer)) for layer in range(DEPTH)]
        item_base = [sum(n_items[:layer]) for layer in range(DEPTH + 1)]
        norms = [(layer, n) for layer in range(DEPTH) for n in ("n1", "n2")] + [(DEPTH, "n1")]

        def norm_at(layer, n):
            return norms.index((layer, n))

        def norm_tokens(layer, n):
            if layer == DEPTH:
                return CTX, LAT
            return (0, TOK) if n == "n1" else tokens_of(layer)

        RSTD_AT = {(layer, n): 4 * layer + i + 1 for layer in range(DEPTH) for i, n in enumerate(("n1", "cs", "ds", "n2"))}
        RSTD_AT[DEPTH, "n1"] = 4 * DEPTH + 1
        DIAG_AT = {(layer, n): 5 * layer + i + 1 for layer in range(DEPTH) for i, n in enumerate(("n1", "cs", "ds0", "ds1", "n2"))}
        DIAG_AT[DEPTH, "n1"] = 5 * DEPTH + 1

        ADA_FIRST = 16
        ADA_ALL = 48 * DEPTH
        ADA_PER_ITEM = -(-(ADA_ALL - ADA_FIRST) // n_items[0])

        def ada_range(j):
            return range(min(ADA_FIRST + ADA_PER_ITEM * j, ADA_ALL), min(ADA_FIRST + ADA_PER_ITEM * (j + 1), ADA_ALL))

        block = ctx.enter_context(nc.Block())

        @block.sync
        def _(sp):
            def load_unit(u):
                layer, kind = UNITS[u]
                if u >= SLICES:
                    sp.wait_ge(w_hi_done, u - SLICES + 1)
                    sp.wait_ge(w_lo_done, u - SLICES + 1)
                dst = unit_view(raw, u)
                s = raw_landed[u % SLICES]

                def rows(w, c0, width):
                    return w[:, c0:c0 + width].rearrange("(k p) c -> p k c", p=P)

                if kind == "uq":
                    sp.dma_start(dst, rows(w_uq[layer], 0, 384)).then_inc(s, 16)
                elif kind == "ukv":
                    sp.dma_start(dst, rows(w_ukv[layer], 0, 512)).then_inc(s, 16)
                elif isinstance(kind, str):
                    c0 = {"cq": C_CQ, "ckv": C_CKV, "nq": C_NQ, "nk": C_NK, "nv": C_NV, "wq": C_WQ,
                          "wkv": C_WKV, "dq": C_DQ, "dk": C_DK, "dv": C_DV}[kind]
                    sp.dma_start(dst, rows(w_in[layer], c0, unit_shape(u)[1])).then_inc(s, 16)
                elif kind[0] == "g":
                    for i in range(2):
                        c0 = (2 * kind[2] + i) * D + kind[1] * P
                        sp.dma_start(dst[:, :, i * P:(i + 1) * P], rows(w_gate[layer], c0, P)).then_inc(s, 16)
                elif kind[0] == "b":
                    sp.dma_start(dst, rows(w_branch[layer], kind[1] * P, P)).then_inc(s, 16)
                elif kind[0] == "o":
                    sp.dma_start(dst, rows(w_out[layer], kind[1] * 256, 256)).then_inc(s, 16)
                elif kind[0] == "f1":
                    c0 = kind[1] * HID * P + kind[2] * 256
                    sp.dma_start(dst, rows(w_ff1[layer], c0, 256)).then_inc(s, 16)
                else:
                    r0 = kind[1] * HID * P
                    sp.dma_start(dst, rows(w_ff2[layer][r0:r0 + HID * P], kind[2] * 256, 256)).then_inc(s, 16)

            def load_ada(n):
                if n >= ADA_SLOTS:
                    sp.wait_ge(ada_done, n - ADA_SLOTS + 1)
                layer, j = divmod(n, 48)
                sp.dma_start(ada_raw[:, n % ADA_SLOTS], w_ada[layer][:, j * P:(j + 1) * P]
                             .rearrange("(k p) c -> p k c", p=P)).then_inc(ada_landed[n % ADA_SLOTS], 16)

            def load_bias(layer, h):
                n = layer * HEADS + h
                if n >= 2:
                    before = item_base[(n - 2) // HEADS] + items_of((n - 2) // HEADS).index(("na", (n - 2) % HEADS, "lat", None))
                    sp.wait_ge(shift_ready, before + 1)
                for t in range(2):
                    for half in range(2):
                        r = 2 * t + half
                        start = rpb[layer, h, 7 - r:8 - r, 63:64]
                        src = bass.AP(tensor=start.tensor, offset=start.offset, ap=[[RPB_PAD - 1, 64], [RPB_ROW, 4], [1, 64]])
                        dst = bias[64 * half:64 * half + 64, n % 2, t, :].rearrange("p (w c) -> p w c", w=4)
                        sp.dma_start(dst, src).then_inc(bias_landed[n % 2], 16)

            sp.dma_start(cvec[:], c2).then_inc(c_landed, 16)
            sp.dma_start(par[:], par_in).then_inc(small_landed, 16)
            sp.dma_start(con[:], con_in).then_inc(small_landed, 16)
            sp.dma_start(x[:], xT).then_inc(x_landed, 16)
            for n in range(ADA_FIRST):
                load_ada(n)
                if n == ADA_FIRST // 2:
                    load_unit(0)
            load_unit(1)
            for layer in range(DEPTH):
                first, before = UNIT_AT[layer, "cq"], UNIT_AT[layer, ("g", 0, 0)]
                after = UNIT_AT[layer, ("f2", QUARTERS - 1, 3)] + 1
                load_bias(layer, 0)
                load_bias(layer, 1)
                for u in range(first, before):
                    load_unit(u + SLICES)
                na_heads = [j for j, it in enumerate(items_of(layer)) if it[0] == "na" and it[2] == "lat"]
                for j in range(n_items[layer]):
                    if layer == 0:
                        for n in ada_range(j):
                            load_ada(n)
                    if j in na_heads[1:3]:
                        load_bias(layer, na_heads.index(j) + 1)
                for u in range(before, after):
                    if u + SLICES < len(UNITS):
                        load_unit(u + SLICES)
            for m in range(KD):
                sp.wait_ge(out_ready, m + 1)
                sp.dma_start(out[m * P:(m + 1) * P, :], out_sb[:, m, :]).then_inc(stored, 16)
            sp.wait_ge(stored, 16 * KD)

        @block.tensor
        def _(pe):
            def begin(layer, name):
                g = GROUP_AT[layer, name]
                if g >= BANKS:
                    engine, n = EMPTIED[g - BANKS]
                    pe.wait_ge(by_act if engine == "act" else by_dve, n)
                return bank(layer, name)

            def have_unit(u):
                pe.wait_ge(w_hi_done, u + 1)
                pe.wait_ge(w_lo_done, u + 1)
                return unit_view(w_hi, u), unit_view(w_lo, u)

            def product3(dst, lhs, rhs, first, last):
                (lh, ll), (rh, rl) = lhs, rhs
                pe.matmul(dst, lh, rh, start=first, stop=False)
                pe.matmul(dst, lh, rl, start=False, stop=False)
                return pe.matmul(dst, ll, rh, start=False, stop=last)

            def weights_by_tokens(layer, name, unit, c0, width, acts, first, ready=None):
                dst = begin(layer, name)[:width, 0:TOK - first]
                hi, lo = have_unit(unit)
                kt = unit_shape(unit)[0]
                for k in range(kt):
                    if ready is not None:
                        pe.wait_ge(ready[0], ready[1] + k + 1)
                    mm = product3(dst, (hi[:, k, c0:c0 + width], lo[:, k, c0:c0 + width]),
                                  (acts[0][:, k, first:TOK], acts[1][:, k, first:TOK]), k == 0, k == kt - 1)
                mm.then_inc(group_done, 1)

            def tokens_by_weights(layer, name, t, unit, cols, acts, k0=0):
                dst = begin(layer, name)
                hi, lo = have_unit(unit)
                kt = unit_shape(unit)[0]
                for k in range(kt):
                    rh, rl = cols(hi[:, k]), cols(lo[:, k])
                    width = int(np.prod(rh.shape[1:]))
                    tt = slice(t * P, (t + 1) * P)
                    mm = product3(dst[:, 0:width], (acts[0][:, k0 + k, tt], acts[1][:, k0 + k, tt]), (rh, rl),
                                  k == 0, k == kt - 1)
                mm.then_inc(group_done, 1)

            def sums_of_squares(layer, name):
                t0, n = norm_tokens(layer, name)
                dst = begin(layer, name)
                for k in range(KD):
                    pe.wait_ge(squares_ready, KD * norm_at(layer, name) + k + 1)
                    for t in range(n // P):
                        mm = pe.matmul(dst[:, t:t + 1], sq[:, k, t0 + t * P:t0 + (t + 1) * P], cc("ones", 0, 1),
                                       start=(k == 0 and t == 0), stop=(k == KD - 1), skip_group_check=True)
                mm.then_inc(group_done, 1)

            def spread(layer, name, key, blocks, b0=0):
                pe.wait_ge(diag_ready, DIAG_AT[layer, key])
                dst = begin(layer, name)
                pe.matmul(dst[:, 0:blocks * P], cc("ones"), diag[:, b0:b0 + blocks, :].rearrange("p a b -> p (a b)"),
                          start=True, stop=True).then_inc(group_done, 1)

            def ada_tile(n):
                pe.wait_ge(ada_landed[n % ADA_SLOTS], 16 * (n // ADA_SLOTS + 1))
                for k in range(KD):
                    mm = pe.matmul(ada_ps[:, 2 * n:2 * n + 2], ada_raw[:, n % ADA_SLOTS, k, :], silu[:, k, :],
                                   start=(k == 0), stop=(k == KD - 1))
                mm.then_inc(ada_done, 1)

            def rotate(layer, name, src, rows, dim):
                dst = begin(layer, name)
                pe.matmul(dst[rows, 0:LAT], cc(f"rot{dim}")[rows, rows], src[rows, CTX:TOK],
                          start=True, stop=True).then_inc(group_done, 1)

            pe.wait_ge(small_landed, 32)
            pe.wait_ge(silu_ready, 1)
            for n in range(ADA_FIRST):
                ada_tile(n)

            for layer in range(DEPTH):
                t0, nt = tokens_of(layer)
                unit = {name: UNIT_AT[layer, name] for name in units_of(layer)}
                h = (h_hi, h_lo)
                full = slice(0, P)

                sums_of_squares(layer, "n1")
                spread(layer, "n1b", "n1", TOK // P)
                weights_by_tokens(layer, "cq0", unit["cq"], 0, P, h, t0, (h_lo_ready, KD * norm_at(layer, "n1")))
                weights_by_tokens(layer, "cq1", unit["cq"], P, P, h, t0)
                weights_by_tokens(layer, "ckv", unit["ckv"], 0, P, h, 0)
                weights_by_tokens(layer, "kr", unit["ckv"], 64, 96, h, 0)
                for i in range(2):
                    weights_by_tokens(layer, f"nq{i}", unit["nq"], i * P, P, h, t0)
                dst = begin(layer, "cs")
                wait_emptied(pe, layer, "ckv")
                nq_tiles = nt // P
                for t in range(nq_tiles):
                    for i in range(2):
                        pe.matmul(dst[:, t:t + 1], scratch[:, i, t * P:(t + 1) * P], cc("ones", 0, 1),
                                  start=(i == 0), stop=(i == 1), skip_group_check=True)
                for t in range(TOK // P):
                    mm = pe.matmul(dst[:, nq_tiles + t:nq_tiles + t + 1], scratch[:, 2, t * P:(t + 1) * P],
                                   cc("ones", 0, 1), start=True, stop=True, skip_group_check=True)
                mm.then_inc(group_done, 1)
                for i in range(2):
                    weights_by_tokens(layer, f"nk{i}", unit["nk"], i * P, P, h, 0)
                spread(layer, "cb0", "cs", nq_tiles)
                spread(layer, "cb1", "cs", TOK // P, nq_tiles)
                for t in range(4):
                    tokens_by_weights(layer, f"nv{t}", t, unit["nv"], lambda w: w, h)
                for i in range(2):
                    weights_by_tokens(layer, f"wq{i}", unit["wq"], i * P, P, h, t0)
                weights_by_tokens(layer, "wk", unit["wkv"], 0, P, h, 0)
                for t in range(4):
                    tokens_by_weights(layer, f"wv{t}", t, unit["wkv"], lambda w: w[:, P:2 * P], h)
                for i in range(2):
                    weights_by_tokens(layer, f"dq{i}", unit["dq"], i * P, P, h, t0)
                wait_emptied(pe, layer, "wk")
                rotate(layer, "rwq0", wq[:, 0], full, 64)
                rotate(layer, "rwq1", wq[:, 1], full, 64)
                rotate(layer, "rwk", wk[:, 0], full, 64)
                rotate(layer, "rkr", mk[:, 0], slice(64, 96), 32)
                for i in range(2):
                    weights_by_tokens(layer, f"dk{i}", unit["dk"], i * P, P, h, 0)
                for t in range(4):
                    tokens_by_weights(layer, f"dv{t}", t, unit["dv"], lambda w: w, h)
                wait_emptied(pe, layer, "dk1")
                for i in range(2):
                    rotate(layer, f"rdq{i}", dq[:, i], full, 32)
                for i in range(2):
                    rotate(layer, f"rdk{i}", dk[:, i], full, 32)
                pe.wait_ge(latent_lo, 3 * layer + 3)
                cn = (cn_hi, cn_lo)
                for hd in range(HEADS):
                    weights_by_tokens(layer, f"uq{hd}", unit["uq"], hd * 96, 96, cn, t0)
                ckvn = (cn_hi[:, 2:3], cn_lo[:, 2:3])
                for hd in range(HEADS):
                    weights_by_tokens(layer, f"uk{hd}", unit["ukv"], hd * P, 64, ckvn, 0)
                for t in range(4):
                    tokens_by_weights(layer, f"uv{t}", t, unit["ukv"],
                                      lambda w: w.rearrange("p (h c) -> p h c", h=HEADS)[:, :, 64:128], cn, 2)
                wait_emptied(pe, layer, "uq3")
                for hd in range(HEADS):
                    rotate(layer, f"ruq{hd}", mq[:, hd], slice(64, 96), 32)

                items = items_of(layer)
                wait_emptied(pe, layer, "uk3")
                wait_emptied(pe, layer, "ruq3")
                pe.wait_ge(rope_done, len(ROPES) * (layer + 1))
                pe.wait_ge(kr_copied, 3 * (layer + 1))
                pe.wait_ge(wk_copied, layer + 1)

                def score_item(j):
                    kind, hd, part, t = items[j]
                    nkeys = TOK if part == "lat" else CTX
                    col = CTX if part == "lat" else 0
                    for lane in range(2):
                        if kind == "na" or kind == "win":
                            rows = slice(64 * (hd % 2), 64 * (hd % 2) + 64)
                            q_sb, k_sb = (nq, nk) if kind == "na" else (wq, wk)
                            qa = q_sb[rows, hd // 2, col + lane * P:col + (lane + 1) * P]
                            ka = k_sb[rows, hd // 2, 0:nkeys]
                        elif kind == "diff":
                            r0 = 64 * (hd % 2) + 32 * lane
                            qa = dq[r0:r0 + 32, hd // 2, col + t * P:col + (t + 1) * P]
                            ka = dk[r0:r0 + 32, hd // 2, 0:nkeys]
                        else:
                            qa = mq[0:96, hd, col + lane * P:col + (lane + 1) * P]
                            ka = mk[0:96, hd, 0:nkeys]
                        mm = pe.matmul(scores[:, lane, 0:nkeys], qa, ka, start=True, stop=True)
                    mm.then_inc(scores_ready, 1)

                def turn_item(j):
                    kind, hd, part, t = items[j]
                    ntile = (TOK if part == "lat" else CTX) // P
                    pe.wait_ge(probs_ready, item_base[layer] + j + 1)
                    for lane in range(1 if kind == "diff" else 2):
                        dst = begin(layer, ("T", j, lane))
                        for kt in range(ntile):
                            mm = pe.transpose(dst[:, kt * P:(kt + 1) * P], probs[:, j % 2, lane, kt * P:(kt + 1) * P],
                                              cc("ident"))
                        mm.then_inc(group_done, 1)

                def value_item(j):
                    kind, hd, part, t = items[j]
                    ntile = (TOK if part == "lat" else CTX) // P
                    v0 = {"na": V_NA + 64 * hd, "win": V_WIN + 64 * (hd // 2), "diff": V_DIFF + 64 * hd,
                          "mla": V_MLA + 64 * hd}[kind]
                    lanes = 1 if kind == "diff" else 2
                    wait_emptied(pe, layer, ("T", j, lanes - 1))
                    dst = begin(layer, ("PV", j))[64 * (hd % 2):64 * (hd % 2) + 64, 0:lanes * P]
                    for kt in range(ntile):
                        mm = pe.matmul(dst, v_sb[:, kt, v0:v0 + 64], probs_t[:, kt, 0:lanes * P],
                                       start=(kt == 0), stop=(kt == ntile - 1))
                    mm.then_inc(group_done, 1)

                for j in range(len(items) + 1):
                    if j:
                        turn_item(j - 1)
                    if j < len(items):
                        score_item(j)
                        if layer == 0:
                            for n in ada_range(j):
                                if n == ADA_FIRST:
                                    pe.wait_ge(mods_ready, 1)
                                ada_tile(n)
                    if j:
                        value_item(j - 1)

                dst = begin(layer, "ds")
                for pair in range(2):
                    pe.wait_ge(o_squares, 2 * layer + pair + 1)
                    for t in range(nq_tiles):
                        col = 2 * (pair * nq_tiles + t)
                        mm = pe.matmul(dst[:, col:col + 2], scratch[:, pair, t * P:(t + 1) * P], cc("head_ones"),
                                       start=True, stop=True, skip_group_check=True)
                mm.then_inc(group_done, 1)
                for pair in range(2):
                    pe.wait_ge(diag_ready, DIAG_AT[layer, f"ds{pair}"])
                    dst = begin(layer, f"db{pair}")
                    for a in range(2):
                        mm = pe.matmul(dst[64 * a:64 * a + 64, 0:nt], cc("ones", 0, 64),
                                       diag[:, a * nq_tiles:(a + 1) * nq_tiles, :].rearrange("p a b -> p (a b)"),
                                       start=True, stop=True)
                    mm.then_inc(group_done, 1)

                for m in range(KD):
                    for i in range(4):
                        weights_by_tokens(layer, ("g", m, i), unit["g", m, i // 2], (i % 2) * P, P, h, t0)
                    hi, lo = have_unit(unit["b", m])
                    pe.wait_ge(o_lo_ready, KD * (layer + 1))
                    for i in range(4):
                        dst = begin(layer, ("b", m, i))[:, 0:nt]
                        for k in (2 * i, 2 * i + 1):
                            mm = product3(dst, (hi[:, k], lo[:, k]), (o_hi[:, k, t0:], o_lo[:, k, t0:]),
                                          k % 2 == 0, k % 2 == 1)
                        mm.then_inc(group_done, 1)
                for m in range(KD):
                    weights_by_tokens(layer, ("o", m), unit["o", m // 2], (m % 2) * P, P, (y_hi, y_lo), t0,
                                      (y_lo_ready, KD * layer) if m == 0 else None)

                sums_of_squares(layer, "n2")
                spread(layer, "n2b", "n2", nq_tiles)
                for kind, q in FF_ORDER:
                    for m in range(KD):
                        if kind == "f1":
                            weights_by_tokens(layer, ("f1", q, m), unit["f1", q, m // 2], (m % 2) * P, P, h, t0,
                                              (h_lo_ready, KD * norm_at(layer, "n2")) if (q, m) == (0, 0) else None)
                        else:
                            weights_by_tokens(layer, ("f2", q, m), unit["f2", q, m // 2], (m % 2) * P, P,
                                              (hid_hi[q % 2], hid_lo[q % 2]), t0,
                                              (hid_lo_ready, (layer * QUARTERS + q) * HID) if m == 0 else None)
            sums_of_squares(DEPTH, "n1")
            spread(DEPTH, "n1b", "n1", LAT // P)

        @block.scalar
        def _(act):
            def cut(u):
                if u >= len(UNITS):
                    return
                act.wait_ge(raw_landed[u % SLICES], landed_count(u))
                if u >= SLICES:
                    act.wait_ge(group_done, last_group(UNITS[u - SLICES]) + 1)
                act.activation(unit_view(w_hi, u), unit_view(raw, u), ACT.Copy).then_inc(w_hi_done, 1)

            def copy_out(layer, name, dst, rows=slice(0, P), width=TOK):
                wait_group(act, layer, name)
                act.activation(dst, bank(layer, name)[rows, 0:width], ACT.Copy).then_inc(by_act, 1)

            def squares(layer, name):
                t0, n = norm_tokens(layer, name)
                for k in range(KD):
                    if (layer, name) == (0, "n1"):
                        act.wait_ge(x_landed, 16)
                    elif name == "n1":
                        wait_emptied(act, layer - 1, ("f2", QUARTERS - 1, k))
                    else:
                        wait_emptied(act, layer, ("o", k))
                    act.activation(sq[:, k, t0:t0 + n], x[:, k, t0:t0 + n], ACT.Square).then_inc(squares_ready, 1)

            def normed_hi(layer, name):
                t0, n = norm_tokens(layer, name)
                r = KD * norm_at(layer, name)
                for k in range(KD):
                    act.wait_ge(h_ready, r + k + 1)
                    act.activation(h_hi[:, k, t0:t0 + n], scratch[:, k % 4, 0:n], ACT.Copy).then_inc(h_hi_ready, 1)

            act.wait_ge(c_landed, 16)
            act.activation(silu[:], cvec[:], ACT.Tanh, scale=0.5).then_inc(tanh_ready, 1)
            squares(0, "n1")
            cut(0)
            cut(1)
            for layer in range(DEPTH):
                t0, nt = tokens_of(layer)
                U = {name: UNIT_AT[layer, name] for name in units_of(layer)}
                if layer:
                    squares(layer, "n1")
                act.wait_ge(lam_sums, layer + 1)
                act.activation(small[:, layer, LAM_EXP:LAM_EXP + 2], small[:, layer, LAM_SUM:LAM_SUM + 2],
                               ACT.Exp).then_inc(lam_exps, 1)
                normed_hi(layer, "n1")
                for i in range(2):
                    wait_group(act, layer, f"cq{i}")
                    act.activation(latent[:, i, 0:nt], bank(layer, f"cq{i}")[:, 0:nt], ACT.Copy)
                    act.activation(scratch[:, i, 0:nt], bank(layer, f"cq{i}")[:, 0:nt], ACT.Square).then_inc(by_act, 1)
                cut(U["cq"] + SLICES)
                wait_group(act, layer, "ckv")
                act.activation(latent[:, 2, :], bank(layer, "ckv"), ACT.Copy)
                act.activation(scratch[:, 2, :], bank(layer, "ckv"), ACT.Square).then_inc(by_act, 1)
                copy_out(layer, "kr", mk[64:96, 0, :], slice(64, 96))
                cut(U["ckv"] + SLICES)
                for i in range(2):
                    copy_out(layer, f"nq{i}", nq[:, i, t0:], width=nt)
                cut(U["nq"] + SLICES)
                for i in range(2):
                    copy_out(layer, f"nk{i}", nk[:, i, :])
                cut(U["nk"] + SLICES)
                for i in range(3):
                    first = t0 if i < 2 else 0
                    gamma = pp(layer, "q_norm", i) if i < 2 else pp(layer, "kv_norm")
                    act.wait_ge(latent_scaled, 3 * layer + i + 1)
                    act.activation(cn_hi[:, i, first:], latent[:, i, 0:TOK - first], ACT.Identity,
                                   scale=gamma).then_inc(latent_hi, 1)
                cut(U["nv"] + SLICES)
                for i in range(2):
                    copy_out(layer, f"wq{i}", wq[:, i, t0:], width=nt)
                cut(U["wq"] + SLICES)
                copy_out(layer, "wk", wk[:, 0, :])
                cut(U["wkv"] + SLICES)
                for i in range(2):
                    copy_out(layer, f"dq{i}", dq[:, i, t0:], width=nt)
                cut(U["dq"] + SLICES)
                for i in range(2):
                    copy_out(layer, f"dk{i}", dk[:, i, :])
                cut(U["dk"] + SLICES)
                act.wait_ge(rope_done, len(ROPES) * layer + ROPES.index("rwk") + 1)
                act.activation(wk[0:64, 1, :], wk[64:128, 0, :], ACT.Copy)
                act.activation(wk[64:128, 1, :], wk[64:128, 0, :], ACT.Copy).then_inc(scalar_step, 1)
                act.wait_ge(scalar_step, layer + 1)
                act.activation(wk[64:128, 0, :], wk[0:64, 0, :], ACT.Copy).then_inc(wk_copied, 1)
                cut(U["dv"] + SLICES)
                act.wait_ge(latent_lo, 3 * layer + 3)
                for hd in range(HEADS):
                    copy_out(layer, f"uq{hd}", mq[0:96, hd, t0:], slice(0, 96), nt)
                cut(U["uq"] + SLICES)
                for hd in range(HEADS):
                    copy_out(layer, f"uk{hd}", mk[0:64, hd, :], slice(0, 64))
                cut(U["ukv"] + SLICES)

                items = items_of(layer)
                scale = {"na": NA_SCALE, "win": WIN_SCALE, "diff": DIFF_SCALE, "mla": MLA_SCALE}

                def turned(j):
                    kind, hd, part, t = items[j]
                    ntile = (TOK if part == "lat" else CTX) // P
                    for lane in range(1 if kind == "diff" else 2):
                        wait_group(act, layer, ("T", j, lane))
                        act.activation(probs_t[:, 0:ntile, lane * P:(lane + 1) * P],
                                       bank(layer, ("T", j, lane))[:, 0:ntile * P].rearrange("p (k q) -> p k q", q=P),
                                       ACT.Copy).then_inc(by_act, 1)

                for j in range(len(items) + 1):
                    if j:
                        turned(j - 1)
                    if j < len(items):
                        kind, hd, part, t = items[j]
                        nkeys = TOK if part == "lat" else CTX
                        act.wait_ge(shift_ready, item_base[layer] + j + 1)
                        col = 2 * (item_base[layer] + j)
                        if kind == "win":
                            act.activation(stats[:, 3, col:col + 2], stats[:, 1, col:col + 2], ACT.Exp,
                                           bias=pp(layer, "sink", hd))
                        for lane in range(2):
                            mm = act.activation(probs[:, j % 2, lane, 0:nkeys], scores[:, lane, 0:nkeys], ACT.Exp,
                                                bias=stats[:, 1, col + lane:col + lane + 1], scale=scale[kind],
                                                accum_out=stats[:, 2, col + lane:col + lane + 1])
                        mm.then_inc(exp_done, 1)
                last_diff = max(j for j, it in enumerate(items) if it[0] == "diff")
                wait_emptied(act, layer, ("PV", last_diff))
                for pair in range(2):
                    act.activation(scratch[:, pair, 0:nt], dq[:, pair, t0:], ACT.Square).then_inc(o_squares, 1)
                wait_emptied(act, layer, ("PV", len(items) - 1))
                for k in (6, 7, 4, 5, 0, 1, 2, 3):
                    if k in (2, 3):
                        wait_emptied(act, layer, f"db{k - 2}")
                    act.activation(o_hi[:, k, t0:], BRANCH_TILES[k][:, t0:], ACT.Copy).then_inc(o_hi_ready, 1)

                for m in range(KD):
                    if m:
                        act.wait_ge(y_lo_ready, KD * layer + m)
                    for i in range(4):
                        wait_group(act, layer, ("g", m, i))
                        act.activation(scratch[:, i, 0:nt], bank(layer, ("g", m, i))[:, 0:nt], ACT.Tanh, scale=0.5,
                                       bias=half_gate_bias[:, layer, i * KD + m:i * KD + m + 1]).then_inc(by_act, 1)
                        if i % 2:
                            cut(U["g", m, i // 2] + SLICES)
                    act.wait_ge(y_sum_ready, KD * layer + m + 1)
                    act.activation(y_hi[:, m, t0:], scratch[:, 0, 0:nt], ACT.Copy, scale=0.5).then_inc(y_hi_ready, 1)
                    cut(U["b", m] + SLICES)
                for i in range(4):
                    cut(U["o", i] + SLICES)

                squares(layer, "n2")
                normed_hi(layer, "n2")

                def hidden_hi(q, m):
                    f = (layer * QUARTERS + q) * HID + m
                    act.wait_ge(relu2_ready, f + 1)
                    act.activation(hid_hi[q % 2][:, m, t0:], scratch[:, f % 4, 0:nt], ACT.Copy).then_inc(hid_hi_ready, 1)

                for kind, q in FF_ORDER:
                    for i in range(4):
                        if kind == "f1":
                            for m in (2 * i, 2 * i + 1):
                                f = (layer * QUARTERS + q) * HID + m
                                if f >= 4:
                                    act.wait_ge(hid_lo_ready, f - 3)
                                wait_group(act, layer, ("f1", q, m))
                                act.activation(scratch[:, f % 4, 0:nt], bank(layer, ("f1", q, m))[:, 0:nt],
                                               ACT.Relu).then_inc(by_act, 1)
                                if m:
                                    hidden_hi(q, m - 1)
                            if i == 3:
                                hidden_hi(q, HID - 1)
                        cut(U[kind, q, i] + SLICES)
            squares(DEPTH, "n1")

        @block.vector
        def _(dve):
            steps = [0]

            def step(ins):
                steps[0] += 1
                ins.then_inc(vector_step, 1)
                dve.wait_ge(vector_step, steps[0])

            def cut(u):
                if u >= len(UNITS):
                    return
                dve.wait_ge(w_hi_done, u + 1)
                dve.tensor_tensor(unit_view(w_lo, u), unit_view(raw, u), unit_view(w_hi, u).bitcast(F32),
                                  ALU.subtract).then_inc(w_lo_done, 1)

            def variance(layer, name, cols, inverse):
                wait_group(dve, layer, name)
                b = bank(layer, name)
                for n, (c0, c1) in enumerate(cols):
                    ins = dve.tensor_scalar(var[:, c0:c1], b[:, c0:c1], inverse[n], EPS, ALU.mult, ALU.add)
                ins.then_inc(by_dve, 1)

            def diagonal(key, layer, blocks, source, b0=0, inc=True):
                ident = cc("ident").unsqueeze(1).to_broadcast([P, blocks, P])
                ins = dve.tensor_tensor(diag[:, b0:b0 + blocks, :], ident, source.unsqueeze(2).to_broadcast([P, blocks, P]),
                                        ALU.mult)
                if inc:
                    ins.then_inc(diag_ready, 1)

            def rstd_of_tokens(layer, name):
                t0, n = norm_tokens(layer, name)
                variance(layer, name, [(0, n // P)], [1.0 / D])
                dve.wait_ge(rstd_ready, RSTD_AT[layer, name])
                diagonal(name, layer, n // P, rstd[:, 0:n // P])
                wait_group(dve, layer, name + "b")
                dve.tensor_copy(rstd_rows[:, 0, 0:n], bank(layer, name + "b")[:, 0:n]).then_inc(by_dve, 1)

            def parts(t0, n):
                return [(0, 0, CTX), (1, CTX, TOK)] if n == TOK else [(1, 0, n)]

            def modulated(layer, name):
                t0, n = norm_tokens(layer, name)
                which = 0 if name == "n1" else 1
                r = KD * norm_at(layer, name)
                for k in range(KD):
                    dve.wait_ge(scaled_ready, r + k + 1)
                    for group, a, b in parts(t0, n):
                        s = scratch[:, k % 4, a:b]
                        ins = dve.tensor_scalar(s, s, gain[:, layer, which, k, group:group + 1],
                                                mods[:, layer, 24 * which + k, group:group + 1], ALU.mult, ALU.add)
                    ins.then_inc(h_ready, 1)

            def modulations(n0, n1):
                layer = n0 // 48
                b = pp(layer, "b_ada")[:, n0 % 48:n0 % 48 + n1 - n0].unsqueeze(2).to_broadcast([P, n1 - n0, 2])
                dve.wait_ge(ada_done, n1)
                return dve.tensor_tensor(mods[:, layer, n0 % 48:n0 % 48 + n1 - n0, :],
                                         ada_ps[:, 2 * n0:2 * n1].rearrange("p (j g) -> p j g", g=2), b, ALU.add)

            def gains(layer, which):
                g = pp(layer, "norm_ffn" if which else "norm_mix").unsqueeze(2).to_broadcast([P, KD, 2])
                return dve.scalar_tensor_tensor(gain[:, layer, which], mods[:, layer, 24 * which + KD:24 * which + 2 * KD, :],
                                                1.0, g, ALU.add, ALU.mult)

            def residual(layer, name, mod, k):
                t0, nt = tokens_of(layer)
                wait_group(dve, layer, name)
                for group, a, b in parts(t0, nt):
                    xs = x[:, k, t0 + a:t0 + b]
                    ins = dve.scalar_tensor_tensor(xs, bank(layer, name)[:, a:b], mods[:, layer, mod * KD + k, group:group + 1],
                                                   xs, ALU.mult, ALU.add)
                ins.then_inc(by_dve, 1)

            dve.wait_ge(tanh_ready, 1)
            step(dve.scalar_tensor_tensor(silu[:], silu[:], 1.0, cvec[:], ALU.add, ALU.mult))
            dve.tensor_scalar(silu[:], silu[:], 0.5, None, ALU.mult).then_inc(silu_ready, 1)
            dve.wait_ge(small_landed, 32)
            for layer in range(DEPTH):
                dve.tensor_scalar(half_gate_bias[:, layer, :], pp(layer, "b_gate"), 0.5, None, ALU.mult)
                dve.tensor_scalar(small[:, layer, SINK8:SINK8 + HEADS], pp(layer, "sink"), 8.0, None, ALU.mult)
                dve.tensor_scalar(small[:, layer, SUBLN:SUBLN + 1], pp(layer, "subln"), 1.0 - LAMBDA_INIT[layer], None, ALU.mult)
                lam = pp(layer, "lam").rearrange("p (a b c) -> p a b c", a=2, b=2)
                step(dve.tensor_tensor(lam_prod[:], lam[:, :, 0, :], lam[:, :, 1, :], ALU.mult))
                dve.reduce_sum(small[:, layer, LAM_SUM:LAM_SUM + 2], lam_prod[:], AX_X).then_inc(lam_sums, 1)
                dve.wait_ge(lam_sums, layer + 1)
            cut(0)
            cut(1)
            step(modulations(0, ADA_FIRST))
            gains(0, 0).then_inc(mods_ready, 1)
            dve.wait_ge(mods_ready, 1)

            for layer in range(DEPTH):
                t0, nt = tokens_of(layer)
                U = {name: UNIT_AT[layer, name] for name in units_of(layer)}
                nq_tiles = nt // P
                dve.wait_ge(lam_exps, layer + 1)
                e = small[:, layer, LAM_EXP:LAM_EXP + 2]
                step(dve.tensor_tensor(small[:, layer, NEG_LAM:NEG_LAM + 1], e[:, 1:2], e[:, 0:1], ALU.subtract))
                step(dve.tensor_scalar(small[:, layer, NEG_LAM:NEG_LAM + 1], small[:, layer, NEG_LAM:NEG_LAM + 1],
                                       LAMBDA_INIT[layer], None, ALU.subtract))
                rstd_of_tokens(layer, "n1")
                modulated(layer, "n1")
                cut(U["cq"] + SLICES)
                cut(U["ckv"] + SLICES)
                variance(layer, "cs", [(0, nq_tiles), (nq_tiles, nq_tiles + 4)], [1.0 / 256, 1.0 / 128])
                dve.wait_ge(rstd_ready, RSTD_AT[layer, "cs"])
                diagonal("cs", layer, nq_tiles + 4, rstd[:, 0:nq_tiles + 4])
                cut(U["nq"] + SLICES)
                for i, n in ((0, nt), (1, TOK)):
                    wait_group(dve, layer, f"cb{i}")
                    dve.tensor_copy(rstd_rows[:, i, 0:n], bank(layer, f"cb{i}")[:, 0:n]).then_inc(by_dve, 1)
                wait_emptied(dve, layer, "cb1")
                for i in range(3):
                    n = nt if i < 2 else TOK
                    dve.tensor_tensor(latent[:, i, 0:n], latent[:, i, 0:n], rstd_rows[:, i // 2, 0:n],
                                      ALU.mult).then_inc(latent_scaled, 1)
                for i in range(3):
                    first = t0 if i < 2 else 0
                    gamma = pp(layer, "q_norm", i) if i < 2 else pp(layer, "kv_norm")
                    dve.wait_ge(latent_hi, 3 * layer + i + 1)
                    dve.scalar_tensor_tensor(cn_lo[:, i, first:], latent[:, i, 0:TOK - first], gamma,
                                             cn_hi[:, i, first:].bitcast(F32), ALU.mult, ALU.subtract).then_inc(latent_lo, 1)
                cut(U["nk"] + SLICES)

                def values(name, v0, width):
                    for t in range(4):
                        wait_group(dve, layer, f"{name}{t}")
                        dve.tensor_copy(v_sb[:, t, v0:v0 + width], bank(layer, f"{name}{t}")[:, 0:width]).then_inc(by_dve, 1)

                def turn_products(names):
                    for name in names:
                        r = len(ROPES) * layer + ROPES.index(name)
                        dim = 64 if name.startswith("rw") else 32
                        rows = slice(64, 96) if name[1] in "ku" else slice(0, P)
                        if r >= 4:
                            dve.wait_ge(rope_done, r - 3)
                        wait_group(dve, layer, name)
                        dve.tensor_tensor(scratch[rows, r % 4, 0:LAT], bank(layer, name)[rows, 0:LAT],
                                          cc(f"sin{dim}")[rows], ALU.mult).then_inc(by_dve, 1)

                values("nv", V_NA, 256)
                cut(U["nv"] + SLICES)
                cut(U["wq"] + SLICES)
                values("wv", V_WIN, 128)
                cut(U["wkv"] + SLICES)
                cut(U["dq"] + SLICES)
                turn_products(ROPES[0:4])
                cut(U["dk"] + SLICES)
                values("dv", V_DIFF, 256)
                cut(U["dv"] + SLICES)
                turn_products(ROPES[4:8])
                cut(U["uq"] + SLICES)
                values("uv", V_MLA, 256)
                cut(U["ukv"] + SLICES)
                turn_products(ROPES[8:12])

                items = items_of(layer)
                scale = {"na": NA_SCALE, "win": WIN_SCALE, "diff": DIFF_SCALE, "mla": MLA_SCALE}

                def shift(j):
                    kind, hd, part, t = items[j]
                    nkeys = TOK if part == "lat" else CTX
                    col = 2 * (item_base[layer] + j)
                    dve.wait_ge(scores_ready, item_base[layer] + j + 1)
                    if part == "lat" and kind in ("na", "win"):
                        if kind == "na":
                            dve.wait_ge(bias_ready, layer * HEADS + hd + 1)
                            add = bias[:, (layer * HEADS + hd) % 2]
                        else:
                            add = cc("band").rearrange("p (t k) -> p t k", t=2)
                        step(dve.tensor_tensor(scores[:, :, CTX:TOK], scores[:, :, CTX:TOK], add, ALU.add))
                    step(dve.tensor_reduce(stats[:, 0, col:col + 2], scores[:, :, 0:nkeys], AX_X, ALU.max))
                    if kind == "win":
                        ins = dve.tensor_scalar(stats[:, 1, col:col + 2], stats[:, 0, col:col + 2],
                                                small[:, layer, SINK8 + hd:SINK8 + hd + 1], -scale[kind], ALU.max, ALU.mult)
                    else:
                        ins = dve.tensor_scalar(stats[:, 1, col:col + 2], stats[:, 0, col:col + 2], -scale[kind], None, ALU.mult)
                    ins.then_inc(shift_ready, 1)

                def normalise(j):
                    kind, hd, part, t = items[j]
                    nkeys = TOK if part == "lat" else CTX
                    col = 2 * (item_base[layer] + j)
                    s = stats[:, 2, col:col + 2]
                    dve.wait_ge(exp_done, item_base[layer] + j + 1)
                    if kind == "win":
                        step(dve.tensor_tensor(s, s, stats[:, 3, col:col + 2], ALU.add))
                    step(dve.reciprocal(s, s))
                    pr = [probs[:, j % 2, lane, 0:nkeys] for lane in range(2)]
                    if kind == "diff":
                        step(dve.tensor_scalar(pr[1], pr[1], s[:, 1:2], small[:, layer, NEG_LAM:NEG_LAM + 1], ALU.mult, ALU.mult))
                        ins = dve.scalar_tensor_tensor(pr[0], pr[0], s[:, 0:1], pr[1], ALU.mult, ALU.add)
                    else:
                        for lane in range(2):
                            ins = dve.tensor_scalar(pr[lane], pr[lane], s[:, lane:lane + 1], None, ALU.mult)
                    ins.then_inc(probs_ready, 1)

                def outputs(j):
                    kind, hd, part, t = items[j]
                    rows = slice(64 * (hd % 2), 64 * (hd % 2) + 64)
                    c0 = (CTX if part == "lat" else 0) + (t * P if kind == "diff" else 0)
                    width = P if kind == "diff" else 2 * P
                    wait_group(dve, layer, ("PV", j))
                    dve.tensor_copy(head_out(kind, hd)[rows, c0:c0 + width],
                                    bank(layer, ("PV", j))[rows, 0:width]).then_inc(by_dve, 1)

                for j in range(len(items) + 1):
                    if j < len(items):
                        shift(j)
                        normalise(j)
                    if j:
                        outputs(j - 1)

                if layer == 0:
                    modulations(ADA_FIRST, 48)
                    step(modulations(48, 2 * 48))
                    gains(0, 1)
                    gains(1, 0)
                    step(gains(1, 1))

                variance(layer, "ds", [(0, 4 * nq_tiles)], [1.0 / 64])
                dve.wait_ge(rstd_ready, RSTD_AT[layer, "ds"])
                for pair in range(2):
                    if pair:
                        wait_group(dve, layer, "db0")
                    r = rstd[:, 2 * pair * nq_tiles:2 * (pair + 1) * nq_tiles].rearrange("p (t a) -> p t a", a=2)
                    for a in range(2):
                        diagonal(f"ds{pair}", layer, nq_tiles, r[:, :, a], a * nq_tiles, inc=(a == 1))
                for pair in range(2):
                    wait_group(dve, layer, f"db{pair}")
                    o = dq[:, pair, t0:]
                    dve.scalar_tensor_tensor(o, o, small[:, layer, SUBLN:SUBLN + 1], bank(layer, f"db{pair}")[:, 0:nt],
                                             ALU.mult, ALU.mult).then_inc(by_dve, 1)

                for m in range(KD):
                    cut(U["g", m, 0] + SLICES)
                    cut(U["g", m, 1] + SLICES)
                    wait_emptied(dve, layer, ("g", m, 3))
                    for i in range(4):
                        wait_group(dve, layer, ("b", m, i))
                        s = scratch[:, i, 0:nt]
                        dve.scalar_tensor_tensor(s, s, 1.0, bank(layer, ("b", m, i))[:, 0:nt], ALU.add,
                                                 ALU.mult).then_inc(by_dve, 1)
                    dve.wait_ge(y_hi_ready, KD * layer + m + 1)
                    dve.scalar_tensor_tensor(y_lo[:, m, t0:], scratch[:, 0, 0:nt], 0.5, y_hi[:, m, t0:].bitcast(F32),
                                             ALU.mult, ALU.subtract).then_inc(y_lo_ready, 1)
                    cut(U["b", m] + SLICES)
                for m in range(KD):
                    residual(layer, ("o", m), 2, m)
                    if m % 2:
                        cut(U["o", m // 2] + SLICES)

                rstd_of_tokens(layer, "n2")
                modulated(layer, "n2")

                def hidden_lo(q, m):
                    f = (layer * QUARTERS + q) * HID + m
                    dve.wait_ge(hid_hi_ready, f + 1)
                    dve.tensor_tensor(hid_lo[q % 2][:, m, t0:], scratch[:, f % 4, 0:nt],
                                      hid_hi[q % 2][:, m, t0:].bitcast(F32), ALU.subtract).then_inc(hid_lo_ready, 1)

                for kind, q in FF_ORDER:
                    for i in range(4):
                        for m in (2 * i, 2 * i + 1):
                            if kind == "f1":
                                hidden_lo(q, m)
                            else:
                                residual(layer, (kind, q, m), 5, m)
                        cut(U[kind, q, i] + SLICES)

            rstd_of_tokens(DEPTH, "n1")
            wait_emptied(dve, DEPTH, "n1b")
            for k in range(KD):
                dve.scalar_tensor_tensor(out_sb[:, k, :], x[:, k, CTX:TOK], par[:, DEPTH * PAR_LAYER + k:DEPTH * PAR_LAYER + k + 1],
                                         rstd_rows[:, 0, 0:LAT], ALU.mult, ALU.mult).then_inc(out_ready, 1)

        @block.gpsimd
        def _(pool):
            steps = [0]

            def step(ins):
                steps[0] += 1
                ins.then_inc(gpsimd_step, 1)
                pool.wait_ge(gpsimd_step, steps[0])

            def power(layer, name, cols):
                wait_emptied(pool, layer, name)
                if RSTD_AT[layer, name] > 1:
                    key = {v: k for k, v in RSTD_AT.items()}[RSTD_AT[layer, name] - 1]
                    last = "ds1" if key[1] == "ds" else key[1]
                    pool.wait_ge(diag_ready, DIAG_AT[key[0], last])
                pool.tensor_tensor(rstd[:, 0:cols], var[:, 0:cols], neg_half[:, 0:cols], ALU.pow).then_inc(rstd_ready, 1)

            def scaled(layer, name):
                t0, n = norm_tokens(layer, name)
                r = KD * norm_at(layer, name)
                wait_emptied(pool, layer, name + "b")

                def low(k):
                    pool.wait_ge(h_hi_ready, r + k + 1)
                    pool.tensor_tensor(h_lo[:, k, t0:t0 + n], scratch[:, k % 4, 0:n], h_hi[:, k, t0:t0 + n].bitcast(F32),
                                       ALU.subtract).then_inc(h_lo_ready, 1)

                for k in range(KD + 2):
                    if k >= 2:
                        low(k - 2)
                    if k < KD:
                        if k >= 4:
                            pool.wait_ge(h_lo_ready, r + k - 3)
                        pool.tensor_tensor(scratch[:, k % 4, 0:n], x[:, k, t0:t0 + n], rstd_rows[:, 0, 0:n],
                                           ALU.mult).then_inc(scaled_ready, 1)

            step(pool.memset(neg_half[:], -0.5))
            for layer in range(DEPTH):
                t0, nt = tokens_of(layer)
                nq_tiles = nt // P

                def ready_bias(hd):
                    n = layer * HEADS + hd
                    pool.wait_ge(bias_landed[n % 2], 64 * (n // 2 + 1))
                    b = bias[:, n % 2]
                    step(pool.tensor_scalar(b, b, 8.0, None, ALU.mult))
                    pool.tensor_tensor(b, b, cc("near").rearrange("p (t k) -> p t k", t=2), ALU.add).then_inc(bias_ready, 1)

                power(layer, "n1", TOK // P)
                scaled(layer, "n1")
                if layer == 0:
                    pool.wait_ge(small_landed, 32)
                ready_bias(0)
                ready_bias(1)
                power(layer, "cs", nq_tiles + 4)

                def finish_rope(name, tile):
                    r = len(ROPES) * layer + ROPES.index(name)
                    dim = 64 if name.startswith("rw") else 32
                    rows = slice(64, 96) if name[1] in "ku" else slice(0, P)
                    wait_emptied(pool, layer, name)
                    if r:
                        pool.wait_ge(rope_done, r)
                    part = tile[rows, CTX:TOK]
                    step(pool.tensor_tensor(part, part, cc(f"cos{dim}")[rows], ALU.mult))
                    pool.tensor_tensor(part, part, scratch[rows, r % 4, 0:LAT], ALU.add).then_inc(rope_done, 1)

                tiles = [wq[:, 0], wq[:, 1], wk[:, 0], mk[:, 0], dq[:, 0], dq[:, 1], dk[:, 0], dk[:, 1]]
                tiles += [mq[:, hd] for hd in range(HEADS)]
                for n, name in enumerate(ROPES):
                    finish_rope(name, tiles[n])
                    if name == "rkr":
                        pool.wait_ge(rope_done, len(ROPES) * layer + n + 1)
                        for hd in range(1, HEADS):
                            pool.tensor_copy(mk[64:96, hd, :], mk[64:96, 0, :]).then_inc(kr_copied, 1)
                            pool.wait_ge(kr_copied, 3 * layer + hd)
                ready_bias(2)
                ready_bias(3)
                power(layer, "ds", 4 * nq_tiles)
                for n, k in enumerate((6, 7, 4, 5, 0, 1, 2, 3)):
                    pool.wait_ge(o_hi_ready, KD * layer + n + 1)
                    pool.tensor_tensor(o_lo[:, k, t0:], BRANCH_TILES[k][:, t0:], o_hi[:, k, t0:].bitcast(F32),
                                       ALU.subtract).then_inc(o_lo_ready, 1)
                for m in range(KD):
                    wait_emptied(pool, layer, ("b", m, 3))
                    s = [scratch[:, i, 0:nt] for i in range(4)]
                    pool.tensor_tensor(s[0], s[0], s[1], ALU.add)
                    step(pool.tensor_tensor(s[2], s[2], s[3], ALU.add))
                    pool.tensor_tensor(s[0], s[0], s[2], ALU.add).then_inc(y_sum_ready, 1)
                power(layer, "n2", nq_tiles)
                scaled(layer, "n2")
                for q in range(QUARTERS):
                    for m in range(HID):
                        f = (layer * QUARTERS + q) * HID + m
                        wait_emptied(pool, layer, ("f1", q, m))
                        s = scratch[:, f % 4, 0:nt]
                        pool.tensor_tensor(s, s, s, ALU.mult).then_inc(relu2_ready, 1)
            power(DEPTH, "n1", LAT // P)


def kernel(**inputs):
    import concourse.bacc as bacc
    from concourse.bass_utils import run_bass_kernel_spmd

    a = {k: np.ascontiguousarray(v) for k, v in inputs.items()}

    def columns(v):
        return v.reshape(-1, P).T

    def rows(v):
        return np.broadcast_to(v.reshape(1, -1), (P, v.size))

    par = []
    for layer in range(DEPTH):
        par += [columns(a["norm_mix"][layer]), columns(a["norm_ffn"][layer]), columns(a["b_ada"][layer]),
                columns(a["mla_q_norm"][layer]), columns(a["mla_kv_norm"][layer]),
                np.concatenate([a["diff_subln"][layer]] * 2).reshape(P, 1), columns(a["b_gate"][layer]),
                rows(a["diff_lambda"][layer]), rows(a["win_sink"][layer])]
    par.append(columns(a["final_norm"]))
    feeds = {
        "xT": np.concatenate([a["ctx"][0], a["x"][0]]).T.reshape(KD, P, TOK).transpose(1, 0, 2),
        "c2": np.stack([columns(a["c_ctx"]), columns(a["c"][0])], axis=2),
        "con_in": constants(),
        "par_in": np.concatenate(par, axis=1),
        "rpb": np.tile(np.pad(a["na_rpb"], ((0, 0), (0, 0), (0, 0), (48, 48))), (1, 1, 1, GRID_W)),
        **{n: a[n] for n in ("w_ada", "w_in", "w_uq", "w_ukv", "w_gate", "w_branch", "w_out", "w_ff1", "w_ff2")},
    }
    nc = bacc.Bacc("TRN2", target_bir_lowering=False, num_devices=1)
    arrays, args = {}, []
    for name, v in feeds.items():
        v = np.ascontiguousarray(v)
        arrays[f"{name}_dram"] = v
        args.append(nc.dram_tensor(f"{name}_dram", v.shape, mybir.dt.from_np(v.dtype), kind="ExternalInput").ap())
    args.append(nc.dram_tensor("out_dram", (D, LAT), F32, kind="ExternalOutput").ap())
    block_program(nc, *args)
    r = run_bass_kernel_spmd(nc, [arrays], core_ids=[0])
    return np.ascontiguousarray(r.results[0]["out_dram"].T).reshape(1, LAT, D)
```

```python
from contextlib import ExitStack

import numpy as np

import concourse.bass as bass
from concourse import mybir

F32 = mybir.dt.float32
F32R = mybir.dt.float32r
ALU = mybir.AluOpType
ACT = mybir.ActivationFunctionType
AX_X = mybir.AxisListType.X

P = 128
D = 1024
KD = D // P
CTX = 256
LAT = 256
TOK = CTX + LAT
DEPTH = 2
FFN = 4 * D
EPS = 1e-6
MASKED = -1e30
IN_WIDTH = 2464
HEADS = 4
NA_SCALE = WIN_SCALE = 64 ** -0.5
DIFF_SCALE = 32 ** -0.5
MLA_SCALE = 96 ** -0.5
GRID_W = 64
RPB_PAD = 127
RPB_ROW = GRID_W * RPB_PAD
LAMBDA_INIT = [0.8 - 0.6 * float(np.exp(-0.3 * layer)) for layer in range(DEPTH)]

C_CQ, C_CKV, C_DQ, C_DK, C_DV = 0, 256, 416, 672, 928
C_WQ, C_WKV, C_NQ, C_NK, C_NV = 1184, 1440, 1696, 1952, 2208
V_MLA, V_DIFF, V_NA, V_WIN, V_WIDTH = 0, 256, 512, 768, 896

_PAR = [("norm_mix", KD), ("norm_ffn", KD), ("b_ada", 48), ("q_norm", 2), ("kv_norm", 1),
        ("subln", 1), ("b_gate", 32), ("lam", 128), ("sink", HEADS)]
PAR_LAYER = sum(w for _, w in _PAR)
PAR_WIDTH = DEPTH * PAR_LAYER + KD


def par_at(layer, name):
    off = layer * PAR_LAYER
    for n, w in _PAR:
        if n == name:
            return off, off + w
        off += w
    raise KeyError(name)


_CON = [("ident", P), ("ones", P), ("head_ones", 2), ("rot64", P), ("rot32", P),
        ("cos64", LAT), ("sin64", LAT), ("cos32", LAT), ("sin32", LAT),
        ("band", 2 * LAT), ("near", 2 * LAT)]
CON_WIDTH = sum(w for _, w in _CON)


def con_at(name):
    off = 0
    for n, w in _CON:
        if n == name:
            return off, off + w
        off += w
    raise KeyError(name)


def constants():
    c = {"ident": np.eye(P), "ones": np.ones((P, P)), "head_ones": np.kron(np.eye(2), np.ones((64, 1)))}
    for dim in (64, 32):
        q = dim // 4
        rot = np.zeros((P, P))
        for i in range(P):
            block, j = i - i % dim, i % dim
            part = j // q
            rot[i, block + j + (q if part % 2 == 0 else -q)] = -1.0 if part % 2 == 0 else 1.0
        c[f"rot{dim}"] = rot.T
        inv = np.float32(10000.0) ** (-np.arange(q, dtype=np.float32) / np.float32(q))
        t = np.arange(LAT)
        row = (t // GRID_W).astype(np.float32)[:, None] * inv
        col = (t % GRID_W).astype(np.float32)[:, None] * inv
        ang = np.concatenate([row, row, col, col], axis=1).astype(np.float64).T
        c[f"cos{dim}"] = np.tile(np.cos(ang), (P // dim, 1))
        c[f"sin{dim}"] = np.tile(np.sin(ang), (P // dim, 1))
    k = np.arange(LAT)
    band, near = np.zeros((P, 2, LAT)), np.zeros((P, 2, LAT))
    for t in range(2):
        q = t * P + np.arange(P)[:, None]
        band[:, t] = np.where(np.abs(q - k) <= 128, 0.0, 8 * MASKED)
        start = np.clip(q % GRID_W - 8, 0, GRID_W - 16)
        inside = (k % GRID_W >= start) & (k % GRID_W < start + 16)
        near[:, t] = np.where(inside, 0.0, MASKED)
    c["band"], c["near"] = band.reshape(P, -1), near.reshape(P, -1)
    return np.concatenate([c[n] for n, _ in _CON], axis=1).astype(np.float32)


RAW_SLOTS = 2
SLOTS = 4
RING = 5
ATTN_RING = 3
QUARTERS = 4
HID = FFN // QUARTERS // P
PAIRS = HEADS // 2
ADA_BLOCKS = 6 * D // 256
ADA_BATCHES = [(0, 0, 8), (0, 8, 16), (1, 0, 24)]
ADA_ROWS = 4 * max(n for _, _, n in ADA_BATCHES)


def items_of(layer):
    parts = ("lat", "ctx") if layer < DEPTH - 1 else ("lat",)

    def pairs(kind, which, part):
        return [(kind, p, part, t) for p in which for t in range(2)]

    out = pairs("na", [0], "lat")
    if len(parts) > 1:
        out += pairs("na", [0, 1], "ctx")
    for part in parts:
        out += pairs("win", [0, 1], part)
    out += pairs("na", [1], "lat")
    for part in parts:
        out += [("diff", h, part, t) for p in range(PAIRS) for t in range(2) for h in (2 * p, 2 * p + 1)]
    for p in range(PAIRS):
        for part in parts:
            out += pairs("mla", [p], part)
    return out


FF_ORDER = [("f1", 0), ("f1", 1), ("f2", 0), ("f1", 2), ("f2", 1), ("f1", 3), ("f2", 2), ("f2", 3)]


def ada_blocks(batch):
    layer, first, n = ADA_BATCHES[batch]
    return [(batch, layer, first + i, i) for i in range(n)]


def units_of(layer):
    out = [("a", *b) for b in ada_blocks(0)] if layer == 0 else []
    out += ["cq", "ckv", "nq", "nk", "nv", "wq", "wkv", "dq", "dk", "dv", "uq", "ukv"]
    if layer == 0:
        out += [("a", *b) for n in (1, 2) for b in ada_blocks(n)]
    for m in range(KD):
        out += [("g", m, 0), ("g", m, 1), ("b", m)]
    out += [("o", i) for i in range(4)]
    for kind, q in FF_ORDER:
        out += [(kind, q, i) for i in range(4)]
    return out


def groups_of(layer):
    a, v = "act", "dve"
    out = ([(("at", 0), v)] if layer == 0 else []) + [("n1", v), ("n1b", v), ("cq0", a), ("cq1", a), ("ckv", a), ("kr", a), ("nq0", a), ("nq1", a),
           ("cs", v), ("nk0", a), ("nk1", a), ("cb0", v), ("cb1", v)]
    out += [(f"nv{t}", v) for t in range(4)] + [("wq0", a), ("wq1", a), ("wk", a)]
    out += [(f"wv{t}", v) for t in range(4)] + [("dq0", a), ("dq1", a)]
    out += [(n, v) for n in ("rwq0", "rwq1", "rwk", "rkr")] + [("dk0", a), ("dk1", a)]
    out += [(f"dv{t}", v) for t in range(4)]
    out += [(n, v) for n in ("rdq0", "rdq1", "rdk0", "rdk1")]
    out += [(f"uq{h}", a) for h in range(HEADS)] + [(f"uk{h}", a) for h in range(HEADS)]
    out += [(f"uv{t}", v) for t in range(4)] + [(f"ruq{h}", v) for h in range(HEADS)]
    items = items_of(layer)
    for j in range(len(items) + 1):
        if j < len(items):
            out += [(("T", j, lane), a) for lane in range(1 if items[j][0] == "diff" else 2)]
        if j:
            out.append((("PV", j - 1), v))
    if layer == 0:
        out += [(("at", 1), v), (("at", 2), v)]
    out += [("ds", v), ("db0", v), ("db1", v)]
    for m in range(KD):
        out += [(("g", m, i), a) for i in range(4)] + [(("b", m, i), v) for i in range(4)]
    out += [(("o", m), v) for m in range(KD)] + [("n2", v), ("n2b", v)]
    for kind, q in FF_ORDER:
        out += [((kind, q, m), a if kind == "f1" else v) for m in range(KD)]
    return out


UNITS = [(layer, u) for layer in range(DEPTH) for u in units_of(layer)]
UNIT_AT = {key: i for i, key in enumerate(UNITS)}
GROUPS = [((layer, n), e) for layer in range(DEPTH) for n, e in groups_of(layer)] + [
    ((DEPTH, "n1"), "dve"), ((DEPTH, "n1b"), "dve")]
GROUP_AT = {key: i for i, (key, _) in enumerate(GROUPS)}
ROPES = ["rwq0", "rwq1", "rwk", "rkr", "rdq0", "rdq1", "rdk0", "rdk1", "ruq0", "ruq1", "ruq2", "ruq3"]


def emptied(g):
    engine = GROUPS[g][1]
    return engine, sum(e == engine for _, e in GROUPS[:g + 1])


EMPTIED = [emptied(g) for g in range(len(GROUPS))]


def bank_of(g):
    inside = [isinstance(n, tuple) and n[0] in ("T", "PV") for (_, n), _ in GROUPS[:g + 1]]
    banks = [i % ATTN_RING if x else i % RING for i, x in enumerate(inside)]
    before = [i for i in range(g) if banks[i] == banks[g]]
    return banks[g], before[-1] if before else None


BANK_OF = [bank_of(g) for g in range(len(GROUPS))]


def slices_of(kind):
    if kind == "uq":
        return [(0, 384)], (2, 384)
    if kind == "ukv":
        return [(0, 512)], (1, 512)
    if kind == "ckv":
        return [(0, 128), (64, 96)], (KD, 160)
    if kind[0] == "b":
        return [(0, 128)], (KD, 128)
    return [(0, 128), (128, 128)], (KD, 256)


SLICES = [(u, i) for u, (_, kind) in enumerate(UNITS) for i in range(len(slices_of(kind)[0]))]
SLICE_AT = {key: n for n, key in enumerate(SLICES)}
LOW_BY = ["pool" if UNITS[u][1][0] == "a" and UNITS[u][1][1] > 0 and i == 1 else "dve" for u, i in SLICES]


def low_count(n):
    return sum(e == LOW_BY[n] for e in LOW_BY[:n + 1])


def last_group(n):
    u, i = SLICES[n]
    layer, kind = UNITS[u]
    if isinstance(kind, str):
        both = {"cq": ("cq0", "cq1"), "ckv": ("ckv", "kr"), "nq": ("nq0", "nq1"), "nk": ("nk0", "nk1"),
                "nv": ("nv3", "nv3"), "wq": ("wq0", "wq1"), "wkv": ("wk", "wv3"), "dq": ("dq0", "dq1"),
                "dk": ("dk0", "dk1"), "dv": ("dv3", "dv3"), "uq": ("uq3",), "ukv": ("uv3",)}
        return GROUP_AT[layer, both[kind][i]]
    if kind[0] == "a":
        return None
    if kind[0] == "g":
        return GROUP_AT[layer, ("g", kind[1], 2 * kind[2] + i)]
    if kind[0] == "b":
        return GROUP_AT[layer, ("b", kind[1], 3)]
    if kind[0] == "o":
        return GROUP_AT[layer, ("o", 2 * kind[1] + i)]
    return GROUP_AT[layer, (kind[0], kind[1], 2 * kind[2] + i)]


ADA_UNITS = [u for u, (_, kind) in enumerate(UNITS) if kind[0] == "a"]


def tokens_of(layer):
    first = 0 if layer < DEPTH - 1 else CTX
    return first, TOK - first


def block_program(nc, xT, c2, con_in, par_in, rpb, w_ada, w_in, w_uq, w_ukv, w_gate, w_branch, w_out,
                  w_ff1, w_ff2, out):
    base = -(-nc.sbuf_base // 64) * 64
    at = [base]

    def place(size):
        here = at[0]
        at[0] += -(-size // 64) * 64
        return here

    def sb(name, shape, dtype=F32, offset=None):
        size = 4 * int(np.prod(shape[1:]))
        return nc.alloc_sbuf_tensor_at(name, shape, dtype, offset=place(size) if offset is None else offset)

    x = sb("x", [P, KD, TOK])
    h_hi = sb("h_hi", [P, KD, TOK], F32R)
    h_lo = sb("h_lo", [P, KD, TOK], F32R)
    con = sb("con", [P, CON_WIDTH])
    par = sb("par", [P, PAR_WIDTH])
    raw = sb("raw", [P, RAW_SLOTS, 2048])
    w_hi = sb("w_hi", [P, SLOTS, 1024], F32R)
    w_lo = sb("w_lo", [P, SLOTS, 1024], F32R)
    scratch = sb("scratch", [P, 4, TOK])
    square_sum = sb("square_sum", [P, TOK])
    diag_at = place(4 * 8 * P)
    diag = sb("diag", [P, 8, P], offset=diag_at)
    bias = sb("bias", [P, 2, 2, LAT])
    pair_q = sb("pair_q", [P, 2, 2, P])
    diff_q = sb("diff_q", [P, 4, P])
    silu_parts = sb("silu_parts", [P, KD, 2 * ADA_ROWS - 4], F32R)
    ada_rows = sb("ada_rows", [P, 2, 256])
    cvec = sb("cvec", [P, KD, 2])
    silu = sb("silu", [P, KD, 2])
    mods = sb("mods", [P, DEPTH, 48, 2])
    gain = sb("gain", [P, DEPTH, 2, KD, 2])
    half_gate_bias = sb("half_gate_bias", [P, DEPTH, 32])
    small = sb("small", [P, DEPTH, 16])
    lam_prod = sb("lam_prod", [P, 2, 32])
    var = sb("var", [P, 16])
    rstd = sb("rstd", [P, 16])
    neg_half = sb("neg_half", [P, 16])
    stats = sb("stats", [P, 4, 128])
    kv_at = place(20480 + 4 * 4 * V_WIDTH)
    dk = sb("dk", [P, 2, TOK], offset=kv_at)
    nk = sb("nk", [P, 2, TOK], offset=kv_at + 4096)
    wk = sb("wk", [P, 2, TOK], offset=kv_at + 8192)
    mk = sb("mk", [P, HEADS, TOK], offset=kv_at + 12288)
    v_sb = sb("v_sb", [P, 4, V_WIDTH], offset=kv_at + 20480)
    qp_at = place(32768)
    dq = sb("dq", [P, 2, TOK], offset=qp_at)
    nq = sb("nq", [P, 2, TOK], offset=qp_at + 4096)
    wq = sb("wq", [P, 2, TOK], offset=qp_at + 8192)
    mq = sb("mq", [P, HEADS, TOK], offset=qp_at + 12288)
    probs = [sb(f"probs{i}", [P, 2, TOK], offset=o) for i, o in enumerate((qp_at + 20480, qp_at + 24576, diag_at))]
    probs_t = [sb("probs_t", [P, 4, 2 * P], offset=qp_at + 28672), scratch[:, 2:4, :].rearrange("p a (k q) -> p (a k) q", q=2 * P)]
    cn_hi = sb("cn_hi", [P, 3, TOK], F32R, offset=qp_at + 20480)
    cn_lo = sb("cn_lo", [P, 3, TOK], F32R, offset=qp_at + 20480 + 6144)
    o_hi = sb("o_hi", [P, KD, TOK], F32R, offset=kv_at)
    o_lo = sb("o_lo", [P, KD, TOK], F32R, offset=kv_at + 16384)
    y_hi = sb("y_hi", [P, KD, TOK], F32R, offset=qp_at)
    y_lo = sb("y_lo", [P, KD, TOK], F32R, offset=qp_at + 16384)
    hid_hi = [sb("hid_hi0", [P, HID, TOK], F32R, offset=kv_at), sb("hid_hi1", [P, HID, TOK], F32R, offset=qp_at)]
    hid_lo = [sb("hid_lo0", [P, HID, TOK], F32R, offset=kv_at + 16384),
              sb("hid_lo1", [P, HID, TOK], F32R, offset=qp_at + 16384)]
    out_sb = sb("out_sb", [P, KD, LAT], offset=qp_at)
    latent = mq

    def cc(name, lo=0, hi=None):
        a, b = con_at(name)
        return con[:, a + lo:(b if hi is None else a + hi)]

    def pp(layer, name, i=None):
        a, b = par_at(layer, name)
        return par[:, a:b] if i is None else par[:, a + i:a + i + 1]

    NEG_LAM, SUBLN, LAM_SUM, LAM_EXP, NEG_SINK = 0, 1, 2, 4, 8

    def head_out(kind, h):
        return {"na": nq, "win": wq, "diff": dq, "mla": mq}[kind][:, h // 2, :]

    BRANCH_TILES = [head_out("mla", 0), head_out("mla", 2), head_out("diff", 0), head_out("diff", 2),
                    head_out("win", 0), head_out("win", 2), head_out("na", 0), head_out("na", 2)]

    with ExitStack() as ctx:
        ps = ctx.enter_context(nc.psum_tensor("ps", [P, RING + 2, 512], F32))
        ada_ps = ctx.enter_context(nc.psum_tensor("ada_ps", [P, 512], F32))
        scores = [ps[:, RING:RING + 2, :], ps[:, ATTN_RING:ATTN_RING + 2, :]]

        def sem(name):
            return ctx.enter_context(nc.semaphore(name))

        raw_landed = [sem(f"raw_landed{i}") for i in range(RAW_SLOTS)]
        bias_landed = sem("bias_landed")
        x_landed = sem("x_landed")
        c_landed = sem("c_landed")
        small_landed = sem("small_landed")
        stored = sem("stored")
        w_hi_done = sem("w_hi_done")
        w_lo_by_dve = sem("w_lo_by_dve")
        w_lo_by_pool = sem("w_lo_by_pool")
        group_done = sem("group_done")
        by_act = sem("by_act")
        by_dve = sem("by_dve")
        ada_done = sem("ada_done")
        ada_rows_ready = sem("ada_rows_ready")
        ada_sum_ready = sem("ada_sum_ready")
        tanh_ready = sem("tanh_ready")
        silu_ready = sem("silu_ready")
        silu_zero = sem("silu_zero")
        silu_hi = sem("silu_hi")
        squares_ready = sem("squares_ready")
        square_added = sem("square_added")
        latent_square_sum = sem("latent_square_sum")
        rstd_ready = sem("rstd_ready")
        diag_ready = sem("diag_ready")
        h_ready = sem("h_ready")
        h_hi_ready = sem("h_hi_ready")
        h_lo_ready = sem("h_lo_ready")
        latent_hi = sem("latent_hi")
        latent_lo = sem("latent_lo")
        rope_done = sem("rope_done")
        kr_copied = sem("kr_copied")
        wk_copied = sem("wk_copied")
        bias_ready = sem("bias_ready")
        query_ready = sem("query_ready")
        lam_sums = sem("lam_sums")
        lam_exps = sem("lam_exps")
        scores_ready = sem("scores_ready")
        shift_ready = sem("shift_ready")
        exp_done = sem("exp_done")
        probs_ready = sem("probs_ready")
        o_squares = sem("o_squares")
        o_hi_ready = sem("o_hi_ready")
        o_lo_ready = sem("o_lo_ready")
        y_sum_ready = sem("y_sum_ready")
        y_hi_ready = sem("y_hi_ready")
        y_lo_ready = sem("y_lo_ready")
        relu_ready = sem("relu_ready")
        relu2_ready = sem("relu2_ready")
        hid_hi_ready = sem("hid_hi_ready")
        hid_lo_ready = sem("hid_lo_ready")
        vector_step = sem("vector_step")
        gpsimd_step = sem("gpsimd_step")
        scalar_step = sem("scalar_step")
        out_ready = sem("out_ready")

        def wait_group(eng, layer, name):
            eng.wait_ge(group_done, GROUP_AT[layer, name] + 1)

        def wait_emptied(eng, layer, name):
            engine, n = EMPTIED[GROUP_AT[layer, name]]
            eng.wait_ge(by_act if engine == "act" else by_dve, n)

        def bank(layer, name):
            return ps[:, BANK_OF[GROUP_AT[layer, name]][0], :]

        def raw_dmas(u):
            kind = UNITS[u][1]
            return 2 if kind[0] == "g" and not isinstance(kind, str) else 1

        def landed_count(u):
            return 16 * sum(raw_dmas(v) for v in range(u % RAW_SLOTS, u + 1, RAW_SLOTS))

        def raw_view(u):
            k, w = slices_of(UNITS[u][1])[1]
            return raw[:, u % RAW_SLOTS, :k * w].rearrange("p (k c) -> p k c", k=k)

        def slice_view(tensor, n):
            u, i = SLICES[n]
            slices, (k, _) = slices_of(UNITS[u][1])
            w = slices[i][1]
            return tensor[:, n % SLOTS, :k * w].rearrange("p (k c) -> p k c", k=k)

        def slice_source(n):
            u, i = SLICES[n]
            c0, w = slices_of(UNITS[u][1])[0][i]
            return raw_view(u)[:, :, c0:c0 + w]

        def wait_low(eng, n):
            eng.wait_ge(w_lo_by_pool if LOW_BY[n] == "pool" else w_lo_by_dve, low_count(n))

        def wait_slot(eng, n):
            if n < SLOTS:
                return
            g = last_group(n - SLOTS)
            if g is None:
                eng.wait_ge(ada_done, ADA_UNITS.index(SLICES[n - SLOTS][0]) + 1)
            else:
                eng.wait_ge(group_done, g + 1)

        def cuts_after(u):
            mine = [SLICE_AT[u, i] + SLOTS for i in range(len(slices_of(UNITS[u][1])[0]))]
            return [n for n in mine if n < len(SLICES)]

        n_items = [len(items_of(layer)) for layer in range(DEPTH)]
        item_base = [sum(n_items[:layer]) for layer in range(DEPTH + 1)]
        norms = [(layer, n) for layer in range(DEPTH) for n in ("n1", "n2")] + [(DEPTH, "n1")]

        def norm_at(layer, n):
            return norms.index((layer, n))

        def norm_tokens(layer, n):
            if layer == DEPTH:
                return CTX, LAT
            return (0, TOK) if n == "n1" else tokens_of(layer)

        RSTD_AT = {(layer, n): 4 * layer + i + 1 for layer in range(DEPTH) for i, n in enumerate(("n1", "cs", "ds", "n2"))}
        RSTD_AT[DEPTH, "n1"] = 4 * DEPTH + 1
        DIAG_AT = {(layer, n): 5 * layer + i + 1 for layer in range(DEPTH) for i, n in enumerate(("n1", "cs", "ds0", "ds1", "n2"))}
        DIAG_AT[DEPTH, "n1"] = 5 * DEPTH + 1

        def parts_of(n):
            return [(0, 0, CTX), (1, CTX, TOK)] if n == TOK else [(1, 0, n)]

        def query_count(layer, j):
            return sum(it[0] != "mla" for prev in range(layer) for it in items_of(prev)) + sum(
                it[0] != "mla" for it in items_of(layer)[:j + 1])

        block = ctx.enter_context(nc.Block())

        @block.sync
        def _(sp):
            def load_unit(u):
                layer, kind = UNITS[u]
                if u >= RAW_SLOTS:
                    for i in range(len(slices_of(UNITS[u - RAW_SLOTS][1])[0])):
                        n = SLICE_AT[u - RAW_SLOTS, i]
                        wait_low(sp, n)
                    sp.wait_ge(w_hi_done, n + 1)
                dst = raw_view(u)
                s = raw_landed[u % RAW_SLOTS]

                def rows(w, c0, width):
                    return w[:, c0:c0 + width].rearrange("(k p) c -> p k c", p=P)

                if kind == "uq":
                    sp.dma_start(dst, rows(w_uq[layer], 0, 384)).then_inc(s, 16)
                elif kind == "ukv":
                    sp.dma_start(dst, rows(w_ukv[layer], 0, 512)).then_inc(s, 16)
                elif isinstance(kind, str):
                    c0 = {"cq": C_CQ, "ckv": C_CKV, "nq": C_NQ, "nk": C_NK, "nv": C_NV, "wq": C_WQ,
                          "wkv": C_WKV, "dq": C_DQ, "dk": C_DK, "dv": C_DV}[kind]
                    sp.dma_start(dst, rows(w_in[layer], c0, slices_of(kind)[1][1])).then_inc(s, 16)
                elif kind[0] == "a":
                    sp.dma_start(dst, rows(w_ada[kind[2]], kind[3] * 256, 256)).then_inc(s, 16)
                elif kind[0] == "g":
                    for i in range(2):
                        c0 = (2 * kind[2] + i) * D + kind[1] * P
                        sp.dma_start(dst[:, :, i * P:(i + 1) * P], rows(w_gate[layer], c0, P)).then_inc(s, 16)
                elif kind[0] == "b":
                    sp.dma_start(dst, rows(w_branch[layer], kind[1] * P, P)).then_inc(s, 16)
                elif kind[0] == "o":
                    sp.dma_start(dst, rows(w_out[layer], kind[1] * 256, 256)).then_inc(s, 16)
                elif kind[0] == "f1":
                    c0 = kind[1] * HID * P + kind[2] * 256
                    sp.dma_start(dst, rows(w_ff1[layer], c0, 256)).then_inc(s, 16)
                else:
                    r0 = kind[1] * HID * P
                    sp.dma_start(dst, rows(w_ff2[layer][r0:r0 + HID * P], kind[2] * 256, 256)).then_inc(s, 16)

            sp.dma_start(cvec[:], c2).then_inc(c_landed, 16)
            load_unit(0)
            load_unit(1)
            sp.dma_start(x[:], xT).then_inc(x_landed, 16)
            sp.dma_start(par[:], par_in).then_inc(small_landed, 16)
            sp.dma_start(con[:], con_in).then_inc(small_landed, 16)
            for u in range(RAW_SLOTS, len(UNITS)):
                load_unit(u)
            for m in range(KD):
                sp.wait_ge(out_ready, m + 1)
                sp.dma_start(out[m * P:(m + 1) * P, :], out_sb[:, m, :]).then_inc(stored, 16)
            sp.wait_ge(stored, 16 * KD)

        @block.tensor
        def _(pe):
            def begin(layer, name):
                here, before = BANK_OF[GROUP_AT[layer, name]]
                if before is not None:
                    engine, n = EMPTIED[before]
                    pe.wait_ge(by_act if engine == "act" else by_dve, n)
                return ps[:, here, :]

            def have_slice(n):
                pe.wait_ge(w_hi_done, n + 1)
                wait_low(pe, n)
                return slice_view(w_hi, n), slice_view(w_lo, n)

            def have_both(u):
                n = SLICE_AT[u, 0]
                assert n % 2 == 0
                have_slice(n)
                have_slice(n + 1)
                return [w[:, n % SLOTS:n % SLOTS + 2, :].rearrange("p s (k c) -> p k s c", k=KD) for w in (w_hi, w_lo)]

            def product3(dst, lhs, rhs, first, last):
                (lh, ll), (rh, rl) = lhs, rhs
                pe.matmul(dst, lh, rh, start=first, stop=False)
                pe.matmul(dst, lh, rl, start=False, stop=False)
                return pe.matmul(dst, ll, rh, start=False, stop=last)

            def weights_by_tokens(layer, name, n, c0, width, acts, first, ready=None):
                dst = begin(layer, name)[:width, 0:TOK - first]
                hi, lo = have_slice(n)
                kt = hi.shape[1]
                for k in range(kt):
                    if ready is not None:
                        pe.wait_ge(ready[0], ready[1] + k + 1)
                    mm = product3(dst, (hi[:, k, c0:c0 + width], lo[:, k, c0:c0 + width]),
                                  (acts[0][:, k, first:TOK], acts[1][:, k, first:TOK]), k == 0, k == kt - 1)
                mm.then_inc(group_done, 1)

            def two_while_arriving(layer, names, u, acts, first, ready):
                dst = [begin(layer, name)[:, 0:TOK - first] for name in names]
                parts = [have_slice(SLICE_AT[u, i]) for i in range(2)]
                for k in range(KD):
                    pe.wait_ge(ready[0], ready[1] + k + 1)
                    for i in range(2):
                        mm = product3(dst[i], (parts[i][0][:, k], parts[i][1][:, k]),
                                      (acts[0][:, k, first:TOK], acts[1][:, k, first:TOK]), k == 0, k == KD - 1)
                        if k == KD - 1:
                            mm.then_inc(group_done, 1)

            def tokens_by_weights(layer, name, t, cols, kt, acts, k0=0):
                dst = begin(layer, name)
                for k in range(kt):
                    rh, rl = cols(0, k), cols(1, k)
                    width = int(np.prod(rh.shape[1:]))
                    tt = slice(t * P, (t + 1) * P)
                    mm = product3(dst[:, 0:width], (acts[0][:, k0 + k, tt], acts[1][:, k0 + k, tt]), (rh, rl),
                                  k == 0, k == kt - 1)
                mm.then_inc(group_done, 1)

            def sums_of_squares(layer, name):
                t0, n = norm_tokens(layer, name)
                pe.wait_ge(square_added, (KD - 1) * (norm_at(layer, name) + 1))
                dst = begin(layer, name)
                for t in range(n // P):
                    mm = pe.matmul(dst[:, t:t + 1], square_sum[:, t * P:(t + 1) * P], cc("ones", 0, 1),
                                   start=True, stop=True, skip_group_check=True)
                mm.then_inc(group_done, 1)

            def spread(layer, name, key, blocks, b0=0):
                pe.wait_ge(diag_ready, DIAG_AT[layer, key])
                dst = begin(layer, name)
                pe.matmul(dst[:, 0:blocks * P], cc("ones"), diag[:, b0:b0 + blocks, :].rearrange("p a b -> p (a b)"),
                          start=True, stop=True).then_inc(group_done, 1)

            def ada_block(u):
                _, batch, _, _, i = UNITS[u][1]
                size = ADA_BATCHES[batch][2]
                hi, lo = have_both(u)
                at_ = ADA_ROWS - 4 - 4 * i
                if batch and i == 0:
                    pe.wait_ge(ada_rows_ready, batch)
                for k in range(KD):
                    for w in (hi, lo):
                        mm = pe.matmul(ada_ps[0:4 * size, 0:256], silu_parts[:, k, at_:at_ + 4 * size], w[:, k],
                                       start=(i == 0 and k == 0 and w is hi),
                                       stop=(i == size - 1 and k == KD - 1 and w is lo), skip_group_check=True)
                mm.then_inc(ada_done, 1)

            def ada_turn(batch):
                rows = 4 * ADA_BATCHES[batch][2]
                pe.wait_ge(ada_rows_ready, batch + 1)
                dst = begin(0, ("at", batch))
                for half in range(2):
                    mm = pe.transpose(dst[:, half * P:half * P + rows], ada_rows[0:rows, batch % 2, half * P:(half + 1) * P],
                                      cc("ident", 0, rows)[0:rows])
                mm.then_inc(group_done, 1)

            def rotate(layer, name, src, rows, dim):
                dst = begin(layer, name)
                pe.matmul(dst[rows, 0:LAT], cc(f"rot{dim}")[rows, rows], src[rows, CTX:TOK],
                          start=True, stop=True).then_inc(group_done, 1)

            pe.wait_ge(silu_ready, 1)
            for u in ADA_UNITS[:ADA_BATCHES[0][2]]:
                ada_block(u)
            pe.wait_ge(small_landed, 32)
            ada_turn(0)

            for layer in range(DEPTH):
                t0, nt = tokens_of(layer)
                block_at = {name: UNIT_AT[layer, name] for name in units_of(layer)}
                part = {name: [SLICE_AT[u, i] for i in range(len(slices_of(UNITS[u][1])[0]))] for name, u in block_at.items()}
                h = (h_hi, h_lo)
                full = slice(0, P)

                sums_of_squares(layer, "n1")
                spread(layer, "n1b", "n1", TOK // P)
                two_while_arriving(layer, ("cq0", "cq1"), block_at["cq"], h, t0, (h_lo_ready, KD * norm_at(layer, "n1")))
                weights_by_tokens(layer, "ckv", part["ckv"][0], 0, P, h, 0)
                weights_by_tokens(layer, "kr", part["ckv"][1], 0, 96, h, 0)
                for i in range(2):
                    weights_by_tokens(layer, f"nq{i}", part["nq"][i], 0, P, h, t0)
                dst = begin(layer, "cs")
                pe.wait_ge(latent_square_sum, layer + 1)
                wait_emptied(pe, layer, "ckv")
                nq_tiles = nt // P
                for t in range(nq_tiles):
                    pe.matmul(dst[:, t:t + 1], scratch[:, 0, t * P:(t + 1) * P], cc("ones", 0, 1),
                              start=True, stop=True, skip_group_check=True)
                for t in range(TOK // P):
                    mm = pe.matmul(dst[:, nq_tiles + t:nq_tiles + t + 1], scratch[:, 2, t * P:(t + 1) * P],
                                   cc("ones", 0, 1), start=True, stop=True, skip_group_check=True)
                mm.then_inc(group_done, 1)
                for i in range(2):
                    weights_by_tokens(layer, f"nk{i}", part["nk"][i], 0, P, h, 0)
                spread(layer, "cb0", "cs", nq_tiles)
                spread(layer, "cb1", "cs", TOK // P, nq_tiles)
                both = have_both(block_at["nv"])
                for t in range(4):
                    tokens_by_weights(layer, f"nv{t}", t, lambda low, k: both[low][:, k], KD, h)
                for i in range(2):
                    weights_by_tokens(layer, f"wq{i}", part["wq"][i], 0, P, h, t0)
                weights_by_tokens(layer, "wk", part["wkv"][0], 0, P, h, 0)
                one = have_slice(part["wkv"][1])
                for t in range(4):
                    tokens_by_weights(layer, f"wv{t}", t, lambda low, k: one[low][:, k], KD, h)
                for i in range(2):
                    weights_by_tokens(layer, f"dq{i}", part["dq"][i], 0, P, h, t0)
                wait_emptied(pe, layer, "wk")
                rotate(layer, "rwq0", wq[:, 0], full, 64)
                rotate(layer, "rwq1", wq[:, 1], full, 64)
                rotate(layer, "rwk", wk[:, 0], full, 64)
                rotate(layer, "rkr", mk[:, 0], slice(64, 96), 32)
                for i in range(2):
                    weights_by_tokens(layer, f"dk{i}", part["dk"][i], 0, P, h, 0)
                both = have_both(block_at["dv"])
                for t in range(4):
                    tokens_by_weights(layer, f"dv{t}", t, lambda low, k: both[low][:, k], KD, h)
                wait_emptied(pe, layer, "dk1")
                for i in range(2):
                    rotate(layer, f"rdq{i}", dq[:, i], full, 32)
                for i in range(2):
                    rotate(layer, f"rdk{i}", dk[:, i], full, 32)
                pe.wait_ge(latent_lo, 3 * layer + 3)
                cn = (cn_hi, cn_lo)
                for hd in range(HEADS):
                    weights_by_tokens(layer, f"uq{hd}", part["uq"][0], hd * 96, 96, cn, t0)
                ckvn = (cn_hi[:, 2:3], cn_lo[:, 2:3])
                for hd in range(HEADS):
                    weights_by_tokens(layer, f"uk{hd}", part["ukv"][0], hd * P, 64, ckvn, 0)
                one = have_slice(part["ukv"][0])
                for t in range(4):
                    tokens_by_weights(layer, f"uv{t}", t, lambda low, k: one[low][:, k].rearrange(
                        "p (h c) -> p h c", h=HEADS)[:, :, 64:128], 1, cn, 2)
                wait_emptied(pe, layer, "uq3")
                for hd in range(HEADS):
                    rotate(layer, f"ruq{hd}", mq[:, hd], slice(64, 96), 32)

                items = items_of(layer)
                wait_emptied(pe, layer, "uk3")
                wait_emptied(pe, layer, "ruq3")
                pe.wait_ge(rope_done, len(ROPES) * (layer + 1))
                pe.wait_ge(kr_copied, 3 * (layer + 1))
                pe.wait_ge(wk_copied, layer + 1)

                def score_item(j):
                    kind, which, part_, t = items[j]
                    nkeys = TOK if part_ == "lat" else CTX
                    col = (CTX if part_ == "lat" else 0) + t * P
                    if kind != "mla":
                        pe.wait_ge(query_ready, query_count(layer, j))
                    for lane in range(2):
                        if kind == "diff":
                            qa, ka = diff_q[:, 2 * (which % 2) + lane, :], dk[:, which // 2, 0:nkeys]
                        elif kind == "mla":
                            hd = 2 * which + lane
                            qa, ka = mq[0:96, hd, col:col + P], mk[0:96, hd, 0:nkeys]
                        else:
                            qa = pair_q[:, j % 2, lane, :]
                            ka = (nk if kind == "na" else wk)[:, which, 0:nkeys]
                        mm = pe.matmul(scores[j % 2][:, lane, 0:nkeys], qa, ka, start=True, stop=True)
                    mm.then_inc(scores_ready, 1)

                def turn_item(j):
                    kind, which, part_, t = items[j]
                    ntile = (TOK if part_ == "lat" else CTX) // P
                    pe.wait_ge(probs_ready, item_base[layer] + j + 1)
                    for lane in range(1 if kind == "diff" else 2):
                        dst = begin(layer, ("T", j, lane))
                        for kt in range(ntile):
                            mm = pe.transpose(dst[:, kt * P:(kt + 1) * P], probs[j % 3][:, lane, kt * P:(kt + 1) * P],
                                              cc("ident"))
                        mm.then_inc(group_done, 1)

                def value_item(j):
                    kind, which, part_, t = items[j]
                    ntile = (TOK if part_ == "lat" else CTX) // P
                    if kind == "diff":
                        heads = [(which % 2, V_DIFF + 64 * which)]
                    elif kind == "win":
                        heads = [(lane, V_WIN + 64 * which) for lane in range(2)]
                    else:
                        heads = [(lane, (V_NA if kind == "na" else V_MLA) + 64 * (2 * which + lane)) for lane in range(2)]
                    wait_emptied(pe, layer, ("T", j, len(heads) - 1))
                    dst = begin(layer, ("PV", j))
                    for kt in range(ntile):
                        for lane, (half, v0) in enumerate(heads):
                            mm = pe.matmul(dst[64 * half:64 * half + 64, 0:P], v_sb[:, kt, v0:v0 + 64],
                                           probs_t[j % 2][:, kt, lane * P:(lane + 1) * P],
                                           start=(kt == 0), stop=(kt == ntile - 1))
                    mm.then_inc(group_done, 1)

                for j in range(len(items) + 3):
                    if j < len(items):
                        if j >= 2:
                            pe.wait_ge(exp_done, item_base[layer] + j - 1)
                        score_item(j)
                    if 2 <= j < len(items) + 2:
                        turn_item(j - 2)
                    if j < len(items):
                        if layer == 0:
                            ada_block(ADA_UNITS[ADA_BATCHES[0][2] + j])
                    if j >= 3:
                        value_item(j - 3)
                if layer == 0:
                    ada_turn(1)
                    ada_turn(2)

                dst = begin(layer, "ds")
                for pair in range(2):
                    pe.wait_ge(o_squares, 2 * layer + pair + 1)
                    for t in range(nq_tiles):
                        col = 2 * (pair * nq_tiles + t)
                        mm = pe.matmul(dst[:, col:col + 2], scratch[:, pair, t * P:(t + 1) * P], cc("head_ones"),
                                       start=True, stop=True, skip_group_check=True)
                mm.then_inc(group_done, 1)
                for pair in range(2):
                    pe.wait_ge(diag_ready, DIAG_AT[layer, f"ds{pair}"])
                    dst = begin(layer, f"db{pair}")
                    for a in range(2):
                        mm = pe.matmul(dst[64 * a:64 * a + 64, 0:nt], cc("ones", 0, 64),
                                       diag[:, a * nq_tiles:(a + 1) * nq_tiles, :].rearrange("p a b -> p (a b)"),
                                       start=True, stop=True)
                    mm.then_inc(group_done, 1)

                for m in range(KD):
                    for i in range(4):
                        weights_by_tokens(layer, ("g", m, i), part["g", m, i // 2][i % 2], 0, P, h, t0)
                    hi, lo = have_slice(part["b", m][0])
                    pe.wait_ge(o_lo_ready, KD * (layer + 1))
                    for i in range(4):
                        dst = begin(layer, ("b", m, i))[:, 0:nt]
                        for k in (2 * i, 2 * i + 1):
                            mm = product3(dst, (hi[:, k], lo[:, k]), (o_hi[:, k, t0:], o_lo[:, k, t0:]),
                                          k % 2 == 0, k % 2 == 1)
                        mm.then_inc(group_done, 1)
                for m in range(KD):
                    weights_by_tokens(layer, ("o", m), part["o", m // 2][m % 2], 0, P, (y_hi, y_lo), t0,
                                      (y_lo_ready, KD * layer) if m == 0 else None)

                sums_of_squares(layer, "n2")
                spread(layer, "n2b", "n2", nq_tiles)
                for kind, q in FF_ORDER:
                    for m in range(KD):
                        if (kind, q) == ("f1", 0) and m < 2:
                            if m == 0:
                                two_while_arriving(layer, (("f1", 0, 0), ("f1", 0, 1)), block_at["f1", 0, 0], h, t0,
                                                   (h_lo_ready, KD * norm_at(layer, "n2")))
                        elif kind == "f1":
                            weights_by_tokens(layer, ("f1", q, m), part["f1", q, m // 2][m % 2], 0, P, h, t0)
                        else:
                            weights_by_tokens(layer, ("f2", q, m), part["f2", q, m // 2][m % 2], 0, P,
                                              (hid_hi[q % 2], hid_lo[q % 2]), t0,
                                              (hid_lo_ready, (layer * QUARTERS + q) * HID) if m == 0 else None)
            sums_of_squares(DEPTH, "n1")
            spread(DEPTH, "n1b", "n1", LAT // P)

        @block.scalar
        def _(act):
            def cut(n):
                u = SLICES[n][0]
                act.wait_ge(raw_landed[u % RAW_SLOTS], landed_count(u))
                wait_slot(act, n)
                act.activation(slice_view(w_hi, n), slice_source(n), ACT.Copy).then_inc(w_hi_done, 1)

            def cut_after(u, i=None):
                for n in cuts_after(u) if i is None else cuts_after(u)[i:i + 1]:
                    cut(n)

            def load_bias(layer, pair):
                if (layer, pair) != (0, 0):
                    lp, pp_ = (layer, 0) if pair else (layer - 1, 1)
                    act.wait_ge(shift_ready, item_base[lp] + items_of(lp).index(("na", pp_, "lat", 1)) + 1)
                for i in range(2):
                    for t in range(2):
                        for half in range(2):
                            r = 2 * t + half
                            start = rpb[layer, 2 * pair + i, 7 - r:8 - r, 63:64]
                            src = bass.AP(tensor=start.tensor, offset=start.offset,
                                          ap=[[RPB_PAD - 1, 64], [RPB_ROW, 4], [1, 64]])
                            dst = bias[64 * half:64 * half + 64, i, t, :].rearrange("p (w c) -> p w c", w=4)
                            act.dma_start(dst, src).then_inc(bias_landed, 16)

            def copy_out(layer, name, dst, rows=slice(0, P), width=TOK):
                wait_group(act, layer, name)
                act.activation(dst, bank(layer, name)[rows, 0:width], ACT.Copy).then_inc(by_act, 1)

            def square(layer, name, k):
                t0, n = norm_tokens(layer, name)
                if (layer, name) == (0, "n1"):
                    act.wait_ge(x_landed, 16)
                elif name == "n1":
                    wait_emptied(act, layer - 1, ("f2", QUARTERS - 1, k))
                else:
                    wait_emptied(act, layer, ("o", k))
                if k > 4:
                    act.wait_ge(square_added, (KD - 1) * norm_at(layer, name) + k - 4)
                dst = square_sum[:, 0:n] if k == 0 else scratch[:, k % 4, 0:n]
                act.activation(dst, x[:, k, t0:t0 + n], ACT.Square).then_inc(squares_ready, 1)

            def normed_hi(layer, name):
                t0, n = norm_tokens(layer, name)
                which = 0 if name == "n1" else 1
                for k in range(KD):
                    if k == KD - 1:
                        wait_emptied(act, layer, name + "b")
                    else:
                        act.wait_ge(h_ready, (KD - 1) * norm_at(layer, name) + k + 1)
                    for group, a, b in parts_of(n):
                        ins = act.activation(h_hi[:, k, t0 + a:t0 + b], scratch[:, k % 4, a:b], ACT.Identity,
                                             bias=mods[:, layer, 24 * which + k, group:group + 1])
                    ins.then_inc(h_hi_ready, 1)

            load_bias(0, 0)
            act.wait_ge(c_landed, 16)
            act.activation(silu[:], cvec[:], ACT.Tanh, scale=0.5).then_inc(tanh_ready, 1)
            act.wait_ge(silu_ready, 1)
            act.wait_ge(silu_zero, 1)
            act.activation(silu_parts[:, :, ADA_ROWS - 4:ADA_ROWS - 2], silu[:], ACT.Copy).then_inc(silu_hi, 1)
            for n in range(SLOTS):
                cut(n)
            for i, u in enumerate(ADA_UNITS[:ADA_BATCHES[0][2]]):
                cut_after(u)
                if i >= 4:
                    square(0, "n1", 2 * i - 8)
                    square(0, "n1", 2 * i - 7)
            for layer in range(DEPTH):
                t0, nt = tokens_of(layer)
                U = {name: UNIT_AT[layer, name] for name in units_of(layer)}
                act.wait_ge(lam_sums, layer + 1)
                act.activation(small[:, layer, LAM_EXP:LAM_EXP + 2], small[:, layer, LAM_SUM:LAM_SUM + 2],
                               ACT.Exp).then_inc(lam_exps, 1)
                normed_hi(layer, "n1")
                for i in range(2):
                    wait_group(act, layer, f"cq{i}")
                    act.activation(latent[:, i, 0:nt], bank(layer, f"cq{i}")[:, 0:nt], ACT.Copy)
                    act.activation(scratch[:, i, 0:nt], bank(layer, f"cq{i}")[:, 0:nt], ACT.Square).then_inc(by_act, 1)
                cut_after(U["cq"])
                wait_group(act, layer, "ckv")
                act.activation(latent[:, 2, :], bank(layer, "ckv"), ACT.Copy)
                act.activation(scratch[:, 2, :], bank(layer, "ckv"), ACT.Square).then_inc(by_act, 1)
                copy_out(layer, "kr", mk[64:96, 0, :], slice(64, 96))
                cut_after(U["ckv"])
                for i in range(2):
                    copy_out(layer, f"nq{i}", nq[:, i, t0:], width=nt)
                cut_after(U["nq"])
                for i in range(2):
                    copy_out(layer, f"nk{i}", nk[:, i, :])
                cut_after(U["nk"])
                for i in range(3):
                    first = t0 if i < 2 else 0
                    gamma = pp(layer, "q_norm", i) if i < 2 else pp(layer, "kv_norm")
                    wait_emptied(act, layer, f"cb{i // 2}")
                    act.activation(cn_hi[:, i, first:], latent[:, i, 0:TOK - first], ACT.Identity,
                                   scale=gamma).then_inc(latent_hi, 1)
                cut_after(U["nv"])
                for i in range(2):
                    copy_out(layer, f"wq{i}", wq[:, i, t0:], width=nt)
                cut_after(U["wq"])
                copy_out(layer, "wk", wk[:, 0, :])
                cut_after(U["wkv"])
                for i in range(2):
                    copy_out(layer, f"dq{i}", dq[:, i, t0:], width=nt)
                cut_after(U["dq"])
                for i in range(2):
                    copy_out(layer, f"dk{i}", dk[:, i, :])
                cut_after(U["dk"])
                act.wait_ge(rope_done, len(ROPES) * layer + ROPES.index("rwk") + 1)
                act.activation(wk[0:64, 1, :], wk[64:128, 0, :], ACT.Copy)
                act.activation(wk[64:128, 1, :], wk[64:128, 0, :], ACT.Copy).then_inc(scalar_step, 1)
                act.wait_ge(scalar_step, layer + 1)
                act.activation(wk[64:128, 0, :], wk[0:64, 0, :], ACT.Copy).then_inc(wk_copied, 1)
                cut_after(U["dv"])
                act.wait_ge(latent_lo, 3 * layer + 3)
                for hd in range(HEADS):
                    copy_out(layer, f"uq{hd}", mq[0:96, hd, t0:], slice(0, 96), nt)
                cut_after(U["uq"])
                for hd in range(HEADS):
                    copy_out(layer, f"uk{hd}", mk[0:64, hd, :], slice(0, 64))
                cut_after(U["ukv"])

                items = items_of(layer)
                scale = {"na": NA_SCALE, "win": WIN_SCALE, "diff": DIFF_SCALE, "mla": MLA_SCALE}

                def turned(j):
                    kind, hd, part, t = items[j]
                    ntile = (TOK if part == "lat" else CTX) // P
                    for lane in range(1 if kind == "diff" else 2):
                        wait_group(act, layer, ("T", j, lane))
                        act.activation(probs_t[j % 2][:, 0:ntile, lane * P:(lane + 1) * P],
                                       bank(layer, ("T", j, lane))[:, 0:ntile * P].rearrange("p (k q) -> p k q", q=P),
                                       ACT.Copy).then_inc(by_act, 1)

                for j in range(len(items) + 2):
                    if j == 2:
                        load_bias(layer, 1)
                    if j >= 2:
                        turned(j - 2)
                    if j < len(items):
                        kind, which, part_, t = items[j]
                        nkeys = TOK if part_ == "lat" else CTX
                        act.wait_ge(shift_ready, item_base[layer] + j + 1)
                        col = 2 * (item_base[layer] + j)
                        if kind == "win":
                            act.activation(stats[:, 3, col:col + 2], stats[:, 3, col:col + 2], ACT.Exp)
                        for lane in range(2):
                            mm = act.activation(probs[j % 3][:, lane, 0:nkeys], scores[j % 2][:, lane, 0:nkeys], ACT.Exp,
                                                bias=stats[:, 1, col + lane:col + lane + 1], scale=scale[kind],
                                                accum_out=stats[:, 2, col + lane:col + lane + 1])
                        mm.then_inc(exp_done, 1)
                        if layer == 0:
                            cut_after(ADA_UNITS[ADA_BATCHES[0][2] + j])
                if layer < DEPTH - 1:
                    load_bias(layer + 1, 0)
                last_diff = max(j for j, it in enumerate(items) if it[0] == "diff")
                wait_emptied(act, layer, ("PV", last_diff))
                for pair in range(2):
                    act.activation(scratch[:, pair, 0:nt], dq[:, pair, t0:], ACT.Square).then_inc(o_squares, 1)
                wait_emptied(act, layer, ("PV", len(items) - 1))
                for k in (6, 7, 4, 5, 0, 1, 2, 3):
                    if k in (2, 3):
                        wait_emptied(act, layer, f"db{k - 2}")
                    act.activation(o_hi[:, k, t0:], BRANCH_TILES[k][:, t0:], ACT.Copy).then_inc(o_hi_ready, 1)

                for m in range(KD):
                    if m:
                        act.wait_ge(y_lo_ready, KD * layer + m)
                    for i in range(4):
                        wait_group(act, layer, ("g", m, i))
                        act.activation(scratch[:, i, 0:nt], bank(layer, ("g", m, i))[:, 0:nt], ACT.Tanh, scale=0.5,
                                       bias=half_gate_bias[:, layer, i * KD + m:i * KD + m + 1]).then_inc(by_act, 1)
                        cut_after(U["g", m, i // 2], i % 2)
                    act.wait_ge(y_sum_ready, KD * layer + m + 1)
                    act.activation(y_hi[:, m, t0:], scratch[:, 0, 0:nt], ACT.Copy, scale=0.5).then_inc(y_hi_ready, 1)
                    cut_after(U["b", m])
                for m in range(KD):
                    cut_after(U["o", m // 2], m % 2)
                    square(layer, "n2", m)

                normed_hi(layer, "n2")

                def hidden_hi(q, m):
                    f = (layer * QUARTERS + q) * HID + m
                    act.wait_ge(relu2_ready, f + 1)
                    act.activation(hid_hi[q % 2][:, m, t0:], scratch[:, f % 4, 0:nt], ACT.Copy).then_inc(hid_hi_ready, 1)

                for kind, q in FF_ORDER:
                    for i in range(4):
                        if kind == "f1":
                            for m in (2 * i, 2 * i + 1):
                                f = (layer * QUARTERS + q) * HID + m
                                if f >= 4:
                                    act.wait_ge(hid_lo_ready, f - 3)
                                wait_group(act, layer, ("f1", q, m))
                                act.activation(scratch[:, f % 4, 0:nt], bank(layer, ("f1", q, m))[:, 0:nt],
                                               ACT.Relu).then_inc(by_act, 1)
                                if m:
                                    hidden_hi(q, m - 1)
                            if i == 3:
                                hidden_hi(q, HID - 1)
                        cut_after(U[kind, q, i])
                        if (kind, q) == ("f2", QUARTERS - 1):
                            square(layer + 1, "n1", 2 * i)
                            square(layer + 1, "n1", 2 * i + 1)

        @block.vector
        def _(dve):
            steps = [0]

            def step(ins):
                steps[0] += 1
                ins.then_inc(vector_step, 1)
                dve.wait_ge(vector_step, steps[0])

            def cut(n):
                if LOW_BY[n] == "dve":
                    dve.wait_ge(w_hi_done, n + 1)
                    dve.tensor_tensor(slice_view(w_lo, n), slice_source(n), slice_view(w_hi, n).bitcast(F32),
                                      ALU.subtract).then_inc(w_lo_by_dve, 1)

            def cut_after(u, i=None):
                for n in cuts_after(u) if i is None else cuts_after(u)[i:i + 1]:
                    cut(n)

            def variance(layer, name, cols, inverse):
                wait_group(dve, layer, name)
                b = bank(layer, name)
                for n, (c0, c1) in enumerate(cols):
                    ins = dve.tensor_scalar(var[:, c0:c1], b[:, c0:c1], inverse[n], EPS, ALU.mult, ALU.add)
                ins.then_inc(by_dve, 1)

            def diagonal(key, layer, blocks, source, b0=0, inc=True):
                ident = cc("ident").unsqueeze(1).to_broadcast([P, blocks, P])
                ins = dve.tensor_tensor(diag[:, b0:b0 + blocks, :], ident, source.unsqueeze(2).to_broadcast([P, blocks, P]),
                                        ALU.mult)
                if inc:
                    ins.then_inc(diag_ready, 1)

            def add_square(layer, name, k):
                n = norm_tokens(layer, name)[1]
                if k:
                    r = norm_at(layer, name)
                    dve.wait_ge(squares_ready, KD * r + k + 1)
                    if k > 1:
                        dve.wait_ge(square_added, (KD - 1) * r + k - 1)
                    dve.tensor_tensor(square_sum[:, 0:n], square_sum[:, 0:n], scratch[:, k % 4, 0:n],
                                      ALU.add).then_inc(square_added, 1)

            def rstd_of_tokens(layer, name):
                t0, n = norm_tokens(layer, name)
                variance(layer, name, [(0, n // P)], [1.0 / D])
                dve.wait_ge(rstd_ready, RSTD_AT[layer, name])
                diagonal(name, layer, n // P, rstd[:, 0:n // P])

            def modulated(layer, name):
                t0, n = norm_tokens(layer, name)
                which = 0 if name == "n1" else 1
                r = norm_at(layer, name)
                wait_group(dve, layer, name + "b")
                for k in range(KD + 1):
                    if k < KD:
                        for group, a, b in parts_of(n):
                            ins = dve.scalar_tensor_tensor(scratch[:, k % 4, a:b], x[:, k, t0 + a:t0 + b],
                                                           gain[:, layer, which, k, group:group + 1],
                                                           bank(layer, name + "b")[:, a:b], ALU.mult, ALU.mult)
                        ins.then_inc(h_ready if k < KD - 1 else by_dve, 1)
                    if k:
                        dve.wait_ge(h_hi_ready, KD * r + k)
                        for group, a, b in parts_of(n):
                            ins = dve.scalar_tensor_tensor(h_lo[:, k - 1, t0 + a:t0 + b], scratch[:, (k - 1) % 4, a:b],
                                                           mods[:, layer, 24 * which + k - 1, group:group + 1],
                                                           h_hi[:, k - 1, t0 + a:t0 + b].bitcast(F32), ALU.add, ALU.subtract)
                        ins.then_inc(h_lo_ready, 1)

            def modulations(batch):
                layer, first, size = ADA_BATCHES[batch]
                dst = mods[:, layer, 2 * first:2 * (first + size), :].rearrange("p (i h) g -> p h i g", h=2)
                b = pp(layer, "b_ada")[:, 2 * first:2 * (first + size)].rearrange("p (i h) -> p h i", h=2)
                b = b.unsqueeze(3).to_broadcast([P, 2, size, 2])
                wait_group(dve, 0, ("at", batch))
                src = bank(0, ("at", batch))[:, 0:2 * P].rearrange("p (h c) -> p h c", h=2)[:, :, 0:4 * size]
                src = src.rearrange("p h (i v g) -> p v h i g", v=2, g=2)
                step(dve.tensor_tensor(dst, src[:, 0], b, ALU.add))
                dve.tensor_tensor(dst, dst, src[:, 1], ALU.add).then_inc(by_dve, 1)
                wait_emptied(dve, 0, ("at", batch))

            def copy_ada_rows(batch):
                size = ADA_BATCHES[batch][2]
                dve.wait_ge(ada_done, sum(n for _, _, n in ADA_BATCHES[:batch + 1]))
                dve.tensor_copy(ada_rows[0:4 * size, batch % 2, :], ada_ps[0:4 * size, 0:256]).then_inc(ada_rows_ready, 1)

            def gains(layer, which):
                g = pp(layer, "norm_ffn" if which else "norm_mix").unsqueeze(2).to_broadcast([P, KD, 2])
                return dve.scalar_tensor_tensor(gain[:, layer, which], mods[:, layer, 24 * which + KD:24 * which + 2 * KD, :],
                                                1.0, g, ALU.add, ALU.mult)

            def residual(layer, name, mod, k):
                t0, nt = tokens_of(layer)
                wait_group(dve, layer, name)
                for group, a, b in parts_of(nt):
                    xs = x[:, k, t0 + a:t0 + b]
                    ins = dve.scalar_tensor_tensor(xs, bank(layer, name)[:, a:b], mods[:, layer, mod * KD + k, group:group + 1],
                                                   xs, ALU.mult, ALU.add)
                ins.then_inc(by_dve, 1)

            dve.wait_ge(tanh_ready, 1)
            step(dve.scalar_tensor_tensor(silu[:], silu[:], 1.0, cvec[:], ALU.add, ALU.mult))
            dve.tensor_scalar(silu[:], silu[:], 0.5, None, ALU.mult).then_inc(silu_ready, 1)
            dve.wait_ge(silu_hi, 1)
            dve.tensor_tensor(silu_parts[:, :, ADA_ROWS - 2:ADA_ROWS], silu[:],
                              silu_parts[:, :, ADA_ROWS - 4:ADA_ROWS - 2].bitcast(F32), ALU.subtract).then_inc(silu_ready, 1)
            for n in range(SLOTS):
                cut(n)
            dve.wait_ge(small_landed, 32)
            for layer in range(DEPTH):
                dve.tensor_scalar(half_gate_bias[:, layer, :], pp(layer, "b_gate"), 0.5, None, ALU.mult)
                dve.tensor_scalar(small[:, layer, NEG_SINK:NEG_SINK + HEADS], pp(layer, "sink"), -1.0, None, ALU.mult)
                dve.tensor_scalar(small[:, layer, SUBLN:SUBLN + 1], pp(layer, "subln"), 1.0 - LAMBDA_INIT[layer], None, ALU.mult)
                lam = pp(layer, "lam").rearrange("p (a b c) -> p a b c", a=2, b=2)
                step(dve.tensor_tensor(lam_prod[:], lam[:, :, 0, :], lam[:, :, 1, :], ALU.mult))
                dve.reduce_sum(small[:, layer, LAM_SUM:LAM_SUM + 2], lam_prod[:], AX_X).then_inc(lam_sums, 1)
                dve.wait_ge(lam_sums, layer + 1)
            for i, u in enumerate(ADA_UNITS[:ADA_BATCHES[0][2]]):
                cut_after(u)
                if i >= 4:
                    add_square(0, "n1", 2 * i - 8)
                    add_square(0, "n1", 2 * i - 7)
            copy_ada_rows(0)
            modulations(0)
            step(gains(0, 0))

            for layer in range(DEPTH):
                t0, nt = tokens_of(layer)
                U = {name: UNIT_AT[layer, name] for name in units_of(layer)}
                nq_tiles = nt // P
                dve.wait_ge(lam_exps, layer + 1)
                e = small[:, layer, LAM_EXP:LAM_EXP + 2]
                step(dve.tensor_tensor(small[:, layer, NEG_LAM:NEG_LAM + 1], e[:, 1:2], e[:, 0:1], ALU.subtract))
                step(dve.tensor_scalar(small[:, layer, NEG_LAM:NEG_LAM + 1], small[:, layer, NEG_LAM:NEG_LAM + 1],
                                       LAMBDA_INIT[layer], None, ALU.subtract))
                rstd_of_tokens(layer, "n1")
                modulated(layer, "n1")
                cut_after(U["cq"])
                for i in range(2):
                    wait_emptied(dve, layer, f"cq{i}")
                dve.tensor_tensor(scratch[:, 0, 0:nt], scratch[:, 0, 0:nt], scratch[:, 1, 0:nt],
                                  ALU.add).then_inc(latent_square_sum, 1)
                cut_after(U["ckv"])
                variance(layer, "cs", [(0, nq_tiles), (nq_tiles, nq_tiles + 4)], [1.0 / 256, 1.0 / 128])
                dve.wait_ge(rstd_ready, RSTD_AT[layer, "cs"])
                diagonal("cs", layer, nq_tiles + 4, rstd[:, 0:nq_tiles + 4])
                cut_after(U["nq"])
                for i in range(3):
                    n = nt if i < 2 else TOK
                    wait_group(dve, layer, f"cb{i // 2}")
                    ins = dve.tensor_tensor(latent[:, i, 0:n], latent[:, i, 0:n], bank(layer, f"cb{i // 2}")[:, 0:n], ALU.mult)
                    if i:
                        ins.then_inc(by_dve, 1)
                for i in range(3):
                    first = t0 if i < 2 else 0
                    gamma = pp(layer, "q_norm", i) if i < 2 else pp(layer, "kv_norm")
                    dve.wait_ge(latent_hi, 3 * layer + i + 1)
                    dve.scalar_tensor_tensor(cn_lo[:, i, first:], latent[:, i, 0:TOK - first], gamma,
                                             cn_hi[:, i, first:].bitcast(F32), ALU.mult, ALU.subtract).then_inc(latent_lo, 1)
                cut_after(U["nk"])

                def values(name, v0, width):
                    for t in range(4):
                        wait_group(dve, layer, f"{name}{t}")
                        dve.tensor_copy(v_sb[:, t, v0:v0 + width], bank(layer, f"{name}{t}")[:, 0:width]).then_inc(by_dve, 1)

                def turn_products(names):
                    for name in names:
                        r = len(ROPES) * layer + ROPES.index(name)
                        dim = 64 if name.startswith("rw") else 32
                        rows = slice(64, 96) if name[1] in "ku" else slice(0, P)
                        if r >= 4:
                            dve.wait_ge(rope_done, r - 3)
                        wait_group(dve, layer, name)
                        dve.tensor_tensor(scratch[rows, r % 4, 0:LAT], bank(layer, name)[rows, 0:LAT],
                                          cc(f"sin{dim}")[rows], ALU.mult).then_inc(by_dve, 1)

                values("nv", V_NA, 256)
                cut_after(U["nv"])
                cut_after(U["wq"])
                values("wv", V_WIN, 128)
                cut_after(U["wkv"])
                cut_after(U["dq"])
                turn_products(ROPES[0:4])
                cut_after(U["dk"])
                values("dv", V_DIFF, 256)
                cut_after(U["dv"])
                turn_products(ROPES[4:8])
                cut_after(U["uq"])
                values("uv", V_MLA, 256)
                cut_after(U["ukv"])
                turn_products(ROPES[8:12])

                items = items_of(layer)
                scale = {"na": NA_SCALE, "win": WIN_SCALE, "diff": DIFF_SCALE, "mla": MLA_SCALE}

                def shift(j):
                    kind, which, part_, t = items[j]
                    nkeys = TOK if part_ == "lat" else CTX
                    col = 2 * (item_base[layer] + j)
                    sc = scores[j % 2]
                    dve.wait_ge(scores_ready, item_base[layer] + j + 1)
                    if part_ == "lat" and kind == "na":
                        dve.wait_ge(bias_ready, layer * PAIRS + which + 1)
                        step(dve.scalar_tensor_tensor(sc[:, :, CTX:TOK], bias[:, :, t, :], 8.0, sc[:, :, CTX:TOK],
                                                      ALU.mult, ALU.add))
                    if part_ == "lat" and kind == "win":
                        band = cc("band").rearrange("p (t k) -> p t k", t=2)[:, t:t + 1, :].to_broadcast([P, 2, LAT])
                        step(dve.tensor_tensor(sc[:, :, CTX:TOK], sc[:, :, CTX:TOK], band, ALU.add))
                    step(dve.tensor_reduce(stats[:, 0, col:col + 2], sc[:, :, 0:nkeys], AX_X, ALU.max))
                    if kind == "win":
                        ns = small[:, layer, NEG_SINK + 2 * which:NEG_SINK + 2 * which + 2]
                        step(dve.scalar_tensor_tensor(stats[:, 1, col:col + 2], stats[:, 0, col:col + 2], -scale[kind], ns,
                                                      ALU.mult, ALU.min))
                        ins = dve.tensor_tensor(stats[:, 3, col:col + 2], stats[:, 1, col:col + 2], ns, ALU.subtract)
                    else:
                        ins = dve.tensor_scalar(stats[:, 1, col:col + 2], stats[:, 0, col:col + 2], -scale[kind], None, ALU.mult)
                    ins.then_inc(shift_ready, 1)

                def normalise(j):
                    kind, which, part_, t = items[j]
                    nkeys = TOK if part_ == "lat" else CTX
                    col = 2 * (item_base[layer] + j)
                    s = stats[:, 2, col:col + 2]
                    dve.wait_ge(exp_done, item_base[layer] + j + 1)
                    if kind == "win":
                        step(dve.tensor_tensor(s, s, stats[:, 3, col:col + 2], ALU.add))
                    step(dve.reciprocal(s, s))
                    pr = [probs[j % 3][:, lane, 0:nkeys] for lane in range(2)]
                    if kind == "diff":
                        step(dve.tensor_scalar(pr[1], pr[1], s[:, 1:2], small[:, layer, NEG_LAM:NEG_LAM + 1], ALU.mult, ALU.mult))
                        ins = dve.scalar_tensor_tensor(pr[0], pr[0], s[:, 0:1], pr[1], ALU.mult, ALU.add)
                    else:
                        for lane in range(2):
                            ins = dve.tensor_scalar(pr[lane], pr[lane], s[:, lane:lane + 1], None, ALU.mult)
                    ins.then_inc(probs_ready, 1)

                def outputs(j):
                    kind, which, part_, t = items[j]
                    c0 = (CTX if part_ == "lat" else 0) + t * P
                    wait_group(dve, layer, ("PV", j))
                    if kind == "diff":
                        rows = slice(64 * (which % 2), 64 * (which % 2) + 64)
                        dst = dq[rows, which // 2, c0:c0 + P]
                    else:
                        rows = slice(0, P)
                        dst = {"na": nq, "win": wq, "mla": mq}[kind][:, which, c0:c0 + P]
                    dve.tensor_copy(dst, bank(layer, ("PV", j))[rows, 0:P]).then_inc(by_dve, 1)

                for j in range(len(items) + 3):
                    if j < len(items):
                        shift(j)
                    if 1 <= j <= len(items):
                        normalise(j - 1)
                        if layer == 0:
                            cut_after(ADA_UNITS[ADA_BATCHES[0][2] + j - 1])
                            if j == ADA_BATCHES[1][2]:
                                copy_ada_rows(1)
                            if j == len(items):
                                copy_ada_rows(2)
                    if j >= 3:
                        outputs(j - 3)

                if layer == 0:
                    modulations(1)
                    modulations(2)
                    gains(0, 1)
                    gains(1, 0)
                    step(gains(1, 1))

                variance(layer, "ds", [(0, 4 * nq_tiles)], [1.0 / 64])
                dve.wait_ge(rstd_ready, RSTD_AT[layer, "ds"])
                for pair in range(2):
                    if pair:
                        wait_group(dve, layer, "db0")
                    r = rstd[:, 2 * pair * nq_tiles:2 * (pair + 1) * nq_tiles].rearrange("p (t a) -> p t a", a=2)
                    for a in range(2):
                        diagonal(f"ds{pair}", layer, nq_tiles, r[:, :, a], a * nq_tiles, inc=(a == 1))
                for pair in range(2):
                    wait_group(dve, layer, f"db{pair}")
                    o = dq[:, pair, t0:]
                    dve.scalar_tensor_tensor(o, o, small[:, layer, SUBLN:SUBLN + 1], bank(layer, f"db{pair}")[:, 0:nt],
                                             ALU.mult, ALU.mult).then_inc(by_dve, 1)

                for m in range(KD):
                    cut_after(U["g", m, 0])
                    cut_after(U["g", m, 1])
                    wait_emptied(dve, layer, ("g", m, 3))
                    for i in range(4):
                        wait_group(dve, layer, ("b", m, i))
                        s = scratch[:, i, 0:nt]
                        dve.scalar_tensor_tensor(s, s, 1.0, bank(layer, ("b", m, i))[:, 0:nt], ALU.add,
                                                 ALU.mult).then_inc(by_dve, 1)
                    dve.wait_ge(y_hi_ready, KD * layer + m + 1)
                    dve.scalar_tensor_tensor(y_lo[:, m, t0:], scratch[:, 0, 0:nt], 0.5, y_hi[:, m, t0:].bitcast(F32),
                                             ALU.mult, ALU.subtract).then_inc(y_lo_ready, 1)
                    cut_after(U["b", m])
                for m in range(KD):
                    cut_after(U["o", m // 2], m % 2)
                    residual(layer, ("o", m), 2, m)
                    if m:
                        add_square(layer, "n2", m - 1)
                add_square(layer, "n2", KD - 1)

                rstd_of_tokens(layer, "n2")
                modulated(layer, "n2")

                def hidden_lo(q, m):
                    f = (layer * QUARTERS + q) * HID + m
                    dve.wait_ge(hid_hi_ready, f + 1)
                    dve.tensor_tensor(hid_lo[q % 2][:, m, t0:], scratch[:, f % 4, 0:nt],
                                      hid_hi[q % 2][:, m, t0:].bitcast(F32), ALU.subtract).then_inc(hid_lo_ready, 1)

                for kind, q in FF_ORDER:
                    for i in range(4):
                        for m in (2 * i, 2 * i + 1):
                            cut_after(U[kind, q, i], m % 2)
                            if kind == "f1":
                                hidden_lo(q, m)
                            else:
                                residual(layer, (kind, q, m), 5, m)
                                if q == QUARTERS - 1 and m:
                                    add_square(layer + 1, "n1", m - 1)
                add_square(layer + 1, "n1", KD - 1)

            rstd_of_tokens(DEPTH, "n1")
            wait_group(dve, DEPTH, "n1b")
            for k in range(KD):
                dve.scalar_tensor_tensor(out_sb[:, k, :], x[:, k, CTX:TOK], par[:, DEPTH * PAR_LAYER + k:DEPTH * PAR_LAYER + k + 1],
                                         bank(DEPTH, "n1b")[:, 0:LAT], ALU.mult, ALU.mult).then_inc(out_ready, 1)

        @block.gpsimd
        def _(pool):
            steps = [0]

            def step(ins):
                steps[0] += 1
                ins.then_inc(gpsimd_step, 1)
                pool.wait_ge(gpsimd_step, steps[0])

            def power(layer, name, cols):
                wait_emptied(pool, layer, name)
                if RSTD_AT[layer, name] > 1:
                    key = {v: k for k, v in RSTD_AT.items()}[RSTD_AT[layer, name] - 1]
                    last = "ds1" if key[1] == "ds" else key[1]
                    pool.wait_ge(diag_ready, DIAG_AT[key[0], last])
                pool.tensor_tensor(rstd[:, 0:cols], var[:, 0:cols], neg_half[:, 0:cols], ALU.pow).then_inc(rstd_ready, 1)

            pool.memset(silu_parts[:].bitcast(F32), 0.0).then_inc(silu_zero, 1)
            step(pool.memset(pair_q[:], 0.0))
            step(pool.memset(diff_q[:], 0.0))
            step(pool.memset(neg_half[:], -0.5))
            pool.wait_ge(small_landed, 32)
            for layer in range(DEPTH):
                t0, nt = tokens_of(layer)
                nq_tiles = nt // P
                items = items_of(layer)

                def ready_bias(pair):
                    pool.wait_ge(bias_landed, 128 * (layer * PAIRS + pair + 1))
                    b = bias[:].rearrange("p i t k -> p i (t k)")
                    near = cc("near").unsqueeze(1).to_broadcast([P, 2, 2 * LAT])
                    pool.tensor_tensor(b, b, near, ALU.add).then_inc(bias_ready, 1)
                    pool.wait_ge(bias_ready, layer * PAIRS + pair + 1)

                def fill_query(j):
                    if j >= len(items) or items[j][0] == "mla":
                        return
                    kind, which, part_, t = items[j]
                    cols = slice((CTX if part_ == "lat" else 0) + t * P, (CTX if part_ == "lat" else 0) + (t + 1) * P)
                    if item_base[layer] + j >= 2:
                        pool.wait_ge(scores_ready, item_base[layer] + j - 1)
                    for lane in range(2):
                        if kind == "diff":
                            r0 = 64 * (which % 2) + 32 * lane
                            rows = slice(r0, r0 + 32)
                            ins = pool.tensor_copy(diff_q[rows, 2 * (which % 2) + lane, :], dq[rows, which // 2, cols])
                        else:
                            rows = slice(64 * lane, 64 * lane + 64)
                            ins = pool.tensor_copy(pair_q[rows, j % 2, lane, :], (nq if kind == "na" else wq)[rows, which, cols])
                        if lane == 0:
                            step(ins)
                    ins.then_inc(query_ready, 1)
                    pool.wait_ge(query_ready, query_count(layer, j))

                def cut_low(u):
                    for n in cuts_after(u):
                        if LOW_BY[n] == "pool":
                            pool.wait_ge(w_hi_done, n + 1)
                            pool.tensor_tensor(slice_view(w_lo, n), slice_source(n), slice_view(w_hi, n).bitcast(F32),
                                               ALU.subtract).then_inc(w_lo_by_pool, 1)
                            pool.wait_ge(w_lo_by_pool, low_count(n))

                power(layer, "n1", TOK // P)
                ready_bias(0)
                power(layer, "cs", nq_tiles + 4)

                def finish_rope(name, tile):
                    r = len(ROPES) * layer + ROPES.index(name)
                    dim = 64 if name.startswith("rw") else 32
                    rows = slice(64, 96) if name[1] in "ku" else slice(0, P)
                    wait_emptied(pool, layer, name)
                    part = tile[rows, CTX:TOK]
                    step(pool.tensor_tensor(part, part, cc(f"cos{dim}")[rows], ALU.mult))
                    pool.tensor_tensor(part, part, scratch[rows, r % 4, 0:LAT], ALU.add).then_inc(rope_done, 1)
                    pool.wait_ge(rope_done, r + 1)

                tiles = [wq[:, 0], wq[:, 1], wk[:, 0], mk[:, 0], dq[:, 0], dq[:, 1], dk[:, 0], dk[:, 1]]
                tiles += [mq[:, hd] for hd in range(HEADS)]
                for n, name in enumerate(ROPES):
                    finish_rope(name, tiles[n])
                    if name == "rkr":
                        for hd in range(1, HEADS):
                            pool.tensor_copy(mk[64:96, hd, :], mk[64:96, 0, :]).then_inc(kr_copied, 1)
                            pool.wait_ge(kr_copied, 3 * layer + hd)
                if layer == 0:
                    cut_low(UNIT_AT[0, "dv"])
                    cut_low(UNIT_AT[0, "uq"])
                    cut_low(UNIT_AT[0, "ukv"])
                fill_query(0)
                fill_query(1)
                for j in range(len(items)):
                    fill_query(j + 2)
                    if layer == 0:
                        cut_low(ADA_UNITS[ADA_BATCHES[0][2] + j])
                    if j == 4:
                        ready_bias(1)
                power(layer, "ds", 4 * nq_tiles)
                for n, k in enumerate((6, 7, 4, 5, 0, 1, 2, 3)):
                    pool.wait_ge(o_hi_ready, KD * layer + n + 1)
                    pool.tensor_tensor(o_lo[:, k, t0:], BRANCH_TILES[k][:, t0:], o_hi[:, k, t0:].bitcast(F32),
                                       ALU.subtract).then_inc(o_lo_ready, 1)
                for m in range(KD):
                    wait_emptied(pool, layer, ("b", m, 3))
                    s = [scratch[:, i, 0:nt] for i in range(4)]
                    pool.tensor_tensor(s[0], s[0], s[1], ALU.add)
                    step(pool.tensor_tensor(s[2], s[2], s[3], ALU.add))
                    pool.tensor_tensor(s[0], s[0], s[2], ALU.add).then_inc(y_sum_ready, 1)
                power(layer, "n2", nq_tiles)
                for q in range(QUARTERS):
                    for m in range(HID):
                        f = (layer * QUARTERS + q) * HID + m
                        wait_emptied(pool, layer, ("f1", q, m))
                        s = scratch[:, f % 4, 0:nt]
                        pool.tensor_tensor(s, s, s, ALU.mult).then_inc(relu2_ready, 1)
            power(DEPTH, "n1", LAT // P)


def kernel(**inputs):
    import concourse.bacc as bacc
    from concourse.bass_utils import run_bass_kernel_spmd

    a = {k: np.ascontiguousarray(v) for k, v in inputs.items()}

    def columns(v):
        return v.reshape(-1, P).T

    def rows(v):
        return np.broadcast_to(v.reshape(1, -1), (P, v.size))

    par = []
    for layer in range(DEPTH):
        par += [columns(a["norm_mix"][layer]), columns(a["norm_ffn"][layer]), columns(a["b_ada"][layer]),
                columns(a["mla_q_norm"][layer]), columns(a["mla_kv_norm"][layer]),
                np.concatenate([a["diff_subln"][layer]] * 2).reshape(P, 1), columns(a["b_gate"][layer]),
                rows(a["diff_lambda"][layer]), rows(a["win_sink"][layer])]
    par.append(columns(a["final_norm"]))
    feeds = {
        "xT": np.concatenate([a["ctx"][0], a["x"][0]]).T.reshape(KD, P, TOK).transpose(1, 0, 2),
        "c2": np.stack([columns(a["c_ctx"]), columns(a["c"][0])], axis=2),
        "con_in": constants(),
        "par_in": np.concatenate(par, axis=1),
        "rpb": np.tile(np.pad(a["na_rpb"], ((0, 0), (0, 0), (0, 0), (48, 48))), (1, 1, 1, GRID_W)),
        **{n: a[n] for n in ("w_ada", "w_in", "w_uq", "w_ukv", "w_gate", "w_branch", "w_out", "w_ff1", "w_ff2")},
    }
    nc = bacc.Bacc("TRN2", target_bir_lowering=False, num_devices=1)
    arrays, args = {}, []
    for name, v in feeds.items():
        v = np.ascontiguousarray(v)
        arrays[f"{name}_dram"] = v
        args.append(nc.dram_tensor(f"{name}_dram", v.shape, mybir.dt.from_np(v.dtype), kind="ExternalInput").ap())
    args.append(nc.dram_tensor("out_dram", (D, LAT), F32, kind="ExternalOutput").ap())
    block_program(nc, *args)
    r = run_bass_kernel_spmd(nc, [arrays], core_ids=[0])
    return np.ascontiguousarray(r.results[0]["out_dram"].T).reshape(1, LAT, D)
```

```python
from contextlib import ExitStack

import numpy as np

import concourse.bass as bass
from concourse import mybir

F32 = mybir.dt.float32
F32R = mybir.dt.float32r
ALU = mybir.AluOpType
ACT = mybir.ActivationFunctionType
AX_X = mybir.AxisListType.X

P = 128
D = 1024
KD = D // P
CTX = 256
LAT = 256
TOK = CTX + LAT
DEPTH = 2
FFN = 4 * D
EPS = 1e-6
MASKED = -1e30
HEADS = 4
NA_SCALE = WIN_SCALE = 64 ** -0.5
DIFF_SCALE = 32 ** -0.5
MLA_SCALE = 96 ** -0.5
GRID_W = 64
RPB_PAD = 127
RPB_ROW = GRID_W * RPB_PAD
LAMBDA_INIT = [0.8 - 0.6 * float(np.exp(-0.3 * layer)) for layer in range(DEPTH)]

C_CQ, C_CKV, C_DQ, C_DK, C_DV = 0, 256, 416, 672, 928
C_WQ, C_WKV, C_NQ, C_NK, C_NV = 1184, 1440, 1696, 1952, 2208
V_MLA, V_DIFF, V_NA, V_WIN, V_WIDTH = 0, 256, 512, 768, 896

_PAR = [("norm_mix", KD), ("norm_ffn", KD), ("b_ada", 48), ("q_norm", 2), ("kv_norm", 1),
        ("subln", 1), ("b_gate", 32), ("lam", 128), ("sink", HEADS)]
PAR_LAYER = sum(w for _, w in _PAR)
PAR_WIDTH = DEPTH * PAR_LAYER + KD


def par_at(layer, name):
    off = layer * PAR_LAYER
    for n, w in _PAR:
        if n == name:
            return off, off + w
        off += w
    raise KeyError(name)


_CON = [("ident", P), ("ones", P), ("head_ones", 2), ("rot64", P), ("rot32", P),
        ("cos64", LAT), ("sin64", LAT), ("cos32", LAT), ("sin32", LAT),
        ("band", 2 * LAT), ("near", 2 * LAT)]
CON_WIDTH = sum(w for _, w in _CON)


def con_at(name):
    off = 0
    for n, w in _CON:
        if n == name:
            return off, off + w
        off += w
    raise KeyError(name)


def constants():
    c = {"ident": np.eye(P), "ones": np.ones((P, P)), "head_ones": np.kron(np.eye(2), np.ones((64, 1)))}
    for dim in (64, 32):
        q = dim // 4
        rot = np.zeros((P, P))
        for i in range(P):
            block, j = i - i % dim, i % dim
            part = j // q
            rot[i, block + j + (q if part % 2 == 0 else -q)] = -1.0 if part % 2 == 0 else 1.0
        c[f"rot{dim}"] = rot.T
        inv = np.float32(10000.0) ** (-np.arange(q, dtype=np.float32) / np.float32(q))
        t = np.arange(LAT)
        row = (t // GRID_W).astype(np.float32)[:, None] * inv
        col = (t % GRID_W).astype(np.float32)[:, None] * inv
        ang = np.concatenate([row, row, col, col], axis=1).astype(np.float64).T
        c[f"cos{dim}"] = np.tile(np.cos(ang), (P // dim, 1))
        c[f"sin{dim}"] = np.tile(np.sin(ang), (P // dim, 1))
    k = np.arange(LAT)
    band, near = np.zeros((P, 2, LAT)), np.zeros((P, 2, LAT))
    for t in range(2):
        q = t * P + np.arange(P)[:, None]
        band[:, t] = np.where(np.abs(q - k) <= 128, 0.0, 8 * MASKED)
        start = np.clip(q % GRID_W - 8, 0, GRID_W - 16)
        inside = (k % GRID_W >= start) & (k % GRID_W < start + 16)
        near[:, t] = np.where(inside, 0.0, MASKED)
    c["band"], c["near"] = band.reshape(P, -1), near.reshape(P, -1)
    return np.concatenate([c[n] for n, _ in _CON], axis=1).astype(np.float32)


SLOTS = 4
RING = 5
ATTN_RING = 3
QUARTERS = 4
HID = FFN // QUARTERS // P
PAIRS = HEADS // 2
ADA_BATCHES = [(0, 0, 8), (0, 8, 16), (1, 0, 24)]
ADA_ROWS = 4 * max(n for _, _, n in ADA_BATCHES)


BIAS_PARTS = [2, 4]


def items_of(layer):
    parts = ("lat", "ctx") if layer < DEPTH - 1 else ("lat",)

    def pairs(kind, which, part):
        return [(kind, p, part, t) for p in which for t in range(2)]

    out = pairs("na", [0], "lat")
    if len(parts) > 1:
        out += pairs("na", [0, 1], "ctx")
    for part in parts:
        out += pairs("win", [0, 1], part)
    out += pairs("na", [1], "lat")
    for part in parts:
        out += [("diff", h, part, t) for p in range(PAIRS) for t in range(2) for h in (2 * p, 2 * p + 1)]
    for p in range(PAIRS):
        for part in parts:
            out += pairs("mla", [p], part)
    return out


FF_ORDER = [("f1", 0), ("f1", 1), ("f2", 0), ("f1", 2), ("f2", 1), ("f1", 3), ("f2", 2), ("f2", 3)]


def ada_blocks(batch):
    layer, first, n = ADA_BATCHES[batch]
    return [(batch, layer, first + i, i) for i in range(n)]


def units_of(layer):
    out = [("a", *b) for b in ada_blocks(0)] if layer == 0 else []
    out += ["cq", "ckv", "nq", "nk", "nv", "wq", "wkv", "dq", "dk", "dv", "uq", "ukv"]
    if layer == 0:
        out += [("a", *b) for n in (1, 2) for b in ada_blocks(n)]
    for m in range(KD):
        out += [("g", m, 0), ("g", m, 1), ("b", m)]
    out += [("o", i) for i in range(4)]
    for kind, q in FF_ORDER:
        out += [(kind, q, i) for i in range(4)]
    return out


def groups_of(layer):
    a, v = "act", "dve"
    out = [("n1", v)] + ([(("at", 0), v)] if layer == 0 else []) + [("n1b", v)]
    out += [("cq0", a), ("cq1", a), ("ckv", a), ("kr", a), ("nq0", a), ("nq1", a)]
    out += [("cs", v), ("nk0", a), ("nk1", a), ("cb0", v), ("cb1", v)]
    out += [(f"nv{t}", v) for t in range(4)] + [("wq0", a), ("wq1", a)]
    out += [(f"wkv{t}", v) for t in range(4)] + [("dq0", a), ("wk", a), ("dq1", a)]
    out += [(n, v) for n in ("rwq0", "rwq1", "rwk", "rkr")] + [("dk0", a), ("dk1", a)]
    out += [(f"dv{t}", v) for t in range(4)]
    out += [(n, v) for n in ("rdq0", "rdq1", "rdk0", "rdk1")]
    out += [(f"uq{h}", a) for h in range(HEADS)] + [(f"uk{h}", a) for h in range(HEADS)]
    out += [(f"uv{t}", v) for t in range(4)] + [(f"ruq{h}", v) for h in range(HEADS)]
    items = items_of(layer)
    for j in range(len(items) + 1):
        if j < len(items):
            out += [(("T", j, lane), a) for lane in range(1 if items[j][0] == "diff" else 2)]
        if j:
            out.append((("PV", j - 1), v))
    between = [[("ds", v)], [("db0", v)], [("db1", v)], []]
    if layer == 0:
        between[1].append((("at", 1), v))
        between[2].append((("at", 2), v))
    for m in range(KD):
        for i in range(4):
            out += [(("g", m, i), a)] + (between[i] if m == 0 else [])
        out += [(("b", m, i), v) for i in range(4)]
    out += [(("o", m), v) for m in range(KD)] + [("n2", v), ("n2b", v)]
    for kind, q in FF_ORDER:
        out += [((kind, q, m), a if kind == "f1" else v) for m in range(KD)]
    return out


UNITS = [(layer, u) for layer in range(DEPTH) for u in units_of(layer)]
UNIT_AT = {key: i for i, key in enumerate(UNITS)}
GROUPS = [((layer, n), e) for layer in range(DEPTH) for n, e in groups_of(layer)] + [
    ((DEPTH, "n1"), "dve"), ((DEPTH, "n1b"), "dve")]
GROUP_AT = {key: i for i, (key, _) in enumerate(GROUPS)}
ROPES = ["rwq0", "rwq1", "rwk", "rkr", "rdq0", "rdq1", "rdk0", "rdk1", "ruq0", "ruq1", "ruq2", "ruq3"]


def emptied(g):
    engine = GROUPS[g][1]
    return engine, sum(e == engine for _, e in GROUPS[:g + 1])


EMPTIED = [emptied(g) for g in range(len(GROUPS))]


def bank_of(g):
    inside = [isinstance(n, tuple) and n[0] in ("T", "PV") for (_, n), _ in GROUPS[:g + 1]]
    banks = [i % ATTN_RING if x else i % RING for i, x in enumerate(inside)]
    before = [i for i in range(g) if banks[i] == banks[g]]
    return banks[g], before[-1] if before else None


BANK_OF = [bank_of(g) for g in range(len(GROUPS))]


def slices_of(kind):
    if kind == "uq":
        return [(0, 384)], (2, 384)
    if kind == "ukv":
        return [(0, 512)], (1, 512)
    if kind == "ckv":
        return [(0, 128), (64, 96)], (KD, 160)
    if kind[0] == "b":
        return [(0, 128)], (KD, 128)
    return [(0, 128), (128, 128)], (KD, 256)


SLICES = [(u, i) for u, (_, kind) in enumerate(UNITS) for i in range(len(slices_of(kind)[0]))]
SLICE_AT = {key: n for n, key in enumerate(SLICES)}
LOW_BY = ["pool" if UNITS[u][1][0] == "a" and u >= UNIT_AT[0, "ukv"] + 3 and i == 1 else "dve" for u, i in SLICES]


def low_count(n):
    return sum(e == LOW_BY[n] for e in LOW_BY[:n + 1])


def last_group(n):
    u, i = SLICES[n]
    layer, kind = UNITS[u]
    if isinstance(kind, str):
        both = {"cq": ("cq0", "cq1"), "ckv": ("ckv", "kr"), "nq": ("nq0", "nq1"), "nk": ("nk0", "nk1"),
                "nv": ("nv3", "nv3"), "wq": ("wq0", "wq1"), "wkv": ("wkv3", "wkv3"), "dq": ("dq0", "dq1"),
                "dk": ("dk0", "dk1"), "dv": ("dv3", "dv3"), "uq": ("uq3",), "ukv": ("uv3",)}
        return GROUP_AT[layer, both[kind][i]]
    if kind[0] == "a":
        return None
    if kind[0] == "g":
        return GROUP_AT[layer, ("g", kind[1], 2 * kind[2] + i)]
    if kind[0] == "b":
        return GROUP_AT[layer, ("b", kind[1], 3)]
    if kind[0] == "o":
        return GROUP_AT[layer, ("o", 2 * kind[1] + i)]
    return GROUP_AT[layer, (kind[0], kind[1], 2 * kind[2] + i)]


FIRST_SQUARES = {4: (0, 1), 5: (2, 3, 4), 6: (5, 6, 7)}
ADA_UNITS = [u for u, (_, kind) in enumerate(UNITS) if kind[0] == "a"]


def tokens_of(layer):
    first = 0 if layer < DEPTH - 1 else CTX
    return first, TOK - first


def block_program(nc, xT, c2, con_in, par_in, rpb, w_ada, w_in, w_uq, w_ukv, w_gate, w_branch, w_out,
                  w_ff1, w_ff2, out):
    base = -(-nc.sbuf_base // 64) * 64
    at = [base]

    def place(size):
        here = at[0]
        at[0] += -(-size // 64) * 64
        return here

    def sb(name, shape, dtype=F32, offset=None):
        size = 4 * int(np.prod(shape[1:]))
        return nc.alloc_sbuf_tensor_at(name, shape, dtype, offset=place(size) if offset is None else offset)

    x = sb("x", [P, KD, TOK])
    h_hi = sb("h_hi", [P, KD, TOK], F32R)
    h_lo = sb("h_lo", [P, KD, TOK], F32R)
    con = sb("con", [P, CON_WIDTH])
    par = sb("par", [P, PAR_WIDTH])
    raw = sb("raw", [P, SLOTS, 1024])
    w_hi = sb("w_hi", [P, SLOTS, 1024], F32R)
    w_lo = sb("w_lo", [P, SLOTS, 1024], F32R)
    scratch = sb("scratch", [P, 4, TOK])
    square_sum = sb("square_sum", [P, TOK])
    diag_at = place(4 * 8 * P)
    diag = sb("diag", [P, 8, P], offset=diag_at)
    bias = sb("bias", [P, 2, 2, LAT])
    pair_q = sb("pair_q", [P, 2, 2, P])
    diff_q = sb("diff_q", [P, 4, P])
    silu_parts = sb("silu_parts", [P, KD, 2 * ADA_ROWS - 4], F32R)
    ada_rows = sb("ada_rows", [P, 2, 256])
    cvec = sb("cvec", [P, KD, 2])
    silu = sb("silu", [P, KD, 2])
    mods = sb("mods", [P, DEPTH, 48, 2])
    gain = sb("gain", [P, DEPTH, 2, KD, 2])
    half_gate_bias = sb("half_gate_bias", [P, DEPTH, 32])
    small = sb("small", [P, DEPTH, 16])
    lam_prod = sb("lam_prod", [P, 2, 32])
    var = sb("var", [P, 16])
    rstd = sb("rstd", [P, 16])
    neg_half = sb("neg_half", [P, 16])
    stats = sb("stats", [P, 4, 128])
    kv_at = place(20480 + 4 * 4 * V_WIDTH)
    dk = sb("dk", [P, 2, TOK], offset=kv_at)
    nk = sb("nk", [P, 2, TOK], offset=kv_at + 4096)
    wk = sb("wk", [P, 2, TOK], offset=kv_at + 8192)
    mk = sb("mk", [P, HEADS, TOK], offset=kv_at + 12288)
    v_sb = sb("v_sb", [P, 4, V_WIDTH], offset=kv_at + 20480)
    qp_at = place(32768)
    dq = sb("dq", [P, 2, TOK], offset=qp_at)
    nq = sb("nq", [P, 2, TOK], offset=qp_at + 4096)
    wq = sb("wq", [P, 2, TOK], offset=qp_at + 8192)
    mq = sb("mq", [P, HEADS, TOK], offset=qp_at + 12288)
    probs = [sb(f"probs{i}", [P, 2, TOK], offset=o) for i, o in enumerate((qp_at + 20480, qp_at + 24576, diag_at))]
    probs_t = [sb("probs_t", [P, 4, 2 * P], offset=qp_at + 28672), scratch[:, 2:4, :].rearrange("p a (k q) -> p (a k) q", q=2 * P)]
    cn_hi = sb("cn_hi", [P, 3, TOK], F32R, offset=qp_at + 20480)
    cn_lo = sb("cn_lo", [P, 3, TOK], F32R, offset=qp_at + 20480 + 6144)
    o_hi = sb("o_hi", [P, KD, TOK], F32R, offset=kv_at)
    o_lo = sb("o_lo", [P, KD, TOK], F32R, offset=kv_at + 16384)
    y_hi = sb("y_hi", [P, KD, TOK], F32R, offset=qp_at)
    y_lo = sb("y_lo", [P, KD, TOK], F32R, offset=qp_at + 16384)
    hid_hi = [sb("hid_hi0", [P, HID, TOK], F32R, offset=kv_at), sb("hid_hi1", [P, HID, TOK], F32R, offset=qp_at)]
    hid_lo = [sb("hid_lo0", [P, HID, TOK], F32R, offset=kv_at + 16384),
              sb("hid_lo1", [P, HID, TOK], F32R, offset=qp_at + 16384)]
    out_sb = sb("out_sb", [P, KD, LAT], offset=qp_at)
    latent = mq

    def cc(name, lo=0, hi=None):
        a, b = con_at(name)
        return con[:, a + lo:(b if hi is None else a + hi)]

    def pp(layer, name, i=None):
        a, b = par_at(layer, name)
        return par[:, a:b] if i is None else par[:, a + i:a + i + 1]

    NEG_LAM, SUBLN, LAM_SUM, LAM_EXP, NEG_SINK = 0, 1, 2, 4, 8

    def head_out(kind, h):
        return {"na": nq, "win": wq, "diff": dq, "mla": mq}[kind][:, h // 2, :]

    BRANCH_TILES = [head_out("mla", 0), head_out("mla", 2), head_out("diff", 0), head_out("diff", 2),
                    head_out("win", 0), head_out("win", 2), head_out("na", 0), head_out("na", 2)]

    with ExitStack() as ctx:
        ps = ctx.enter_context(nc.psum_tensor("ps", [P, RING + 2, 512], F32))
        ada_ps = ctx.enter_context(nc.psum_tensor("ada_ps", [P, 512], F32))
        scores = [ps[:, RING:RING + 2, :], ps[:, ATTN_RING:ATTN_RING + 2, :]]

        def sem(name):
            return ctx.enter_context(nc.semaphore(name))

        raw_landed = [sem(f"raw_landed{i}") for i in range(SLOTS)]
        bias_landed = sem("bias_landed")
        x_landed = sem("x_landed")
        c_landed = sem("c_landed")
        small_landed = sem("small_landed")
        stored = sem("stored")
        w_hi_done = sem("w_hi_done")
        w_lo_by_dve = sem("w_lo_by_dve")
        w_lo_by_pool = sem("w_lo_by_pool")
        group_done = sem("group_done")
        by_act = sem("by_act")
        by_dve = sem("by_dve")
        ada_done = sem("ada_done")
        ada_rows_ready = sem("ada_rows_ready")
        tanh_ready = sem("tanh_ready")
        silu_ready = sem("silu_ready")
        silu_zero = sem("silu_zero")
        silu_hi = sem("silu_hi")
        squares_ready = sem("squares_ready")
        square_added = sem("square_added")
        latent_square_sum = sem("latent_square_sum")
        rstd_ready = sem("rstd_ready")
        diag_ready = sem("diag_ready")
        h_ready = sem("h_ready")
        h_hi_ready = sem("h_hi_ready")
        h_lo_ready = sem("h_lo_ready")
        latent_hi = sem("latent_hi")
        latent_lo = sem("latent_lo")
        rope_done = sem("rope_done")
        kr_copied = sem("kr_copied")
        wk_copied = sem("wk_copied")
        bias_ready = sem("bias_ready")
        query_ready = sem("query_ready")
        lam_sums = sem("lam_sums")
        lam_exps = sem("lam_exps")
        scores_ready = sem("scores_ready")
        shift_ready = sem("shift_ready")
        exp_done = sem("exp_done")
        probs_ready = sem("probs_ready")
        o_squares = sem("o_squares")
        o_hi_ready = sem("o_hi_ready")
        o_lo_ready = sem("o_lo_ready")
        y_sum_ready = sem("y_sum_ready")
        y_hi_ready = sem("y_hi_ready")
        y_lo_ready = sem("y_lo_ready")
        relu2_ready = sem("relu2_ready")
        hid_hi_ready = sem("hid_hi_ready")
        hid_lo_ready = sem("hid_lo_ready")
        vector_step = sem("vector_step")
        gpsimd_step = sem("gpsimd_step")
        scalar_step = sem("scalar_step")
        out_ready = sem("out_ready")

        def wait_group(eng, layer, name):
            eng.wait_ge(group_done, GROUP_AT[layer, name] + 1)

        def wait_emptied(eng, layer, name):
            engine, n = EMPTIED[GROUP_AT[layer, name]]
            eng.wait_ge(by_act if engine == "act" else by_dve, n)

        def bank(layer, name):
            return ps[:, BANK_OF[GROUP_AT[layer, name]][0], :]

        def slice_view(tensor, n):
            u, i = SLICES[n]
            slices, (k, _) = slices_of(UNITS[u][1])
            w = slices[i][1]
            return tensor[:, n % SLOTS, :k * w].rearrange("p (k c) -> p k c", k=k)

        def wait_low(eng, n):
            eng.wait_ge(w_lo_by_pool if LOW_BY[n] == "pool" else w_lo_by_dve, low_count(n))

        def wait_slot(eng, n):
            if n < SLOTS:
                return
            g = last_group(n - SLOTS)
            if g is None:
                eng.wait_ge(ada_done, ADA_UNITS.index(SLICES[n - SLOTS][0]) + 1)
            else:
                eng.wait_ge(group_done, g + 1)

        def cuts_after(u):
            mine = [SLICE_AT[u, i] + SLOTS for i in range(len(slices_of(UNITS[u][1])[0]))]
            return [n for n in mine if n < len(SLICES)]

        n_items = [len(items_of(layer)) for layer in range(DEPTH)]
        item_base = [sum(n_items[:layer]) for layer in range(DEPTH + 1)]
        norms = [(layer, n) for layer in range(DEPTH) for n in ("n1", "n2")] + [(DEPTH, "n1")]

        def norm_at(layer, n):
            return norms.index((layer, n))

        def norm_tokens(layer, n):
            if layer == DEPTH:
                return CTX, LAT
            return (0, TOK) if n == "n1" else tokens_of(layer)

        RSTD_AT = {(layer, n): 4 * layer + i + 1 for layer in range(DEPTH) for i, n in enumerate(("n1", "cs", "ds", "n2"))}
        RSTD_AT[DEPTH, "n1"] = 4 * DEPTH + 1
        DIAG_AT = {(layer, n): 5 * layer + i + 1 for layer in range(DEPTH) for i, n in enumerate(("n1", "cs", "ds0", "ds1", "n2"))}
        DIAG_AT[DEPTH, "n1"] = 5 * DEPTH + 1

        def parts_of(n):
            return [(0, 0, CTX), (1, CTX, TOK)] if n == TOK else [(1, 0, n)]

        def query_count(layer, j):
            return sum(it[0] != "mla" for prev in range(layer) for it in items_of(prev)) + sum(
                it[0] != "mla" for it in items_of(layer)[:j + 1])

        block = ctx.enter_context(nc.Block())

        def load_bias(eng, layer, pair, which=range(8)):
            for part in which:
                t, half, i = part // 4, part // 2 % 2, part % 2
                r = 2 * t + half
                start = rpb[layer, 2 * pair + i, 7 - r:8 - r, 63:64]
                src = bass.AP(tensor=start.tensor, offset=start.offset,
                              ap=[[RPB_PAD - 1, 64], [RPB_ROW, 4], [1, 64]])
                dst = bias[64 * half:64 * half + 64, i, t, :].rearrange("p (w c) -> p w c", w=4)
                eng.dma_start(dst, src).then_inc(bias_landed, 16)

        @block.sync
        def _(sp):
            def source(n):
                u, i = SLICES[n]
                layer, kind = UNITS[u]
                first, width = slices_of(kind)[0][i]
                if kind == "uq":
                    return w_uq[layer], 0, 2 * P, first, width
                if kind == "ukv":
                    return w_ukv[layer], 0, P, first, width
                if isinstance(kind, str):
                    c0 = {"cq": C_CQ, "ckv": C_CKV, "nq": C_NQ, "nk": C_NK, "nv": C_NV, "wq": C_WQ,
                          "wkv": C_WKV, "dq": C_DQ, "dk": C_DK, "dv": C_DV}[kind]
                    return w_in[layer], 0, D, c0 + first, width
                if kind[0] == "a":
                    return w_ada[kind[2]], 0, D, kind[3] * 256 + first, width
                if kind[0] == "g":
                    return w_gate[layer], 0, D, (2 * kind[2] + i) * D + kind[1] * P, width
                if kind[0] == "b":
                    return w_branch[layer], 0, D, kind[1] * P, width
                if kind[0] == "o":
                    return w_out[layer], 0, D, kind[1] * 256 + first, width
                if kind[0] == "f1":
                    return w_ff1[layer], 0, D, kind[1] * HID * P + kind[2] * 256 + first, width
                return w_ff2[layer], kind[1] * HID * P, HID * P, kind[2] * 256 + first, width

            def load(n):
                w, r0, rows, c0, width = source(n)
                if n >= SLOTS:
                    wait_low(sp, n - SLOTS)
                sp.dma_start(slice_view(raw, n), w[r0:r0 + rows, c0:c0 + width].rearrange("(k p) c -> p k c", p=P)
                             ).then_inc(raw_landed[n % SLOTS], 16)

            def load_turns(run, per_turn, turns):
                olds = range(run - SLOTS, run + per_turn * (turns - 1) - SLOTS)
                assert per_turn % SLOTS == 0 and all(LOW_BY[n] == LOW_BY[n + per_turn] for n in olds)
                with sp.Fori(0, turns) as turn:
                    for n in range(run, run + per_turn):
                        w, r0, rows, c0, width = source(n)
                        _, r1, _, c1, _ = source(n + per_turn)
                        if r1 != r0:
                            src = w[bass.ds(turn * (r1 - r0) + r0, rows), c0:c0 + width]
                        else:
                            src = w[r0:r0 + rows, bass.ds(turn * (c1 - c0) + c0, width)]
                        old = n - SLOTS
                        step = low_count(old + per_turn) - low_count(old)
                        sp.wait_ge(w_lo_by_pool if LOW_BY[old] == "pool" else w_lo_by_dve, turn * step + low_count(old))
                        sp.dma_start(slice_view(raw, n), src.rearrange("(k p) c -> p k c", p=P)
                                     ).then_inc(raw_landed[n % SLOTS], 16)

            def load_all(first, last):
                for n in range(first, last):
                    load(n)

            sp.dma_start(cvec[:], c2).then_inc(c_landed, 16)
            load_all(0, SLOTS)
            sp.dma_start(par[:], par_in).then_inc(small_landed, 16)
            sp.dma_start(con[:], con_in).then_inc(small_landed, 16)
            load_all(SLOTS, 2 * SLOTS)
            sp.dma_start(x[:], xT).then_inc(x_landed, 16)
            load_all(2 * SLOTS, 4 * SLOTS)
            load_bias(sp, 0, 0)
            n = 4 * SLOTS
            for layer in range(DEPTH):
                runs = []
                if layer == 0:
                    runs.append((SLICE_AT[UNIT_AT[0, ("a", *ada_blocks(2)[0])], 0], SLOTS, ADA_BATCHES[2][2] * 2 // SLOTS))
                runs.append((SLICE_AT[UNIT_AT[layer, ("f1", 1, 0)], 0], 2 * KD, QUARTERS - 1))
                for run, per_turn, turns in runs:
                    load_all(n, run)
                    load_turns(run, per_turn, turns)
                    n = run + per_turn * turns
            load_all(n, len(SLICES))
            for m in range(KD):
                sp.wait_ge(out_ready, m + 1)
                sp.dma_start(out[m * P:(m + 1) * P, :], out_sb[:, m, :]).then_inc(stored, 16)
            sp.wait_ge(stored, 16 * KD)

        @block.tensor
        def _(pe):
            def begin(layer, name):
                here, before = BANK_OF[GROUP_AT[layer, name]]
                if before is not None:
                    engine, n = EMPTIED[before]
                    pe.wait_ge(by_act if engine == "act" else by_dve, n)
                return ps[:, here, :]

            def have_slice(n):
                pe.wait_ge(w_hi_done, n + 1)
                wait_low(pe, n)
                return slice_view(w_hi, n), slice_view(w_lo, n)

            def have_both(u):
                n = SLICE_AT[u, 0]
                assert n % 2 == 0
                have_slice(n)
                have_slice(n + 1)
                return [w[:, n % SLOTS:n % SLOTS + 2, :].rearrange("p s (k c) -> p k s c", k=KD) for w in (w_hi, w_lo)]

            def product3(dst, lhs, rhs, first, last):
                (lh, ll), (rh, rl) = lhs, rhs
                pe.matmul(dst, lh, rh, start=first, stop=False)
                pe.matmul(dst, lh, rl, start=False, stop=False)
                return pe.matmul(dst, ll, rh, start=False, stop=last)

            def weights_by_tokens(layer, name, n, c0, width, acts, first, ready=None):
                dst = begin(layer, name)[:width, 0:TOK - first]
                hi, lo = have_slice(n)
                kt = hi.shape[1]
                for k in range(kt):
                    if ready is not None:
                        pe.wait_ge(ready[0], ready[1] + k + 1)
                    mm = product3(dst, (hi[:, k, c0:c0 + width], lo[:, k, c0:c0 + width]),
                                  (acts[0][:, k, first:TOK], acts[1][:, k, first:TOK]), k == 0, k == kt - 1)
                mm.then_inc(group_done, 1)

            def two_while_arriving(layer, names, u, acts, first, hi_ready, lo_ready, before):
                dst = [begin(layer, name)[:, 0:TOK - first] for name in names]
                parts = [have_slice(SLICE_AT[u, i]) for i in range(2)]
                for k in range(KD):
                    pe.wait_ge(hi_ready, before + k + 1)
                    for i in range(2):
                        for w in parts[i]:
                            pe.matmul(dst[i], w[:, k], acts[0][:, k, first:TOK], start=(k == 0 and w is parts[i][0]), stop=False)
                    pe.wait_ge(lo_ready, before + k + 1)
                    for i in range(2):
                        mm = pe.matmul(dst[i], parts[i][0][:, k], acts[1][:, k, first:TOK], start=False, stop=(k == KD - 1))
                        if k == KD - 1:
                            mm.then_inc(group_done, 1)

            def tokens_by_weights(layer, name, t, cols, kt, acts, k0=0):
                dst = begin(layer, name)
                for k in range(kt):
                    rh, rl = cols(0, k), cols(1, k)
                    width = int(np.prod(rh.shape[1:]))
                    tt = slice(t * P, (t + 1) * P)
                    mm = product3(dst[:, 0:width], (acts[0][:, k0 + k, tt], acts[1][:, k0 + k, tt]), (rh, rl),
                                  k == 0, k == kt - 1)
                mm.then_inc(group_done, 1)

            def sums_of_squares(layer, name):
                t0, n = norm_tokens(layer, name)
                dst = begin(layer, name)
                pe.wait_ge(square_added, (KD - 2) * (norm_at(layer, name) + 1))
                for t in range(n // P):
                    pe.matmul(dst[:, t:t + 1], square_sum[:, t * P:(t + 1) * P], cc("ones", 0, 1),
                              start=(t == 0), stop=False, skip_group_check=True)
                pe.wait_ge(squares_ready, KD * (norm_at(layer, name) + 1))
                for t in range(n // P):
                    mm = pe.matmul(dst[:, t:t + 1], scratch[:, (KD - 1) % 4, t * P:(t + 1) * P], cc("ones", 0, 1),
                                   start=False, stop=(t == n // P - 1), skip_group_check=True)
                mm.then_inc(group_done, 1)

            def spread(layer, name, key, blocks, b0=0):
                pe.wait_ge(diag_ready, DIAG_AT[layer, key])
                dst = begin(layer, name)
                pe.matmul(dst[:, 0:blocks * P], cc("ones"), diag[:, b0:b0 + blocks, :].rearrange("p a b -> p (a b)"),
                          start=True, stop=True).then_inc(group_done, 1)

            def ada_block(u):
                _, batch, _, _, i = UNITS[u][1]
                size = ADA_BATCHES[batch][2]
                hi, lo = have_both(u)
                at_ = ADA_ROWS - 4 - 4 * i
                if batch and i == 0:
                    pe.wait_ge(ada_rows_ready, batch)
                for k in range(KD):
                    for w in (hi, lo):
                        mm = pe.matmul(ada_ps[0:4 * size, 0:256], silu_parts[:, k, at_:at_ + 4 * size], w[:, k],
                                       start=(i == 0 and k == 0 and w is hi),
                                       stop=(i == size - 1 and k == KD - 1 and w is lo), skip_group_check=True)
                mm.then_inc(ada_done, 1)

            def ada_turn(batch):
                rows = 4 * ADA_BATCHES[batch][2]
                pe.wait_ge(ada_rows_ready, batch + 1)
                dst = begin(0, ("at", batch))
                for half in range(2):
                    mm = pe.transpose(dst[:, half * P:half * P + rows], ada_rows[0:rows, batch % 2, half * P:(half + 1) * P],
                                      cc("ident", 0, rows)[0:rows])
                mm.then_inc(group_done, 1)

            def rotate(layer, name, src, rows, dim):
                dst = begin(layer, name)
                pe.matmul(dst[rows, 0:LAT], cc(f"rot{dim}")[rows, rows], src[rows, CTX:TOK],
                          start=True, stop=True).then_inc(group_done, 1)

            pe.wait_ge(silu_ready, 1)
            for u in ADA_UNITS[:ADA_BATCHES[0][2]]:
                ada_block(u)
            pe.wait_ge(small_landed, 32)

            for layer in range(DEPTH):
                t0, nt = tokens_of(layer)
                block_at = {name: UNIT_AT[layer, name] for name in units_of(layer)}
                part = {name: [SLICE_AT[u, i] for i in range(len(slices_of(UNITS[u][1])[0]))] for name, u in block_at.items()}
                h = (h_hi, h_lo)
                full = slice(0, P)

                sums_of_squares(layer, "n1")
                if layer == 0:
                    ada_turn(0)
                spread(layer, "n1b", "n1", TOK // P)
                two_while_arriving(layer, ("cq0", "cq1"), block_at["cq"], h, t0,
                                   h_hi_ready, h_lo_ready, KD * norm_at(layer, "n1"))
                weights_by_tokens(layer, "ckv", part["ckv"][0], 0, P, h, 0)
                weights_by_tokens(layer, "kr", part["ckv"][1], 0, 96, h, 0)
                for i in range(2):
                    weights_by_tokens(layer, f"nq{i}", part["nq"][i], 0, P, h, t0)
                dst = begin(layer, "cs")
                pe.wait_ge(latent_square_sum, layer + 1)
                wait_emptied(pe, layer, "ckv")
                nq_tiles = nt // P
                for t in range(nq_tiles):
                    pe.matmul(dst[:, t:t + 1], scratch[:, 0, t * P:(t + 1) * P], cc("ones", 0, 1),
                              start=True, stop=True, skip_group_check=True)
                for t in range(TOK // P):
                    mm = pe.matmul(dst[:, nq_tiles + t:nq_tiles + t + 1], scratch[:, 2, t * P:(t + 1) * P],
                                   cc("ones", 0, 1), start=True, stop=True, skip_group_check=True)
                mm.then_inc(group_done, 1)
                for i in range(2):
                    weights_by_tokens(layer, f"nk{i}", part["nk"][i], 0, P, h, 0)
                spread(layer, "cb0", "cs", nq_tiles)
                spread(layer, "cb1", "cs", TOK // P, nq_tiles)
                both = have_both(block_at["nv"])
                for t in range(4):
                    tokens_by_weights(layer, f"nv{t}", t, lambda low, k: both[low][:, k], KD, h)
                for i in range(2):
                    weights_by_tokens(layer, f"wq{i}", part["wq"][i], 0, P, h, t0)
                both = have_both(block_at["wkv"])
                for t in range(4):
                    tokens_by_weights(layer, f"wkv{t}", t, lambda low, k: both[low][:, k], KD, h)
                weights_by_tokens(layer, "dq0", part["dq"][0], 0, P, h, t0)
                wait_emptied(pe, layer, "wkv3")
                dst = begin(layer, "wk")
                for t in range(4):
                    mm = pe.transpose(dst[:, t * P:(t + 1) * P], wk[:, 1, t * P:(t + 1) * P], cc("ident"))
                mm.then_inc(group_done, 1)
                weights_by_tokens(layer, "dq1", part["dq"][1], 0, P, h, t0)
                wait_emptied(pe, layer, "wk")
                rotate(layer, "rwq0", wq[:, 0], full, 64)
                rotate(layer, "rwq1", wq[:, 1], full, 64)
                rotate(layer, "rwk", wk[:, 0], full, 64)
                rotate(layer, "rkr", mk[:, 0], slice(64, 96), 32)
                for i in range(2):
                    weights_by_tokens(layer, f"dk{i}", part["dk"][i], 0, P, h, 0)
                both = have_both(block_at["dv"])
                for t in range(4):
                    tokens_by_weights(layer, f"dv{t}", t, lambda low, k: both[low][:, k], KD, h)
                wait_emptied(pe, layer, "dk1")
                for i in range(2):
                    rotate(layer, f"rdq{i}", dq[:, i], full, 32)
                for i in range(2):
                    rotate(layer, f"rdk{i}", dk[:, i], full, 32)
                pe.wait_ge(latent_lo, 3 * layer + 3)
                cn = (cn_hi, cn_lo)
                for hd in range(HEADS):
                    weights_by_tokens(layer, f"uq{hd}", part["uq"][0], hd * 96, 96, cn, t0)
                ckvn = (cn_hi[:, 2:3], cn_lo[:, 2:3])
                for hd in range(HEADS):
                    weights_by_tokens(layer, f"uk{hd}", part["ukv"][0], hd * P, 64, ckvn, 0)
                one = have_slice(part["ukv"][0])
                for t in range(4):
                    tokens_by_weights(layer, f"uv{t}", t, lambda low, k: one[low][:, k].rearrange(
                        "p (h c) -> p h c", h=HEADS)[:, :, 64:128], 1, cn, 2)
                wait_emptied(pe, layer, "uq3")
                for hd in range(HEADS):
                    rotate(layer, f"ruq{hd}", mq[:, hd], slice(64, 96), 32)

                items = items_of(layer)
                kinds = [item[0] for item in items]
                wait_emptied(pe, layer, "nk1")

                def score_item(j):
                    if j == 1:
                        wait_emptied(pe, layer, "uk3")
                        wait_emptied(pe, layer, "ruq3")
                    if j == kinds.index("win"):
                        pe.wait_ge(rope_done, len(ROPES) * layer + ROPES.index("rwk") + 1)
                        pe.wait_ge(wk_copied, layer + 1)
                    if j == kinds.index("diff"):
                        pe.wait_ge(rope_done, len(ROPES) * layer + ROPES.index("rdk1") + 1)
                    if j == kinds.index("mla"):
                        pe.wait_ge(rope_done, len(ROPES) * (layer + 1))
                        pe.wait_ge(kr_copied, 3 * (layer + 1))
                    kind, which, part_, t = items[j]
                    nkeys = TOK if part_ == "lat" else CTX
                    col = (CTX if part_ == "lat" else 0) + t * P
                    if kind != "mla":
                        pe.wait_ge(query_ready, query_count(layer, j))
                    for lane in range(2):
                        if kind == "diff":
                            qa, ka = diff_q[:, 2 * (which % 2) + lane, :], dk[:, which // 2, 0:nkeys]
                        elif kind == "mla":
                            hd = 2 * which + lane
                            qa, ka = mq[0:96, hd, col:col + P], mk[0:96, hd, 0:nkeys]
                        else:
                            qa = pair_q[:, j % 2, lane, :]
                            ka = (nk if kind == "na" else wk)[:, which, 0:nkeys]
                        mm = pe.matmul(scores[j % 2][:, lane, 0:nkeys], qa, ka, start=True, stop=True)
                    mm.then_inc(scores_ready, 1)

                def turn_item(j):
                    kind, which, part_, t = items[j]
                    ntile = (TOK if part_ == "lat" else CTX) // P
                    pe.wait_ge(probs_ready, item_base[layer] + j + 1)
                    for lane in range(1 if kind == "diff" else 2):
                        dst = begin(layer, ("T", j, lane))
                        for kt in range(ntile):
                            mm = pe.transpose(dst[:, kt * P:(kt + 1) * P], probs[j % 3][:, lane, kt * P:(kt + 1) * P],
                                              cc("ident"))
                        mm.then_inc(group_done, 1)

                def value_item(j):
                    kind, which, part_, t = items[j]
                    ntile = (TOK if part_ == "lat" else CTX) // P
                    if kind == "diff":
                        heads = [(which % 2, V_DIFF + 64 * which)]
                    elif kind == "win":
                        heads = [(lane, V_WIN + 64 * which) for lane in range(2)]
                    else:
                        heads = [(lane, (V_NA if kind == "na" else V_MLA) + 64 * (2 * which + lane)) for lane in range(2)]
                    wait_emptied(pe, layer, ("T", j, len(heads) - 1))
                    dst = begin(layer, ("PV", j))
                    for kt in range(ntile):
                        for lane, (half, v0) in enumerate(heads):
                            mm = pe.matmul(dst[64 * half:64 * half + 64, 0:P], v_sb[:, kt, v0:v0 + 64],
                                           probs_t[j % 2][:, kt, lane * P:(lane + 1) * P],
                                           start=(kt == 0), stop=(kt == ntile - 1))
                    mm.then_inc(group_done, 1)

                for j in range(len(items) + 3):
                    if j < len(items):
                        if j >= 2:
                            pe.wait_ge(exp_done, item_base[layer] + j - 1)
                        score_item(j)
                    if 2 <= j < len(items) + 2:
                        turn_item(j - 2)
                    if j < len(items):
                        if layer == 0:
                            ada_block(ADA_UNITS[ADA_BATCHES[0][2] + j])
                    if j >= 3:
                        value_item(j - 3)

                def diff_sums():
                    dst = begin(layer, "ds")
                    for pair in range(2):
                        pe.wait_ge(o_squares, 2 * layer + pair + 1)
                        for t in range(nq_tiles):
                            col = 2 * (pair * nq_tiles + t)
                            mm = pe.matmul(dst[:, col:col + 2], scratch[:, pair, t * P:(t + 1) * P], cc("head_ones"),
                                           start=True, stop=True, skip_group_check=True)
                    mm.then_inc(group_done, 1)

                def diff_spread(pair):
                    pe.wait_ge(diag_ready, DIAG_AT[layer, f"ds{pair}"])
                    dst = begin(layer, f"db{pair}")
                    for a in range(2):
                        mm = pe.matmul(dst[64 * a:64 * a + 64, 0:nt], cc("ones", 0, 64),
                                       diag[:, a * nq_tiles:(a + 1) * nq_tiles, :].rearrange("p a b -> p (a b)"),
                                       start=True, stop=True)
                    mm.then_inc(group_done, 1)

                for m in range(KD):
                    for i in range(4):
                        weights_by_tokens(layer, ("g", m, i), part["g", m, i // 2][i % 2], 0, P, h, t0)
                        if m == 0 and i == 0:
                            diff_sums()
                        elif m == 0 and i < 3:
                            diff_spread(i - 1)
                            if layer == 0:
                                ada_turn(i)
                    hi, lo = have_slice(part["b", m][0])
                    pe.wait_ge(o_lo_ready, KD * (layer + 1))
                    for i in range(4):
                        dst = begin(layer, ("b", m, i))[:, 0:nt]
                        for k in (2 * i, 2 * i + 1):
                            mm = product3(dst, (hi[:, k], lo[:, k]), (o_hi[:, k, t0:], o_lo[:, k, t0:]),
                                          k % 2 == 0, k % 2 == 1)
                        mm.then_inc(group_done, 1)
                two_while_arriving(layer, (("o", 0), ("o", 1)), block_at["o", 0], (y_hi, y_lo), t0,
                                   y_hi_ready, y_lo_ready, KD * layer)
                for m in range(2, KD):
                    weights_by_tokens(layer, ("o", m), part["o", m // 2][m % 2], 0, P, (y_hi, y_lo), t0)

                sums_of_squares(layer, "n2")
                spread(layer, "n2b", "n2", nq_tiles)
                for kind, q in FF_ORDER:
                    for m in range(KD):
                        if (kind, q) == ("f1", 0) and m < 2:
                            if m == 0:
                                two_while_arriving(layer, (("f1", 0, 0), ("f1", 0, 1)), block_at["f1", 0, 0], h, t0,
                                                   h_hi_ready, h_lo_ready, KD * norm_at(layer, "n2"))
                        elif kind == "f1":
                            weights_by_tokens(layer, ("f1", q, m), part["f1", q, m // 2][m % 2], 0, P, h, t0)
                        else:
                            weights_by_tokens(layer, ("f2", q, m), part["f2", q, m // 2][m % 2], 0, P,
                                              (hid_hi[q % 2], hid_lo[q % 2]), t0,
                                              (hid_lo_ready, (layer * QUARTERS + q) * HID) if m == 0 else None)
            sums_of_squares(DEPTH, "n1")
            spread(DEPTH, "n1b", "n1", LAT // P)

        @block.scalar
        def _(act):
            def cut(n):
                u = SLICES[n][0]
                act.wait_ge(raw_landed[n % SLOTS], 16 * (n // SLOTS + 1))
                wait_slot(act, n)
                act.activation(slice_view(w_hi, n), slice_view(raw, n), ACT.Copy).then_inc(w_hi_done, 1)

            def cut_after(u, i=None):
                for n in cuts_after(u) if i is None else cuts_after(u)[i:i + 1]:
                    cut(n)

            def next_bias(layer, pair, which):
                lp, pp_ = (layer, 0) if pair else (layer - 1, 1)
                act.wait_ge(shift_ready, item_base[lp] + items_of(lp).index(("na", pp_, "lat", 1)) + 1)
                load_bias(act, layer, pair, which)

            def copy_out(layer, name, dst, rows=slice(0, P), width=TOK):
                wait_group(act, layer, name)
                act.activation(dst, bank(layer, name)[rows, 0:width], ACT.Copy).then_inc(by_act, 1)

            def square(layer, name, k):
                t0, n = norm_tokens(layer, name)
                if (layer, name) == (0, "n1"):
                    act.wait_ge(x_landed, 16)
                elif name == "n1":
                    wait_emptied(act, layer - 1, ("f2", QUARTERS - 1, k))
                else:
                    wait_emptied(act, layer, ("o", k))
                if k > 4:
                    act.wait_ge(square_added, (KD - 2) * norm_at(layer, name) + k - 4)
                dst = square_sum[:, 0:n] if k == 0 else scratch[:, k % 4, 0:n]
                act.activation(dst, x[:, k, t0:t0 + n], ACT.Square).then_inc(squares_ready, 1)

            def normed_hi(layer, name):
                t0, n = norm_tokens(layer, name)
                which = 0 if name == "n1" else 1
                for k in range(KD):
                    if k == KD - 1:
                        wait_emptied(act, layer, name + "b")
                    else:
                        act.wait_ge(h_ready, (KD - 1) * norm_at(layer, name) + k + 1)
                    for group, a, b in parts_of(n):
                        ins = act.activation(h_hi[:, k, t0 + a:t0 + b], scratch[:, k % 4, a:b], ACT.Identity,
                                             bias=mods[:, layer, 24 * which + k, group:group + 1])
                    ins.then_inc(h_hi_ready, 1)

            act.wait_ge(c_landed, 16)
            act.activation(silu[:], cvec[:], ACT.Tanh, scale=0.5).then_inc(tanh_ready, 1)
            act.wait_ge(silu_ready, 1)
            act.wait_ge(silu_zero, 1)
            act.activation(silu_parts[:, :, ADA_ROWS - 4:ADA_ROWS - 2], silu[:], ACT.Copy).then_inc(silu_hi, 1)
            for n in range(SLOTS):
                cut(n)
            for i, u in enumerate(ADA_UNITS[:ADA_BATCHES[0][2]]):
                for k in FIRST_SQUARES.get(i, ()):
                    square(0, "n1", k)
                cut_after(u)
            for layer in range(DEPTH):
                t0, nt = tokens_of(layer)
                U = {name: UNIT_AT[layer, name] for name in units_of(layer)}
                act.wait_ge(lam_sums, layer + 1)
                act.activation(small[:, layer, LAM_EXP:LAM_EXP + 2], small[:, layer, LAM_SUM:LAM_SUM + 2],
                               ACT.Exp).then_inc(lam_exps, 1)
                normed_hi(layer, "n1")
                for i in range(2):
                    wait_group(act, layer, f"cq{i}")
                    act.activation(latent[:, i, 0:nt], bank(layer, f"cq{i}")[:, 0:nt], ACT.Copy)
                    act.activation(scratch[:, i, 0:nt], bank(layer, f"cq{i}")[:, 0:nt], ACT.Square).then_inc(by_act, 1)
                cut_after(U["cq"])
                wait_group(act, layer, "ckv")
                act.activation(latent[:, 2, :], bank(layer, "ckv"), ACT.Copy)
                act.activation(scratch[:, 2, :], bank(layer, "ckv"), ACT.Square).then_inc(by_act, 1)
                copy_out(layer, "kr", mk[64:96, 0, :], slice(64, 96))
                cut_after(U["ckv"])
                for i in range(2):
                    copy_out(layer, f"nq{i}", nq[:, i, t0:], width=nt)
                cut_after(U["nq"])
                for i in range(2):
                    copy_out(layer, f"nk{i}", nk[:, i, :])
                cut_after(U["nk"])
                for i in range(3):
                    first = t0 if i < 2 else 0
                    gamma = pp(layer, "q_norm", i) if i < 2 else pp(layer, "kv_norm")
                    wait_emptied(act, layer, f"cb{i // 2}")
                    act.activation(cn_hi[:, i, first:], latent[:, i, 0:TOK - first], ACT.Identity,
                                   scale=gamma).then_inc(latent_hi, 1)
                cut_after(U["nv"])
                for i in range(2):
                    copy_out(layer, f"wq{i}", wq[:, i, t0:], width=nt)
                cut_after(U["wq"])
                cut_after(U["wkv"])
                copy_out(layer, "dq0", dq[:, 0, t0:], width=nt)
                copy_out(layer, "wk", wk[:, 0, :])
                copy_out(layer, "dq1", dq[:, 1, t0:], width=nt)
                cut_after(U["dq"])
                for i in range(2):
                    copy_out(layer, f"dk{i}", dk[:, i, :])
                cut_after(U["dk"])
                act.wait_ge(rope_done, len(ROPES) * layer + ROPES.index("rwk") + 1)
                act.activation(wk[0:64, 1, :], wk[64:128, 0, :], ACT.Copy)
                act.activation(wk[64:128, 1, :], wk[64:128, 0, :], ACT.Copy).then_inc(scalar_step, 1)
                act.wait_ge(scalar_step, layer + 1)
                act.activation(wk[64:128, 0, :], wk[0:64, 0, :], ACT.Copy).then_inc(wk_copied, 1)
                cut_after(U["dv"])
                act.wait_ge(latent_lo, 3 * layer + 3)
                for hd in range(HEADS):
                    copy_out(layer, f"uq{hd}", mq[0:96, hd, t0:], slice(0, 96), nt)
                cut_after(U["uq"])
                for hd in range(HEADS):
                    copy_out(layer, f"uk{hd}", mk[0:64, hd, :], slice(0, 64))
                cut_after(U["ukv"])

                items = items_of(layer)
                scale = {"na": NA_SCALE, "win": WIN_SCALE, "diff": DIFF_SCALE, "mla": MLA_SCALE}

                def turned(j):
                    kind, hd, part, t = items[j]
                    ntile = (TOK if part == "lat" else CTX) // P
                    if j == 1:
                        act.wait_ge(rope_done, len(ROPES) * (layer + 1))
                    for lane in range(1 if kind == "diff" else 2):
                        wait_group(act, layer, ("T", j, lane))
                        act.activation(probs_t[j % 2][:, 0:ntile, lane * P:(lane + 1) * P],
                                       bank(layer, ("T", j, lane))[:, 0:ntile * P].rearrange("p (k q) -> p k q", q=P),
                                       ACT.Copy).then_inc(by_act, 1)

                for j in range(len(items) + 2):
                    if 2 <= j < 2 + 8 // BIAS_PARTS[layer]:
                        next_bias(layer, 1, range((j - 2) * BIAS_PARTS[layer], (j - 1) * BIAS_PARTS[layer]))
                    if j >= 2:
                        turned(j - 2)
                    if j < len(items):
                        kind, which, part_, t = items[j]
                        nkeys = TOK if part_ == "lat" else CTX
                        act.wait_ge(shift_ready, item_base[layer] + j + 1)
                        col = 2 * (item_base[layer] + j)
                        if kind == "win":
                            act.activation(stats[:, 3, col:col + 2], stats[:, 3, col:col + 2], ACT.Exp)
                        for lane in range(2):
                            mm = act.activation(probs[j % 3][:, lane, 0:nkeys], scores[j % 2][:, lane, 0:nkeys], ACT.Exp,
                                                bias=stats[:, 1, col + lane:col + lane + 1], scale=scale[kind],
                                                accum_out=stats[:, 2, col + lane:col + lane + 1])
                        mm.then_inc(exp_done, 1)
                        if layer == 0:
                            cut_after(ADA_UNITS[ADA_BATCHES[0][2] + j])
                last_diff = max(j for j, it in enumerate(items) if it[0] == "diff")
                wait_emptied(act, layer, ("PV", last_diff))
                for pair in range(2):
                    act.activation(scratch[:, pair, 0:nt], dq[:, pair, t0:], ACT.Square).then_inc(o_squares, 1)
                wait_emptied(act, layer, ("PV", len(items) - 1))
                for k in (6, 7, 4, 5, 0, 1):
                    act.activation(o_hi[:, k, t0:], BRANCH_TILES[k][:, t0:], ACT.Copy).then_inc(o_hi_ready, 1)
                wait_group(act, layer, "ds")

                for m in range(KD):
                    if m:
                        act.wait_ge(y_lo_ready, KD * layer + m)
                    for i in range(4):
                        wait_group(act, layer, ("g", m, i))
                        act.activation(scratch[:, i, 0:nt], bank(layer, ("g", m, i))[:, 0:nt], ACT.Tanh, scale=0.5,
                                       bias=half_gate_bias[:, layer, i * KD + m:i * KD + m + 1]).then_inc(by_act, 1)
                        cut_after(U["g", m, i // 2], i % 2)
                        if m == 0 and i in (1, 2):
                            k = i + 1
                            wait_emptied(act, layer, f"db{i - 1}")
                            act.activation(o_hi[:, k, t0:], BRANCH_TILES[k][:, t0:], ACT.Copy).then_inc(o_hi_ready, 1)
                    act.wait_ge(y_sum_ready, KD * layer + m + 1)
                    act.activation(y_hi[:, m, t0:], scratch[:, 0, 0:nt], ACT.Copy, scale=0.5).then_inc(y_hi_ready, 1)
                    cut_after(U["b", m])
                    if layer < DEPTH - 1:
                        next_bias(layer + 1, 0, range(m, m + 1))
                for m in range(KD):
                    if m < KD - 1:
                        cut_after(U["o", m // 2], m % 2)
                    if m:
                        square(layer, "n2", m - 1)
                square(layer, "n2", KD - 1)
                cut_after(U["o", (KD - 1) // 2], 1)

                normed_hi(layer, "n2")

                def hidden_hi(q, m):
                    f = (layer * QUARTERS + q) * HID + m
                    act.wait_ge(relu2_ready, f + 1)
                    act.activation(hid_hi[q % 2][:, m, t0:], scratch[:, f % 4, 0:nt], ACT.Copy).then_inc(hid_hi_ready, 1)

                for kind, q in FF_ORDER:
                    for i in range(4):
                        if kind == "f1":
                            for m in (2 * i, 2 * i + 1):
                                f = (layer * QUARTERS + q) * HID + m
                                if f >= 4:
                                    act.wait_ge(hid_lo_ready, f - 3)
                                wait_group(act, layer, ("f1", q, m))
                                act.activation(scratch[:, f % 4, 0:nt], bank(layer, ("f1", q, m))[:, 0:nt],
                                               ACT.Relu).then_inc(by_act, 1)
                                if m:
                                    hidden_hi(q, m - 1)
                            if i == 3:
                                hidden_hi(q, HID - 1)
                        if (kind, q) != ("f2", QUARTERS - 1):
                            cut_after(U[kind, q, i])
                for m in range(KD):
                    if m < KD - 1:
                        cut_after(U["f2", QUARTERS - 1, m // 2], m % 2)
                    if m:
                        square(layer + 1, "n1", m - 1)
                square(layer + 1, "n1", KD - 1)
                cut_after(U["f2", QUARTERS - 1, 3], 1)

        @block.vector
        def _(dve):
            steps = [0]

            def step(ins):
                steps[0] += 1
                ins.then_inc(vector_step, 1)
                dve.wait_ge(vector_step, steps[0])

            def cut(n):
                if LOW_BY[n] == "dve":
                    dve.wait_ge(w_hi_done, n + 1)
                    dve.tensor_tensor(slice_view(w_lo, n), slice_view(raw, n), slice_view(w_hi, n).bitcast(F32),
                                      ALU.subtract).then_inc(w_lo_by_dve, 1)

            def cut_after(u, i=None):
                for n in cuts_after(u) if i is None else cuts_after(u)[i:i + 1]:
                    cut(n)

            def variance(layer, name, cols, inverse):
                wait_group(dve, layer, name)
                b = bank(layer, name)
                for n, (c0, c1) in enumerate(cols):
                    ins = dve.tensor_scalar(var[:, c0:c1], b[:, c0:c1], inverse[n], EPS, ALU.mult, ALU.add)
                ins.then_inc(by_dve, 1)

            def diagonal(key, layer, blocks, source, b0=0, inc=True):
                ident = cc("ident").unsqueeze(1).to_broadcast([P, blocks, P])
                ins = dve.tensor_tensor(diag[:, b0:b0 + blocks, :], ident, source.unsqueeze(2).to_broadcast([P, blocks, P]),
                                        ALU.mult)
                if inc:
                    ins.then_inc(diag_ready, 1)

            def add_square(layer, name, k):
                n = norm_tokens(layer, name)[1]
                if 0 < k < KD - 1:
                    r = norm_at(layer, name)
                    dve.wait_ge(squares_ready, KD * r + k + 1)
                    if k > 1:
                        dve.wait_ge(square_added, (KD - 2) * r + k - 1)
                    dve.tensor_tensor(square_sum[:, 0:n], square_sum[:, 0:n], scratch[:, k % 4, 0:n],
                                      ALU.add).then_inc(square_added, 1)

            def rstd_of_tokens(layer, name, u):
                t0, n = norm_tokens(layer, name)
                variance(layer, name, [(0, n // P)], [1.0 / D])
                if u is not None:
                    cut_after(u, 1)
                if (layer, name) == (0, "n1"):
                    modulations(0)
                    step(gains(0, 0))
                dve.wait_ge(rstd_ready, RSTD_AT[layer, name])
                diagonal(name, layer, n // P, rstd[:, 0:n // P])

            def modulated(layer, name):
                t0, n = norm_tokens(layer, name)
                which = 0 if name == "n1" else 1
                r = norm_at(layer, name)
                wait_group(dve, layer, name + "b")
                for k in range(KD + 1):
                    if k < KD:
                        for group, a, b in parts_of(n):
                            ins = dve.scalar_tensor_tensor(scratch[:, k % 4, a:b], x[:, k, t0 + a:t0 + b],
                                                           gain[:, layer, which, k, group:group + 1],
                                                           bank(layer, name + "b")[:, a:b], ALU.mult, ALU.mult)
                        ins.then_inc(h_ready if k < KD - 1 else by_dve, 1)
                    if k:
                        dve.wait_ge(h_hi_ready, KD * r + k)
                        for group, a, b in parts_of(n):
                            ins = dve.scalar_tensor_tensor(h_lo[:, k - 1, t0 + a:t0 + b], scratch[:, (k - 1) % 4, a:b],
                                                           mods[:, layer, 24 * which + k - 1, group:group + 1],
                                                           h_hi[:, k - 1, t0 + a:t0 + b].bitcast(F32), ALU.add, ALU.subtract)
                        ins.then_inc(h_lo_ready, 1)

            def modulations(batch):
                layer, first, size = ADA_BATCHES[batch]
                dst = mods[:, layer, 2 * first:2 * (first + size), :].rearrange("p (i h) g -> p h i g", h=2)
                b = pp(layer, "b_ada")[:, 2 * first:2 * (first + size)].rearrange("p (i h) -> p h i", h=2)
                b = b.unsqueeze(3).to_broadcast([P, 2, size, 2])
                wait_group(dve, 0, ("at", batch))
                src = bank(0, ("at", batch))[:, 0:2 * P].rearrange("p (h c) -> p h c", h=2)[:, :, 0:4 * size]
                src = src.rearrange("p h (i v g) -> p v h i g", v=2, g=2)
                step(dve.tensor_tensor(dst, src[:, 0], b, ALU.add))
                dve.tensor_tensor(dst, dst, src[:, 1], ALU.add).then_inc(by_dve, 1)
                wait_emptied(dve, 0, ("at", batch))

            def copy_ada_rows(batch):
                size = ADA_BATCHES[batch][2]
                dve.wait_ge(ada_done, sum(n for _, _, n in ADA_BATCHES[:batch + 1]))
                dve.tensor_copy(ada_rows[0:4 * size, batch % 2, :], ada_ps[0:4 * size, 0:256]).then_inc(ada_rows_ready, 1)

            def gains(layer, which):
                g = pp(layer, "norm_ffn" if which else "norm_mix").unsqueeze(2).to_broadcast([P, KD, 2])
                return dve.scalar_tensor_tensor(gain[:, layer, which], mods[:, layer, 24 * which + KD:24 * which + 2 * KD, :],
                                                1.0, g, ALU.add, ALU.mult)

            def residual(layer, name, mod, k):
                t0, nt = tokens_of(layer)
                wait_group(dve, layer, name)
                for group, a, b in parts_of(nt):
                    xs = x[:, k, t0 + a:t0 + b]
                    ins = dve.scalar_tensor_tensor(xs, bank(layer, name)[:, a:b], mods[:, layer, mod * KD + k, group:group + 1],
                                                   xs, ALU.mult, ALU.add)
                ins.then_inc(by_dve, 1)

            dve.wait_ge(tanh_ready, 1)
            step(dve.scalar_tensor_tensor(silu[:], silu[:], 1.0, cvec[:], ALU.add, ALU.mult))
            dve.tensor_scalar(silu[:], silu[:], 0.5, None, ALU.mult).then_inc(silu_ready, 1)
            dve.wait_ge(silu_hi, 1)
            dve.tensor_tensor(silu_parts[:, :, ADA_ROWS - 2:ADA_ROWS], silu[:],
                              silu_parts[:, :, ADA_ROWS - 4:ADA_ROWS - 2].bitcast(F32), ALU.subtract).then_inc(silu_ready, 1)
            for n in range(SLOTS):
                cut(n)
            dve.wait_ge(small_landed, 32)
            for layer in range(DEPTH):
                dve.tensor_scalar(half_gate_bias[:, layer, :], pp(layer, "b_gate"), 0.5, None, ALU.mult)
                dve.tensor_scalar(small[:, layer, NEG_SINK:NEG_SINK + HEADS], pp(layer, "sink"), -1.0, None, ALU.mult)
                dve.tensor_scalar(small[:, layer, SUBLN:SUBLN + 1], pp(layer, "subln"), 1.0 - LAMBDA_INIT[layer], None, ALU.mult)
                lam = pp(layer, "lam").rearrange("p (a b c) -> p a b c", a=2, b=2)
                step(dve.tensor_tensor(lam_prod[:], lam[:, :, 0, :], lam[:, :, 1, :], ALU.mult))
                dve.reduce_sum(small[:, layer, LAM_SUM:LAM_SUM + 2], lam_prod[:], AX_X).then_inc(lam_sums, 1)
                dve.wait_ge(lam_sums, layer + 1)
            for i, u in enumerate(ADA_UNITS[:ADA_BATCHES[0][2]]):
                for k in FIRST_SQUARES.get(i, ()):
                    add_square(0, "n1", k)
                if i == ADA_BATCHES[0][2] - 1:
                    copy_ada_rows(0)
                else:
                    cut_after(u)

            for layer in range(DEPTH):
                t0, nt = tokens_of(layer)
                U = {name: UNIT_AT[layer, name] for name in units_of(layer)}
                nq_tiles = nt // P
                dve.wait_ge(lam_exps, layer + 1)
                e = small[:, layer, LAM_EXP:LAM_EXP + 2]
                step(dve.tensor_tensor(small[:, layer, NEG_LAM:NEG_LAM + 1], e[:, 1:2], e[:, 0:1], ALU.subtract))
                step(dve.tensor_scalar(small[:, layer, NEG_LAM:NEG_LAM + 1], small[:, layer, NEG_LAM:NEG_LAM + 1],
                                       LAMBDA_INIT[layer], None, ALU.subtract))
                rstd_of_tokens(layer, "n1", UNIT_AT[layer - 1, ("f2", QUARTERS - 1, 3)] if layer else None)
                if layer == 0:
                    cut_after(ADA_UNITS[ADA_BATCHES[0][2] - 1])
                modulated(layer, "n1")
                cut_after(U["cq"])
                for i in range(2):
                    wait_emptied(dve, layer, f"cq{i}")
                dve.tensor_tensor(scratch[:, 0, 0:nt], scratch[:, 0, 0:nt], scratch[:, 1, 0:nt],
                                  ALU.add).then_inc(latent_square_sum, 1)
                cut_after(U["ckv"])
                variance(layer, "cs", [(0, nq_tiles), (nq_tiles, nq_tiles + 4)], [1.0 / 256, 1.0 / 128])
                dve.wait_ge(rstd_ready, RSTD_AT[layer, "cs"])
                diagonal("cs", layer, nq_tiles + 4, rstd[:, 0:nq_tiles + 4])
                cut_after(U["nq"])
                for i in range(3):
                    n = nt if i < 2 else TOK
                    wait_group(dve, layer, f"cb{i // 2}")
                    ins = dve.tensor_tensor(latent[:, i, 0:n], latent[:, i, 0:n], bank(layer, f"cb{i // 2}")[:, 0:n], ALU.mult)
                    if i:
                        ins.then_inc(by_dve, 1)
                for i in range(3):
                    first = t0 if i < 2 else 0
                    gamma = pp(layer, "q_norm", i) if i < 2 else pp(layer, "kv_norm")
                    dve.wait_ge(latent_hi, 3 * layer + i + 1)
                    dve.scalar_tensor_tensor(cn_lo[:, i, first:], latent[:, i, 0:TOK - first], gamma,
                                             cn_hi[:, i, first:].bitcast(F32), ALU.mult, ALU.subtract).then_inc(latent_lo, 1)
                cut_after(U["nk"])

                def values(name, v0, width):
                    for t in range(4):
                        wait_group(dve, layer, f"{name}{t}")
                        dve.tensor_copy(v_sb[:, t, v0:v0 + width], bank(layer, f"{name}{t}")[:, 0:width]).then_inc(by_dve, 1)

                def turn_products(names):
                    for name in names:
                        r = len(ROPES) * layer + ROPES.index(name)
                        dim = 64 if name.startswith("rw") else 32
                        rows = slice(64, 96) if name[1] in "ku" else slice(0, P)
                        if r >= 4:
                            dve.wait_ge(rope_done, r - 3)
                        wait_group(dve, layer, name)
                        dve.tensor_tensor(scratch[rows, r % 4, 0:LAT], bank(layer, name)[rows, 0:LAT],
                                          cc(f"sin{dim}")[rows], ALU.mult).then_inc(by_dve, 1)

                values("nv", V_NA, 256)
                cut_after(U["nv"])
                cut_after(U["wq"])
                for t in range(4):
                    wait_group(dve, layer, f"wkv{t}")
                    dve.tensor_copy(wk[:, 1, t * P:(t + 1) * P], bank(layer, f"wkv{t}")[:, 0:P])
                    dve.tensor_copy(v_sb[:, t, V_WIN:V_WIN + P], bank(layer, f"wkv{t}")[:, P:2 * P]).then_inc(by_dve, 1)
                cut_after(U["wkv"])
                cut_after(U["dq"])
                turn_products(ROPES[0:4])
                cut_after(U["dk"])
                values("dv", V_DIFF, 256)
                cut_after(U["dv"])
                turn_products(ROPES[4:8])
                cut_after(U["uq"])
                values("uv", V_MLA, 256)
                cut_after(U["ukv"])
                turn_products(ROPES[8:12])

                items = items_of(layer)
                scale = {"na": NA_SCALE, "win": WIN_SCALE, "diff": DIFF_SCALE, "mla": MLA_SCALE}

                def shift(j):
                    kind, which, part_, t = items[j]
                    nkeys = TOK if part_ == "lat" else CTX
                    col = 2 * (item_base[layer] + j)
                    sc = scores[j % 2]
                    dve.wait_ge(scores_ready, item_base[layer] + j + 1)
                    if part_ == "lat" and kind == "na":
                        dve.wait_ge(bias_ready, layer * PAIRS + which + 1)
                        step(dve.scalar_tensor_tensor(sc[:, :, CTX:TOK], bias[:, :, t, :], 8.0, sc[:, :, CTX:TOK],
                                                      ALU.mult, ALU.add))
                    if part_ == "lat" and kind == "win":
                        band = cc("band").rearrange("p (t k) -> p t k", t=2)[:, t:t + 1, :].to_broadcast([P, 2, LAT])
                        step(dve.tensor_tensor(sc[:, :, CTX:TOK], sc[:, :, CTX:TOK], band, ALU.add))
                    step(dve.tensor_reduce(stats[:, 0, col:col + 2], sc[:, :, 0:nkeys], AX_X, ALU.max))
                    if kind == "win":
                        ns = small[:, layer, NEG_SINK + 2 * which:NEG_SINK + 2 * which + 2]
                        step(dve.scalar_tensor_tensor(stats[:, 1, col:col + 2], stats[:, 0, col:col + 2], -scale[kind], ns,
                                                      ALU.mult, ALU.min))
                        ins = dve.tensor_tensor(stats[:, 3, col:col + 2], stats[:, 1, col:col + 2], ns, ALU.subtract)
                    else:
                        ins = dve.tensor_scalar(stats[:, 1, col:col + 2], stats[:, 0, col:col + 2], -scale[kind], None, ALU.mult)
                    ins.then_inc(shift_ready, 1)

                def normalise(j):
                    kind, which, part_, t = items[j]
                    nkeys = TOK if part_ == "lat" else CTX
                    col = 2 * (item_base[layer] + j)
                    s = stats[:, 2, col:col + 2]
                    dve.wait_ge(exp_done, item_base[layer] + j + 1)
                    if kind == "win":
                        step(dve.tensor_tensor(s, s, stats[:, 3, col:col + 2], ALU.add))
                    step(dve.reciprocal(s, s))
                    pr = [probs[j % 3][:, lane, 0:nkeys] for lane in range(2)]
                    if kind == "diff":
                        step(dve.tensor_scalar(pr[1], pr[1], s[:, 1:2], small[:, layer, NEG_LAM:NEG_LAM + 1], ALU.mult, ALU.mult))
                        ins = dve.scalar_tensor_tensor(pr[0], pr[0], s[:, 0:1], pr[1], ALU.mult, ALU.add)
                    else:
                        for lane in range(2):
                            ins = dve.tensor_scalar(pr[lane], pr[lane], s[:, lane:lane + 1], None, ALU.mult)
                    ins.then_inc(probs_ready, 1)

                def outputs(j):
                    kind, which, part_, t = items[j]
                    c0 = (CTX if part_ == "lat" else 0) + t * P
                    wait_group(dve, layer, ("PV", j))
                    if kind == "diff":
                        rows = slice(64 * (which % 2), 64 * (which % 2) + 64)
                        dst = dq[rows, which // 2, c0:c0 + P]
                    else:
                        rows = slice(0, P)
                        dst = {"na": nq, "win": wq, "mla": mq}[kind][:, which, c0:c0 + P]
                    dve.tensor_copy(dst, bank(layer, ("PV", j))[rows, 0:P]).then_inc(by_dve, 1)

                for j in range(len(items) + 3):
                    if layer == 0 and j == ADA_BATCHES[1][2]:
                        copy_ada_rows(1)
                    if j < len(items):
                        shift(j)
                    if 1 <= j <= len(items):
                        normalise(j - 1)
                        if layer == 0:
                            cut_after(ADA_UNITS[ADA_BATCHES[0][2] + j - 1])
                            if j == len(items):
                                copy_ada_rows(2)
                    if j >= 3:
                        outputs(j - 3)

                variance(layer, "ds", [(0, 4 * nq_tiles)], [1.0 / 64])
                dve.wait_ge(rstd_ready, RSTD_AT[layer, "ds"])
                for pair in range(2):
                    r = rstd[:, 2 * pair * nq_tiles:2 * (pair + 1) * nq_tiles].rearrange("p (t a) -> p t a", a=2)
                    for a in range(2):
                        diagonal(f"ds{pair}", layer, nq_tiles, r[:, :, a], a * nq_tiles, inc=(a == 1))
                    cut_after(U["g", 0, 0], pair)
                    wait_group(dve, layer, f"db{pair}")
                    o = dq[:, pair, t0:]
                    dve.scalar_tensor_tensor(o, o, small[:, layer, SUBLN:SUBLN + 1], bank(layer, f"db{pair}")[:, 0:nt],
                                             ALU.mult, ALU.mult).then_inc(by_dve, 1)
                    if layer == 0:
                        modulations(pair + 1)
                if layer == 0:
                    gains(0, 1)
                    gains(1, 0)
                    step(gains(1, 1))

                for m in range(KD):
                    if m:
                        cut_after(U["g", m, 0])
                    cut_after(U["g", m, 1])
                    wait_emptied(dve, layer, ("g", m, 3))
                    for i in range(4):
                        wait_group(dve, layer, ("b", m, i))
                        s = scratch[:, i, 0:nt]
                        dve.scalar_tensor_tensor(s, s, 1.0, bank(layer, ("b", m, i))[:, 0:nt], ALU.add,
                                                 ALU.mult).then_inc(by_dve, 1)
                    dve.wait_ge(y_hi_ready, KD * layer + m + 1)
                    dve.scalar_tensor_tensor(y_lo[:, m, t0:], scratch[:, 0, 0:nt], 0.5, y_hi[:, m, t0:].bitcast(F32),
                                             ALU.mult, ALU.subtract).then_inc(y_lo_ready, 1)
                    cut_after(U["b", m])
                for m in range(KD):
                    if m < KD - 1:
                        cut_after(U["o", m // 2], m % 2)
                    residual(layer, ("o", m), 2, m)
                    if m:
                        add_square(layer, "n2", m - 1)

                rstd_of_tokens(layer, "n2", U["o", (KD - 1) // 2])
                modulated(layer, "n2")

                def hidden_lo(q, m):
                    f = (layer * QUARTERS + q) * HID + m
                    dve.wait_ge(hid_hi_ready, f + 1)
                    dve.tensor_tensor(hid_lo[q % 2][:, m, t0:], scratch[:, f % 4, 0:nt],
                                      hid_hi[q % 2][:, m, t0:].bitcast(F32), ALU.subtract).then_inc(hid_lo_ready, 1)

                for kind, q in FF_ORDER:
                    for i in range(4):
                        for m in (2 * i, 2 * i + 1):
                            if (kind, q, m) != ("f2", QUARTERS - 1, KD - 1):
                                cut_after(U[kind, q, i], m % 2)
                            if kind == "f1":
                                hidden_lo(q, m)
                            else:
                                residual(layer, (kind, q, m), 5, m)
                                if q == QUARTERS - 1 and m:
                                    add_square(layer + 1, "n1", m - 1)

            rstd_of_tokens(DEPTH, "n1", None)
            wait_group(dve, DEPTH, "n1b")
            for k in range(KD):
                dve.scalar_tensor_tensor(out_sb[:, k, :], x[:, k, CTX:TOK], par[:, DEPTH * PAR_LAYER + k:DEPTH * PAR_LAYER + k + 1],
                                         bank(DEPTH, "n1b")[:, 0:LAT], ALU.mult, ALU.mult).then_inc(out_ready, 1)

        @block.gpsimd
        def _(pool):
            steps = [0]

            def step(ins):
                steps[0] += 1
                ins.then_inc(gpsimd_step, 1)
                pool.wait_ge(gpsimd_step, steps[0])

            def power(layer, name, cols):
                wait_emptied(pool, layer, name)
                if RSTD_AT[layer, name] > 1:
                    key = {v: k for k, v in RSTD_AT.items()}[RSTD_AT[layer, name] - 1]
                    last = "ds1" if key[1] == "ds" else key[1]
                    pool.wait_ge(diag_ready, DIAG_AT[key[0], last])
                pool.tensor_tensor(rstd[:, 0:cols], var[:, 0:cols], neg_half[:, 0:cols], ALU.pow).then_inc(rstd_ready, 1)

            pool.memset(silu_parts[:].bitcast(F32), 0.0).then_inc(silu_zero, 1)
            step(pool.memset(pair_q[:], 0.0))
            step(pool.memset(diff_q[:], 0.0))
            step(pool.memset(neg_half[:], -0.5))
            pool.wait_ge(small_landed, 32)
            for layer in range(DEPTH):
                t0, nt = tokens_of(layer)
                nq_tiles = nt // P
                items = items_of(layer)

                def ready_bias(pair):
                    pool.wait_ge(bias_landed, 128 * (layer * PAIRS + pair + 1))
                    b = bias[:].rearrange("p i t k -> p i (t k)")
                    near = cc("near").unsqueeze(1).to_broadcast([P, 2, 2 * LAT])
                    pool.tensor_tensor(b, b, near, ALU.add).then_inc(bias_ready, 1)
                    pool.wait_ge(bias_ready, layer * PAIRS + pair + 1)

                def fill_query(j):
                    if j >= len(items) or items[j][0] == "mla":
                        return
                    kind, which, part_, t = items[j]
                    cols = slice((CTX if part_ == "lat" else 0) + t * P, (CTX if part_ == "lat" else 0) + (t + 1) * P)
                    if item_base[layer] + j >= 2:
                        pool.wait_ge(scores_ready, item_base[layer] + j - 1)
                    for lane in range(2):
                        if kind == "diff":
                            r0 = 64 * (which % 2) + 32 * lane
                            rows = slice(r0, r0 + 32)
                            ins = pool.tensor_copy(diff_q[rows, 2 * (which % 2) + lane, :], dq[rows, which // 2, cols])
                        else:
                            rows = slice(64 * lane, 64 * lane + 64)
                            ins = pool.tensor_copy(pair_q[rows, j % 2, lane, :], (nq if kind == "na" else wq)[rows, which, cols])
                        if lane == 0:
                            step(ins)
                    ins.then_inc(query_ready, 1)
                    pool.wait_ge(query_ready, query_count(layer, j))

                def cut_low(u):
                    for n in cuts_after(u):
                        if LOW_BY[n] == "pool":
                            pool.wait_ge(w_hi_done, n + 1)
                            pool.tensor_tensor(slice_view(w_lo, n), slice_view(raw, n), slice_view(w_hi, n).bitcast(F32),
                                               ALU.subtract).then_inc(w_lo_by_pool, 1)
                            pool.wait_ge(w_lo_by_pool, low_count(n))

                power(layer, "n1", TOK // P)
                ready_bias(0)
                power(layer, "cs", nq_tiles + 4)

                def finish_rope(name, tile):
                    r = len(ROPES) * layer + ROPES.index(name)
                    dim = 64 if name.startswith("rw") else 32
                    rows = slice(64, 96) if name[1] in "ku" else slice(0, P)
                    wait_emptied(pool, layer, name)
                    part = tile[rows, CTX:TOK]
                    step(pool.tensor_tensor(part, part, cc(f"cos{dim}")[rows], ALU.mult))
                    pool.tensor_tensor(part, part, scratch[rows, r % 4, 0:LAT], ALU.add).then_inc(rope_done, 1)
                    pool.wait_ge(rope_done, r + 1)

                tiles = [wq[:, 0], wq[:, 1], wk[:, 0], mk[:, 0], dq[:, 0], dq[:, 1], dk[:, 0], dk[:, 1]]
                tiles += [mq[:, hd] for hd in range(HEADS)]
                wait_emptied(pool, layer, "nq1")
                fill_query(0)
                fill_query(1)
                for n, name in enumerate(ROPES):
                    if name == "ruq2":
                        fill_query(2)
                    finish_rope(name, tiles[n])
                    if name == "rkr":
                        for hd in range(1, HEADS):
                            pool.tensor_copy(mk[64:96, hd, :], mk[64:96, 0, :]).then_inc(kr_copied, 1)
                            pool.wait_ge(kr_copied, 3 * layer + hd)
                for j in range(len(items)):
                    if j:
                        fill_query(j + 2)
                    if layer == 0:
                        cut_low(ADA_UNITS[ADA_BATCHES[0][2] + j])
                    if j == 2 + 8 // BIAS_PARTS[layer]:
                        ready_bias(1)
                power(layer, "ds", 4 * nq_tiles)
                for n, k in enumerate((6, 7, 4, 5, 0, 1, 2, 3)):
                    pool.wait_ge(o_hi_ready, KD * layer + n + 1)
                    pool.tensor_tensor(o_lo[:, k, t0:], BRANCH_TILES[k][:, t0:], o_hi[:, k, t0:].bitcast(F32),
                                       ALU.subtract).then_inc(o_lo_ready, 1)
                for m in range(KD):
                    wait_emptied(pool, layer, ("b", m, 3))
                    s = [scratch[:, i, 0:nt] for i in range(4)]
                    pool.tensor_tensor(s[0], s[0], s[1], ALU.add)
                    step(pool.tensor_tensor(s[2], s[2], s[3], ALU.add))
                    pool.tensor_tensor(s[0], s[0], s[2], ALU.add).then_inc(y_sum_ready, 1)
                power(layer, "n2", nq_tiles)
                for q in range(QUARTERS):
                    for m in range(HID):
                        f = (layer * QUARTERS + q) * HID + m
                        wait_emptied(pool, layer, ("f1", q, m))
                        s = scratch[:, f % 4, 0:nt]
                        pool.tensor_tensor(s, s, s, ALU.mult).then_inc(relu2_ready, 1)
            power(DEPTH, "n1", LAT // P)


def kernel(**inputs):
    import concourse.bacc as bacc
    from concourse.bass_utils import run_bass_kernel_spmd

    a = {k: np.ascontiguousarray(v) for k, v in inputs.items()}

    def columns(v):
        return v.reshape(-1, P).T

    def rows(v):
        return np.broadcast_to(v.reshape(1, -1), (P, v.size))

    par = []
    for layer in range(DEPTH):
        par += [columns(a["norm_mix"][layer]), columns(a["norm_ffn"][layer]), columns(a["b_ada"][layer]),
                columns(a["mla_q_norm"][layer]), columns(a["mla_kv_norm"][layer]),
                np.concatenate([a["diff_subln"][layer]] * 2).reshape(P, 1), columns(a["b_gate"][layer]),
                rows(a["diff_lambda"][layer]), rows(a["win_sink"][layer])]
    par.append(columns(a["final_norm"]))
    feeds = {
        "xT": np.concatenate([a["ctx"][0], a["x"][0]]).T.reshape(KD, P, TOK).transpose(1, 0, 2),
        "c2": np.stack([columns(a["c_ctx"]), columns(a["c"][0])], axis=2),
        "con_in": constants(),
        "par_in": np.concatenate(par, axis=1),
        "rpb": np.tile(np.pad(a["na_rpb"], ((0, 0), (0, 0), (0, 0), (48, 48))), (1, 1, 1, GRID_W)),
        **{n: a[n] for n in ("w_ada", "w_in", "w_uq", "w_ukv", "w_gate", "w_branch", "w_out", "w_ff1", "w_ff2")},
    }
    nc = bacc.Bacc("TRN2", target_bir_lowering=False, num_devices=1)
    arrays, args = {}, []
    for name, v in feeds.items():
        v = np.ascontiguousarray(v)
        arrays[f"{name}_dram"] = v
        args.append(nc.dram_tensor(f"{name}_dram", v.shape, mybir.dt.from_np(v.dtype), kind="ExternalInput").ap())
    args.append(nc.dram_tensor("out_dram", (D, LAT), F32, kind="ExternalOutput").ap())
    block_program(nc, *args)
    r = run_bass_kernel_spmd(nc, [arrays], core_ids=[0])
    return np.ascontiguousarray(r.results[0]["out_dram"].T).reshape(1, LAT, D)
```
